# Optimizing a Trainium2 kernel written in Bass

```python
import math
import jax, jax.numpy as jnp
from jax import lax
import numpy as np

D_MODEL = 1024
BATCH = 1
SEQ = 512
DEPTH = 2

GRID_W = 64
CTX_LEN = 256
N_AB = (DEPTH + 1) // 2
N_C = DEPTH // 2
A_HEADS = 8
A_KV_HEADS = 2
A_HEAD_DIM = 64
A_WIDTH = A_HEADS * A_HEAD_DIM
A_KV_WIDTH = A_KV_HEADS * A_HEAD_DIM
WINDOW = 128
Q_BLOCK = WINDOW
ROPE_BASE = 10000.0
B_WIDTH = D_MODEL // 2
CONV_W = 3
AB_IN_WIDTH = 2 * A_WIDTH + 2 * A_KV_WIDTH + 4 * B_WIDTH
AB_OUT_WIDTH = A_WIDTH + B_WIDTH
C_HEADS = 8
C_KEY_DIM = 128
C_VAL_DIM = D_MODEL // C_HEADS
C_F_WIDTH = C_HEADS * C_KEY_DIM
C_I_WIDTH = C_HEADS * C_VAL_DIM
C_IN_WIDTH = 3 * C_F_WIDTH + 2 * C_I_WIDTH
CHUNK = 32
DEEPNORM_ALPHA = (2 * DEPTH) ** 0.25
DEEPNORM_BETA = (8 * DEPTH) ** -0.25
LN_EPS = 1e-5
RMS_EPS = 1e-6


def split_cols(p, widths):
    idx = [int(v) for v in np.cumsum(widths)[:-1]]
    return jnp.split(p, idx, axis=-1)

def layer_norm(x, g, b):
    xf = x.astype(jnp.float32)
    mu = xf.mean(-1, keepdims=True)
    var = jnp.square(xf - mu).mean(-1, keepdims=True)
    return ((xf - mu) * lax.rsqrt(var + LN_EPS) * g + b).astype(x.dtype)

def modulate(h, shift, scale):
    return h * (1 + scale) + shift

def rope_1d(x, pos):
    half = x.shape[-1] // 2
    freqs = ROPE_BASE ** (-jnp.arange(half, dtype=jnp.float32) / half)
    ang = pos.astype(jnp.float32)[:, None] * freqs[None, :]
    cos = jnp.cos(ang)[:, None, :].astype(x.dtype)
    sin = jnp.sin(ang)[:, None, :].astype(x.dtype)
    x1, x2 = x[..., :half], x[..., half:]
    return jnp.concatenate([x1 * cos - x2 * sin, x1 * sin + x2 * cos], axis=-1)

def axial_rope(x, row, col):
    half = x.shape[-1] // 2
    return jnp.concatenate([rope_1d(x[..., :half], row), rope_1d(x[..., half:], col)], axis=-1)

def heads(t, n_heads):
    return t.reshape(t.shape[0], t.shape[1], n_heads, A_HEAD_DIM)

def short_conv(u, w):
    pad = CONV_W // 2
    L = u.shape[1]
    up = jnp.pad(u, ((0, 0), (pad, pad), (0, 0)))
    y = up[:, 0:L] * w[0]
    for j in range(1, CONV_W):
        y = y + up[:, j:j + L] * w[j]
    return y

def window_attention(q, k, v, kc, vc, sink):
    B, L = q.shape[:2]
    n_blk = L // Q_BLOCK
    G = A_HEADS // A_KV_HEADS
    scale = A_HEAD_DIM ** -0.5
    lc = kc.shape[1]
    span = Q_BLOCK + 2 * WINDOW
    qb = q.reshape(B, n_blk, Q_BLOCK, A_KV_HEADS, G, A_HEAD_DIM).swapaxes(0, 1)
    kp = jnp.pad(k, ((0, 0), (WINDOW, WINDOW), (0, 0), (0, 0)))
    vp = jnp.pad(v, ((0, 0), (WINDOW, WINDOW), (0, 0), (0, 0)))
    rel = jnp.arange(span)[None, :] - WINDOW - jnp.arange(Q_BLOCK)[:, None]
    in_win = jnp.abs(rel) <= WINDOW
    sink_l = jnp.broadcast_to(sink.astype(jnp.float32).reshape(1, A_KV_HEADS, G, 1, 1),
                              (B, A_KV_HEADS, G, Q_BLOCK, 1))

    def one_block(args):
        n, q_n = args
        start = n * Q_BLOCK
        k_n = lax.dynamic_slice_in_dim(kp, start, span, axis=1)
        v_n = lax.dynamic_slice_in_dim(vp, start, span, axis=1)
        key_pos = start - WINDOW + jnp.arange(span)
        valid = in_win & ((key_pos >= 0) & (key_pos < L))[None, :]
        s_loc = jnp.einsum('bikgd,bjkd->bkgij', q_n, k_n).astype(jnp.float32) * scale
        s_loc = jnp.where(valid, s_loc, -jnp.inf)
        s_ctx = jnp.einsum('bikgd,bjkd->bkgij', q_n, kc).astype(jnp.float32) * scale
        p = jax.nn.softmax(jnp.concatenate([sink_l, s_ctx, s_loc], axis=-1), axis=-1).astype(v.dtype)
        return (jnp.einsum('bkgij,bjkd->bikgd', p[..., 1:1 + lc], vc)
                + jnp.einsum('bkgij,bjkd->bikgd', p[..., 1 + lc:], v_n))

    out = lax.map(one_block, (jnp.arange(n_blk), qb))
    return out.swapaxes(0, 1).reshape(B, L, A_WIDTH)

def context_attention(qc, kc, vc, sink):
    B, lc = qc.shape[:2]
    G = A_HEADS // A_KV_HEADS
    q = qc.reshape(B, lc, A_KV_HEADS, G, A_HEAD_DIM)
    s = jnp.einsum('bikgd,bjkd->bkgij', q, kc).astype(jnp.float32) * (A_HEAD_DIM ** -0.5)
    sink_l = jnp.broadcast_to(sink.astype(jnp.float32).reshape(1, A_KV_HEADS, G, 1, 1),
                              (B, A_KV_HEADS, G, lc, 1))
    p = jax.nn.softmax(jnp.concatenate([sink_l, s], axis=-1), axis=-1).astype(vc.dtype)
    return jnp.einsum('bkgij,bjkd->bikgd', p[..., 1:], vc).reshape(B, lc, A_WIDTH)

def ab_layer(x, xc, mod, mod_c, w_in, w_out, sink, conv_w, ln_g, ln_b, row, col, ctx_out):
    shift, scale, gate = jnp.split(mod, 3, axis=-1)
    shift_c, scale_c, gate_c = jnp.split(mod_c, 3, axis=-1)
    widths = (A_WIDTH, A_KV_WIDTH, A_KV_WIDTH, A_WIDTH, B_WIDTH, B_WIDTH, B_WIDTH, B_WIDTH)
    q, k, v, g_a, xb, b_g, c_g, g_b = split_cols(modulate(x, shift, scale) @ w_in, widths)
    hc = modulate(xc, shift_c, scale_c)
    if ctx_out:
        qc, kc, vc, g_ac, xbc, b_gc, c_gc, g_bc = split_cols(hc @ w_in, widths)
    else:
        kc, vc = split_cols(hc @ w_in[:, A_WIDTH:A_WIDTH + 2 * A_KV_WIDTH], (A_KV_WIDTH, A_KV_WIDTH))
    kc, vc = heads(kc, A_KV_HEADS), heads(vc, A_KV_HEADS)
    q = axial_rope(heads(q, A_HEADS), row, col)
    k = axial_rope(heads(k, A_KV_HEADS), row, col)
    o_a = window_attention(q, k, heads(v, A_KV_HEADS), kc, vc, sink)
    o_b = b_g * short_conv(c_g * xb, conv_w)
    y = jnp.concatenate([o_a * jax.nn.silu(g_a), o_b * jax.nn.silu(g_b)], axis=-1) @ w_out
    x_new = layer_norm(DEEPNORM_ALPHA * x + gate * y, ln_g, ln_b)
    if not ctx_out:
        return x_new, None
    o_ac = context_attention(heads(qc, A_HEADS), kc, vc, sink)
    o_bc = b_gc * short_conv(c_gc * xbc, conv_w)
    yc = jnp.concatenate([o_ac * jax.nn.silu(g_ac), o_bc * jax.nn.silu(g_bc)], axis=-1) @ w_out
    xc_new = layer_norm(DEEPNORM_ALPHA * xc + gate_c * yc, ln_g, ln_b)
    return x_new, xc_new

def to_heads(t, d):
    B, L, _ = t.shape
    return t.reshape(B, L, -1, d).transpose(0, 2, 1, 3).astype(jnp.float32)

def forget_terms(z, lb):
    lb = jnp.clip(lb.astype(jnp.float32), 0.0, 1.0).reshape(C_HEADS, 1, C_KEY_DIM)
    log_f = jnp.logaddexp(jnp.log(lb), jnp.log1p(-lb) + jax.nn.log_sigmoid(z))
    k = (1 - lb) * jax.nn.sigmoid(-z)
    return k, log_f

def hgrn2_scan(q, k, v, log_f, s0, with_outputs):
    B, H, L, dk = k.shape
    n = L // CHUNK
    chunks = lambda t: t.reshape(B, H, n, CHUNK, t.shape[-1])
    to_scan = lambda t: jnp.moveaxis(t, 2, 0)
    k, v, log_f = chunks(k), chunks(v), chunks(log_f)
    b = jnp.cumsum(log_f, axis=3)
    b_last = b[:, :, :, -1:, :]
    k_state = k * jnp.exp(b_last - b)
    decay = jnp.exp(b_last[:, :, :, 0, :])
    if with_outputs:
        q = chunks(q)
        q_inter = q * jnp.exp(b)
        tri = jnp.tril(jnp.ones((CHUNK, CHUNK), dtype=bool))[:, :, None]

        def step(s, xs):
            q_n, k_n, v_n, b_n, qi_n, ks_n, d_n = xs
            o_inter = jnp.einsum('bhcd,bhde->bhce', qi_n, s)
            diff = b_n[:, :, :, None, :] - b_n[:, :, None, :, :]
            w = jnp.exp(jnp.where(tri, diff, -jnp.inf))
            scores = jnp.einsum('bhcd,bhsd,bhcsd->bhcs', q_n, k_n, w)
            o_n = o_inter + jnp.einsum('bhcs,bhse->bhce', scores, v_n)
            return d_n[..., None] * s + jnp.einsum('bhcd,bhce->bhde', ks_n, v_n), o_n

        s_final, o = lax.scan(step, s0, (to_scan(q), to_scan(k), to_scan(v), to_scan(b),
                                         to_scan(q_inter), to_scan(k_state), to_scan(decay)))
        o = jnp.moveaxis(o, 0, 2).reshape(B, H, L, v.shape[-1])
        return o, s_final

    def step_state(s, xs):
        k_n, v_n, d_n = xs
        return d_n[..., None] * s + jnp.einsum('bhcd,bhce->bhde', k_n, v_n), None

    s_final, _ = lax.scan(step_state, s0, (to_scan(k_state), to_scan(v), to_scan(decay)))
    return None, s_final

def hgrn2_direction(q, i, z, lb, qc, ic, zc, ctx_out, reverse):
    flip = (lambda t: jnp.flip(t, axis=2)) if reverse else (lambda t: t)
    B = i.shape[0]
    kc, lfc = forget_terms(zc, lb)
    s0 = jnp.zeros((B, C_HEADS, C_KEY_DIM, C_VAL_DIM), jnp.float32)
    oc, s_ctx = hgrn2_scan(flip(qc) if ctx_out else None, flip(kc), flip(ic), flip(lfc), s0, ctx_out)
    k, lf = forget_terms(z, lb)
    o, _ = hgrn2_scan(flip(q), flip(k), flip(i), flip(lf), s_ctx, True)
    return flip(o), (flip(oc) if ctx_out else None)

def hgrn2_readout(o, g, g_norm, w_out):
    on = o * lax.rsqrt(jnp.mean(o * o, axis=-1, keepdims=True) + RMS_EPS) * g_norm
    B, H, L, dv = on.shape
    return (on.transpose(0, 2, 1, 3).reshape(B, L, H * dv).astype(g.dtype) * jax.nn.silu(g)) @ w_out

def c_layer(x, xc, mod, mod_c, w_in, w_out, lb_f, lb_b, g_norm, ln_g, ln_b, ctx_out):
    shift, scale, gate = jnp.split(mod, 3, axis=-1)
    shift_c, scale_c, gate_c = jnp.split(mod_c, 3, axis=-1)
    widths = (C_F_WIDTH, C_F_WIDTH, C_F_WIDTH, C_I_WIDTH, C_I_WIDTH)
    q, zf, zb, i, g = split_cols(modulate(x, shift, scale) @ w_in, widths)
    hc = modulate(xc, shift_c, scale_c)
    if ctx_out:
        qc, zfc, zbc, ic, gc = split_cols(hc @ w_in, widths)
        qc = jax.nn.silu(to_heads(qc, C_KEY_DIM)) * (C_KEY_DIM ** -0.5)
    else:
        zfc, zbc, ic = split_cols(hc @ w_in[:, C_F_WIDTH:3 * C_F_WIDTH + C_I_WIDTH],
                                  (C_F_WIDTH, C_F_WIDTH, C_I_WIDTH))
        qc = None
    q = jax.nn.silu(to_heads(q, C_KEY_DIM)) * (C_KEY_DIM ** -0.5)
    i, zf, zb = to_heads(i, C_VAL_DIM), to_heads(zf, C_KEY_DIM), to_heads(zb, C_KEY_DIM)
    ic, zfc, zbc = to_heads(ic, C_VAL_DIM), to_heads(zfc, C_KEY_DIM), to_heads(zbc, C_KEY_DIM)
    o_f, oc_f = hgrn2_direction(q, i, zf, lb_f, qc, ic, zfc, ctx_out, reverse=False)
    o_b, oc_b = hgrn2_direction(q, i, zb, lb_b, qc, ic, zbc, ctx_out, reverse=True)
    y = hgrn2_readout(o_f + o_b, g, g_norm, w_out)
    x_new = layer_norm(DEEPNORM_ALPHA * x + gate * y, ln_g, ln_b)
    if not ctx_out:
        return x_new, None
    yc = hgrn2_readout(oc_f + oc_b, gc, g_norm, w_out)
    xc_new = layer_norm(DEEPNORM_ALPHA * xc + gate_c * yc, ln_g, ln_b)
    return x_new, xc_new

def first_inputs(seed: int = 0) -> dict:
    key = jax.random.key(seed)
    ks = jax.random.split(key, 16)
    nrm = lambda k, shape, s: jax.random.normal(k, shape, jnp.float32) * s
    ab_col_scale = jnp.concatenate([
        jnp.ones((A_WIDTH + A_KV_WIDTH,), jnp.float32),
        jnp.full((A_KV_WIDTH,), DEEPNORM_BETA, jnp.float32),
        jnp.ones((A_WIDTH + 4 * B_WIDTH,), jnp.float32)])
    c_col_scale = jnp.concatenate([
        jnp.ones((3 * C_F_WIDTH,), jnp.float32),
        jnp.full((C_I_WIDTH,), DEEPNORM_BETA, jnp.float32),
        jnp.ones((C_I_WIDTH,), jnp.float32)])
    return {
        "x": nrm(ks[0], (BATCH, SEQ, D_MODEL), 1.0),
        "c": nrm(ks[1], (BATCH, D_MODEL), 1.0),
        "ctx": nrm(ks[2], (BATCH, CTX_LEN, D_MODEL), 1.0),
        "c_ctx": nrm(ks[3], (D_MODEL,), 1.0),
        "w_ada": nrm(ks[4], (DEPTH, D_MODEL, 3 * D_MODEL), D_MODEL ** -0.5),
        "b_ada": nrm(ks[5], (DEPTH, 3 * D_MODEL), 0.02),
        "ln_g": 1.0 + nrm(ks[6], (DEPTH, D_MODEL), 0.02),
        "ln_b": nrm(ks[7], (DEPTH, D_MODEL), 0.02),
        "w_in_ab": nrm(ks[8], (N_AB, D_MODEL, AB_IN_WIDTH), D_MODEL ** -0.5) * ab_col_scale,
        "w_out_ab": nrm(ks[9], (N_AB, AB_OUT_WIDTH, D_MODEL), AB_OUT_WIDTH ** -0.5 * DEEPNORM_BETA),
        "sink_ab": nrm(ks[10], (N_AB, A_HEADS), 0.5),
        "conv_ab": nrm(ks[11], (N_AB, CONV_W, B_WIDTH), CONV_W ** -0.5),
        "w_in_c": nrm(ks[12], (N_C, D_MODEL, C_IN_WIDTH), D_MODEL ** -0.5) * c_col_scale,
        "w_out_c": nrm(ks[13], (N_C, C_I_WIDTH, D_MODEL), C_I_WIDTH ** -0.5 * DEEPNORM_BETA),
        "lb_c": nrm(ks[14], (2, N_C, C_F_WIDTH), 0.5),
        "gnorm_c": 1.0 + nrm(ks[15], (N_C, C_VAL_DIM), 0.02),
    }

def first_block(x, c, ctx, c_ctx, w_ada, b_ada, ln_g, ln_b, w_in_ab, w_out_ab, sink_ab, conv_ab,
              w_in_c, w_out_c, lb_c, gnorm_c):
    L = x.shape[1]
    rows = L // GRID_W
    row = jnp.repeat(jnp.arange(rows), GRID_W)
    col = jnp.tile(jnp.arange(GRID_W), rows)
    lb_p = jax.nn.softmax(lb_c.astype(jnp.float32), axis=1)
    lb_all = jnp.cumsum(lb_p, axis=1) - lb_p[:, :1]
    silu_c = jax.nn.silu(c)
    silu_cc = jax.nn.silu(c_ctx)
    xc = ctx
    for l in range(DEPTH):
        mod = (silu_c @ w_ada[l] + b_ada[l])[:, None, :]
        mod_c = silu_cc @ w_ada[l] + b_ada[l]
        ctx_out = l < DEPTH - 1
        j = l // 2
        if l % 2 == 0:
            x, xc = ab_layer(x, xc, mod, mod_c, w_in_ab[j], w_out_ab[j], sink_ab[j], conv_ab[j],
                             ln_g[l], ln_b[l], row, col, ctx_out)
        else:
            x, xc = c_layer(x, xc, mod, mod_c, w_in_c[j], w_out_c[j], lb_all[0, j], lb_all[1, j],
                            gnorm_c[j], ln_g[l], ln_b[l], ctx_out)
    return x


N_EVEN = (DEPTH + 1) // 2
N_ODD = DEPTH // 2
HEAD_DIM = 64
ATT_HEADS = D_MODEL // (2 * HEAD_DIM)
ATT_WIDTH = ATT_HEADS * HEAD_DIM
ROPE_DIM = HEAD_DIM // 4
ROPE_THETA = 500000.0
DILATED_BRANCHES = ((128, 1), (512, 4), (2048, 16))
ATT_BLOCK = 128
NEG_INF = -1e30
SSM_WIDTH = D_MODEL - ATT_WIDTH
SSM_GROUP = 16
SSM_GROUPS = SSM_WIDTH // SSM_GROUP
SSM_STATE = 64
EVEN_IN = 3 * ATT_WIDTH + SSM_WIDTH
LRU_WIDTH = D_MODEL
LRU_BLOCKS = 4
LRU_BLOCK_DIM = LRU_WIDTH // LRU_BLOCKS
CONV_WIDTH = 4
RG_C = 8.0
FFN_HIDDEN = -(-8 * D_MODEL // (3 * 256)) * 256
NORM_EPS = 1e-6


def rms_norm(x, g):
    x32 = x.astype(jnp.float32)
    y = x32 * lax.rsqrt(jnp.mean(x32 * x32, axis=-1, keepdims=True) + NORM_EPS) * g.astype(jnp.float32)
    return y.astype(x.dtype)

def swiglu(x, w_gate, w_up, w_down):
    return (jax.nn.silu(x @ w_gate) * (x @ w_up)) @ w_down

def _linear_combine(e1, e2):
    a1, b1 = e1
    a2, b2 = e2
    return a1 * a2, a2 * b1 + b2

def partial_rope(t, positions):
    half = ROPE_DIM // 2
    inv_freq = ROPE_THETA ** (-(jnp.arange(half, dtype=jnp.float32) * 2.0 / ROPE_DIM))
    ang = positions.astype(jnp.float32)[..., None] * inv_freq
    cos = jnp.cos(ang)[:, :, None, :]
    sin = jnp.sin(ang)[:, :, None, :]
    t1 = t[..., :half]
    t2 = t[..., half:ROPE_DIM]
    return jnp.concatenate([t1 * cos - t2 * sin, t2 * cos + t1 * sin, t[..., ROPE_DIM:]], axis=-1)

def _dilated_branch(q, k, v, window, dilation):
    b, s, h, c = q.shape
    L = s // dilation
    nb = -(-L // ATT_BLOCK)
    Lp = nb * ATT_BLOCK
    span = window // dilation

    def strided(t):
        t = t.reshape(b, L, dilation, h, c).transpose(0, 2, 1, 3, 4)
        return jnp.pad(t, ((0, 0), (0, 0), (0, Lp - L), (0, 0), (0, 0)))

    def band(t):
        t = jnp.pad(strided(t), ((0, 0), (0, 0), (ATT_BLOCK, 0), (0, 0), (0, 0)))
        t = t.reshape(b, dilation, nb + 1, ATT_BLOCK, h, c)
        return jnp.concatenate([t[:, :, :-1], t[:, :, 1:]], axis=3)

    qb = strided(q).reshape(b, dilation, nb, ATT_BLOCK, h, c)
    kb = band(k)
    vb = band(v)
    scores = jnp.einsum('brnqhc,brnkhc->brnhqk', qb, kb)
    qi = jnp.arange(ATT_BLOCK)[:, None] + ATT_BLOCK
    ki = jnp.arange(2 * ATT_BLOCK)[None, :]
    dist = qi - ki
    kpos = jnp.arange(nb)[:, None, None] * ATT_BLOCK + ki[None] - ATT_BLOCK
    mask = ((dist >= 0) & (dist <= span))[None] & (kpos >= 0)
    scores = jnp.where(mask[None, None, :, None], scores, NEG_INF)
    m = jnp.max(scores, axis=-1)
    p = jnp.exp(scores - m[..., None])
    l = jnp.sum(p, axis=-1)
    acc = jnp.einsum('brnhqk,brnkhc->brnqhc', p, vb)

    def unstride(t):
        t = t.reshape((b, dilation, Lp) + t.shape[4:])[:, :, :L]
        t = jnp.moveaxis(t, 1, 2)
        return t.reshape((b, s) + t.shape[3:])

    m = jnp.moveaxis(m, -1, 3)
    l = jnp.moveaxis(l, -1, 3)
    return unstride(acc), unstride(m), unstride(l)

def dilated_attention(q, k, v):
    outs = [_dilated_branch(q, k, v, w, d) for (w, d) in DILATED_BRANCHES]
    acc_all = jnp.stack([o[0] for o in outs])
    m_all = jnp.stack([o[1] for o in outs])
    l_all = jnp.stack([o[2] for o in outs])
    wts = jnp.exp(m_all - jnp.max(m_all, axis=0, keepdims=True))
    num = jnp.einsum('ibsh,ibshc->bshc', wts, acc_all)
    den = jnp.sum(wts * l_all, axis=0)
    return num / den[..., None]

def s5_mixer(u, a_re, a_im, log_dt, b_re, b_im, c_re, c_im, d_skip, w_glu):
    b, s, _ = u.shape
    u = u.reshape(b, s, SSM_GROUPS, SSM_GROUP)
    f32 = jnp.float32
    A = lax.complex(a_re.astype(f32), a_im.astype(f32))
    dt = jnp.exp(log_dt.astype(f32))[:, None]
    a_bar = jnp.exp(A * dt)
    b_bar = ((a_bar - 1.0) / A)[..., None] * lax.complex(b_re.astype(f32), b_im.astype(f32))
    bu = jnp.einsum('gpc,bsgc->bsgp', b_bar, u.astype(jnp.complex64))
    a_seq = jnp.broadcast_to(a_bar, (s,) + a_bar.shape)
    h = jax.vmap(lambda bu_b: lax.associative_scan(_linear_combine, (a_seq, bu_b), axis=0)[1])(bu)
    c_mat = lax.complex(c_re.astype(f32), c_im.astype(f32))
    y = jnp.einsum('gcp,bsgp->bsgc', c_mat, h).real + d_skip.astype(f32) * u
    y = jax.nn.gelu(y.reshape(b, s, SSM_WIDTH))
    return y * jax.nn.sigmoid(y @ w_glu.astype(f32))

def rglru_mixer(xb, conv_w, conv_b, w_r, b_r, w_i, b_i, lam):
    b, s, r = xb.shape
    f32 = jnp.float32
    xc = lax.conv_general_dilated(xb, conv_w.astype(f32)[:, None, :], window_strides=(1,),
                                  padding=[(CONV_WIDTH - 1, 0)],
                                  dimension_numbers=('NWC', 'WIO', 'NWC'),
                                  feature_group_count=r) + conv_b.astype(f32)
    xh = xc.reshape(b, s, LRU_BLOCKS, LRU_BLOCK_DIM)
    gate_r = jax.nn.sigmoid(jnp.einsum('bshi,hij->bshj', xh, w_r.astype(f32)).reshape(b, s, r) + b_r.astype(f32))
    gate_i = jax.nn.sigmoid(jnp.einsum('bshi,hij->bshj', xh, w_i.astype(f32)).reshape(b, s, r) + b_i.astype(f32))
    log_a = -RG_C * gate_r * jax.nn.softplus(-lam.astype(f32))
    a = jnp.exp(log_a)
    mult = jnp.sqrt(-jnp.expm1(2.0 * log_a))
    _, h = lax.associative_scan(_linear_combine, (a, mult * (gate_i * xc)), axis=1)
    return h

def even_mixer(xn, positions, w_in, w_out, a_re, a_im, log_dt, b_re, b_im, c_re, c_im, d_skip, w_glu):
    b, s, _ = xn.shape
    z = (xn @ w_in).astype(jnp.float32)
    q = z[..., :ATT_WIDTH].reshape(b, s, ATT_HEADS, HEAD_DIM)
    k = z[..., ATT_WIDTH:2 * ATT_WIDTH].reshape(b, s, ATT_HEADS, HEAD_DIM)
    v = z[..., 2 * ATT_WIDTH:3 * ATT_WIDTH].reshape(b, s, ATT_HEADS, HEAD_DIM)
    u = z[..., 3 * ATT_WIDTH:]
    q = partial_rope(q, positions) * (HEAD_DIM ** -0.5)
    k = partial_rope(k, positions)
    att = dilated_attention(q, k, v).reshape(b, s, ATT_WIDTH)
    ssm = s5_mixer(u, a_re, a_im, log_dt, b_re, b_im, c_re, c_im, d_skip, w_glu)
    y = jnp.concatenate([att, ssm], axis=-1).astype(w_out.dtype)
    return (y @ w_out).astype(xn.dtype)

def odd_mixer(xn, w_in, w_out, conv_w, conv_b, w_r, b_r, w_i, b_i, lam):
    z = (xn @ w_in).astype(jnp.float32)
    h = rglru_mixer(z[..., :LRU_WIDTH], conv_w, conv_b, w_r, b_r, w_i, b_i, lam)
    y = (h * jax.nn.gelu(z[..., LRU_WIDTH:])).astype(w_out.dtype)
    return (y @ w_out).astype(xn.dtype)

def second_inputs(seed: int = 0) -> dict:
    key = jax.random.key(seed)
    ks = iter(jax.random.split(key, 32))
    f32 = jnp.float32

    def nrm(shape, scale):
        return jax.random.normal(next(ks), shape, f32) * scale

    G, P, NC, BD = SSM_GROUPS, SSM_STATE, SSM_GROUP, LRU_BLOCK_DIM
    x = nrm((BATCH, SEQ, D_MODEL), 1.0)
    offset = jax.random.randint(next(ks), (BATCH, 1), 0, SEQ, dtype=jnp.int32)
    positions = offset + jnp.arange(SEQ, dtype=jnp.int32)[None, :]
    norm_mix_pre = 1.0 + nrm((DEPTH, D_MODEL), 0.05)
    norm_mix_post = 1.0 + nrm((DEPTH, D_MODEL), 0.05)
    norm_ffn_pre = 1.0 + nrm((DEPTH, D_MODEL), 0.05)
    norm_ffn_post = 1.0 + nrm((DEPTH, D_MODEL), 0.05)
    ev_w_in = nrm((N_EVEN, D_MODEL, EVEN_IN), D_MODEL ** -0.5)
    ev_w_out = nrm((N_EVEN, D_MODEL, D_MODEL), D_MODEL ** -0.5)
    s5_a_re = -0.5 * jnp.exp(nrm((N_EVEN, G, P), 0.02))
    s5_a_im = jnp.pi * jnp.arange(P, dtype=f32) + nrm((N_EVEN, G, P), 0.02)
    s5_log_dt = jax.random.uniform(next(ks), (N_EVEN, G), f32, math.log(1e-3), math.log(1e-1))
    s5_b_re = nrm((N_EVEN, G, P, NC), (2 * NC) ** -0.5)
    s5_b_im = nrm((N_EVEN, G, P, NC), (2 * NC) ** -0.5)
    s5_c_re = nrm((N_EVEN, G, NC, P), (2 * P) ** -0.5)
    s5_c_im = nrm((N_EVEN, G, NC, P), (2 * P) ** -0.5)
    s5_d = nrm((N_EVEN, G, NC), 1.0)
    s5_w_glu = nrm((N_EVEN, SSM_WIDTH, SSM_WIDTH), SSM_WIDTH ** -0.5)
    od_w_in = nrm((N_ODD, D_MODEL, 2 * LRU_WIDTH), D_MODEL ** -0.5)
    od_w_out = nrm((N_ODD, LRU_WIDTH, D_MODEL), LRU_WIDTH ** -0.5)
    rg_conv_w = nrm((N_ODD, CONV_WIDTH, LRU_WIDTH), CONV_WIDTH ** -0.5)
    rg_conv_b = nrm((N_ODD, LRU_WIDTH), 0.01)
    rg_w_r = nrm((N_ODD, LRU_BLOCKS, BD, BD), BD ** -0.5)
    rg_b_r = nrm((N_ODD, LRU_WIDTH), 0.01)
    rg_w_i = nrm((N_ODD, LRU_BLOCKS, BD, BD), BD ** -0.5)
    rg_b_i = nrm((N_ODD, LRU_WIDTH), 0.01)
    a0 = jax.random.uniform(next(ks), (N_ODD, LRU_WIDTH), f32, 0.9, 0.999)
    sig = a0 ** (1.0 / RG_C)
    rg_lam = jnp.log(sig) - jnp.log1p(-sig)
    ffn_w_gate = nrm((DEPTH, D_MODEL, FFN_HIDDEN), D_MODEL ** -0.5)
    ffn_w_up = nrm((DEPTH, D_MODEL, FFN_HIDDEN), D_MODEL ** -0.5)
    ffn_w_down = nrm((DEPTH, FFN_HIDDEN, D_MODEL), FFN_HIDDEN ** -0.5)
    return {'x': x, 'positions': positions,
            'norm_mix_pre': norm_mix_pre, 'norm_mix_post': norm_mix_post,
            'norm_ffn_pre': norm_ffn_pre, 'norm_ffn_post': norm_ffn_post,
            'ev_w_in': ev_w_in, 'ev_w_out': ev_w_out,
            's5_a_re': s5_a_re, 's5_a_im': s5_a_im, 's5_log_dt': s5_log_dt,
            's5_b_re': s5_b_re, 's5_b_im': s5_b_im, 's5_c_re': s5_c_re, 's5_c_im': s5_c_im,
            's5_d': s5_d, 's5_w_glu': s5_w_glu,
            'od_w_in': od_w_in, 'od_w_out': od_w_out,
            'rg_conv_w': rg_conv_w, 'rg_conv_b': rg_conv_b,
            'rg_w_r': rg_w_r, 'rg_b_r': rg_b_r, 'rg_w_i': rg_w_i, 'rg_b_i': rg_b_i, 'rg_lam': rg_lam,
            'ffn_w_gate': ffn_w_gate, 'ffn_w_up': ffn_w_up, 'ffn_w_down': ffn_w_down}

def second_block(x, positions, norm_mix_pre, norm_mix_post, norm_ffn_pre, norm_ffn_post,
              ev_w_in, ev_w_out, s5_a_re, s5_a_im, s5_log_dt, s5_b_re, s5_b_im, s5_c_re, s5_c_im,
              s5_d, s5_w_glu, od_w_in, od_w_out, rg_conv_w, rg_conv_b, rg_w_r, rg_b_r, rg_w_i, rg_b_i,
              rg_lam, ffn_w_gate, ffn_w_up, ffn_w_down):
    for layer in range(DEPTH):
        hn = rms_norm(x, norm_mix_pre[layer])
        if layer % 2 == 0:
            e = layer // 2
            mix = even_mixer(hn, positions, ev_w_in[e], ev_w_out[e], s5_a_re[e], s5_a_im[e],
                             s5_log_dt[e], s5_b_re[e], s5_b_im[e], s5_c_re[e], s5_c_im[e],
                             s5_d[e], s5_w_glu[e])
        else:
            o = layer // 2
            mix = odd_mixer(hn, od_w_in[o], od_w_out[o], rg_conv_w[o], rg_conv_b[o],
                            rg_w_r[o], rg_b_r[o], rg_w_i[o], rg_b_i[o], rg_lam[o])
        x = x + rms_norm(mix, norm_mix_post[layer])
        hn = rms_norm(x, norm_ffn_pre[layer])
        ff = swiglu(hn, ffn_w_gate[layer], ffn_w_up[layer], ffn_w_down[layer])
        x = x + rms_norm(ff, norm_ffn_post[layer])
    return x


def setup_inputs(seed=0):
    out = dict(first_inputs(seed))
    for name, value in second_inputs(seed + 1).items():
        if name != "x":
            out[name + "_2"] = value
    return out


def reference(
    x, c, ctx, c_ctx, w_ada, b_ada, ln_g, ln_b, w_in_ab, w_out_ab, sink_ab, conv_ab, w_in_c,
    w_out_c, lb_c, gnorm_c, positions_2, norm_mix_pre_2, norm_mix_post_2, norm_ffn_pre_2,
    norm_ffn_post_2, ev_w_in_2, ev_w_out_2, s5_a_re_2, s5_a_im_2, s5_log_dt_2, s5_b_re_2,
    s5_b_im_2, s5_c_re_2, s5_c_im_2, s5_d_2, s5_w_glu_2, od_w_in_2, od_w_out_2, rg_conv_w_2,
    rg_conv_b_2, rg_w_r_2, rg_b_r_2, rg_w_i_2, rg_b_i_2, rg_lam_2, ffn_w_gate_2, ffn_w_up_2,
    ffn_w_down_2,
):
    x = first_block(
        x, c, ctx, c_ctx, w_ada, b_ada, ln_g, ln_b, w_in_ab, w_out_ab, sink_ab, conv_ab, w_in_c,
        w_out_c, lb_c, gnorm_c,
    )
    return second_block(
        x, positions_2, norm_mix_pre_2, norm_mix_post_2, norm_ffn_pre_2, norm_ffn_post_2,
        ev_w_in_2, ev_w_out_2, s5_a_re_2, s5_a_im_2, s5_log_dt_2, s5_b_re_2, s5_b_im_2,
        s5_c_re_2, s5_c_im_2, s5_d_2, s5_w_glu_2, od_w_in_2, od_w_out_2, rg_conv_w_2,
        rg_conv_b_2, rg_w_r_2, rg_b_r_2, rg_w_i_2, rg_b_i_2, rg_lam_2, ffn_w_gate_2, ffn_w_up_2,
        ffn_w_down_2,
    )


_drawn_inputs = setup_inputs


def setup_inputs(seed=0):
    import zlib

    import numpy as np

    out = dict(_drawn_inputs(seed))
    spreads = {}
    factors = {'ctx': 3.771,
     'sink_ab': 64.0,
     'gnorm_c': 6.724,
     's5_a_re_2': 200.0,
     'rg_conv_b_2': 3.287,
     'rg_b_r_2': 62.602,
     'rg_b_i_2': 26.327,
     's5_a_im_2': 30.32,
     's5_log_dt_2': 36.08,
     's5_b_re_2': 42.248,
     's5_b_im_2': 40.176,
     's5_c_re_2': 41.632,
     's5_c_im_2': 40.872}
    for name, (base, spread) in spreads.items():
        noise = np.random.default_rng([zlib.crc32(name.encode()), seed]).standard_normal(out[name].shape)
        drawn = base * np.exp(spread * noise) if base else spread * noise
        out[name] = __import__('jax').numpy.asarray(drawn.astype(out[name].dtype))
    for name, factor in factors.items():
        out[name] = (out[name] * factor).astype(out[name].dtype)
    return out
```

```python
from contextlib import ExitStack

import numpy as np

import concourse.bass as bass
from concourse import mybir

F32 = mybir.dt.float32
U32 = mybir.dt.uint32
I32 = mybir.dt.int32
ALU = mybir.AluOpType
ACT = mybir.ActivationFunctionType
AX = mybir.AxisListType

P = 128
D = 1024
KD = D // P
L = 512
LC = 256
TL = L // P
TC = LC // P
LT = L + LC
HEADS = 8
DH = 64
AW = HEADS * DH
NEG = -1e30
ALPHA = 4.0 ** 0.25
LN_EPS = 1e-5
RMS_EPS = 1e-6
FFN = 2816
KF = FFN // P
WC = 256
WSLOTS = 4
HH = 4
LEVELS = (64, 32, 16, 8, 4, 2, 1)
TWO_PI = 2.0 * np.pi
MAGIC = 12582912.0


def table_layout():
    sizes = [("ident", P), ("ones", P), ("win_lo", P), ("win_hi", P), ("dil", 1280),
             ("lv_f", 64 * len(LEVELS)), ("lv_b", 64 * len(LEVELS)), ("rot_ax", P), ("rot_pt", P),
             ("cos_ax", L), ("sin_ax", L), ("chunk", L), ("cols", 8)]
    at, out = 0, {}
    for name, n in sizes:
        out[name] = (at, at + n)
        at += n
    return out, at


def make_tables():
    lay, width = table_layout()
    t = np.zeros((P, width), np.float32)

    def put(name, a):
        t[:, lay[name][0]:lay[name][1]] = a

    i = np.arange(P)
    put("ident", np.eye(P))
    put("ones", 1.0)
    put("win_lo", np.where(i[None, :] >= i[:, None], 0.0, NEG))
    put("win_hi", np.where(i[None, :] <= i[:, None], 0.0, NEG))
    off = 0
    for qt in range(TL):
        q = qt * P + i[:, None]
        k = np.arange((qt + 1) * P)[None, :]
        d = q - k
        n = ((d >= 0) & (d <= 128)).astype(int) + ((d >= 0) & (d % 4 == 0)) + ((d >= 0) & (d % 16 == 0))
        b = np.where(n > 0, 8.0 * np.log(np.maximum(n, 1)), NEG)
        t[:, lay["dil"][0] + off:lay["dil"][0] + off + (qt + 1) * P] = b
        off += (qt + 1) * P
    for li, h in enumerate(LEVELS):
        right = np.array([c for c in range(P) if (c // h) % 2 == 1])
        left = np.array([c for c in range(P) if (c // h) % 2 == 0])
        f = (i[:, None] // (2 * h) == right[None, :] // (2 * h)) & ((i[:, None] // h) % 2 == 0)
        b = (i[:, None] // (2 * h) == left[None, :] // (2 * h)) & ((i[:, None] // h) % 2 == 1)
        t[:, lay["lv_f"][0] + 64 * li:lay["lv_f"][0] + 64 * li + 64] = f
        t[:, lay["lv_b"][0] + 64 * li:lay["lv_b"][0] + 64 * li + 64] = b

    def rotation(period, half, used):
        r = np.zeros((P, P), np.float32)
        for m in range(P):
            o = m % period
            if o < used:
                if o < half:
                    r[m + half, m] = -1.0
                else:
                    r[m - half, m] = 1.0
        return r

    put("rot_ax", rotation(32, 16, 32))
    put("rot_pt", rotation(64, 8, 16))
    freqs = (np.float32(10000.0) ** (-np.arange(16, dtype=np.float32) / np.float32(16))).astype(np.float32)
    tok = np.arange(L)
    for p in range(P):
        o = p % DH
        pos = (tok // 64 if o < 32 else tok % 64).astype(np.float32)
        ang = pos * freqs[o % 16]
        t[p, lay["cos_ax"][0]:lay["cos_ax"][1]] = np.cos(ang)
        t[p, lay["sin_ax"][0]:lay["sin_ax"][1]] = np.sin(ang)
    put("chunk", (np.arange(L) % P != 0).astype(np.float32)[None, :])
    inv = (np.float32(500000.0) ** -(np.arange(8, dtype=np.float32) * np.float32(2.0) / np.float32(16))).astype(np.float32)
    c0 = lay["cols"][0]
    for p in range(P):
        o = p % DH
        t[p, c0] = inv[o % 8] if o < 16 else 0.0
    t[:, c0 + 2] = (i // 16) % 2 == 0
    t[:, c0 + 3] = (i // 16) % 2 == 1
    t[:, c0 + 4] = i // DH == 0
    t[:, c0 + 5] = i // DH == 1
    return t


def program(nc, a, out, stop=99, dumps=()):
    lay, tw = table_layout()
    ctx = ExitStack()
    with ctx:
        sems = {}

        def sem(name):
            if name not in sems:
                sems[name] = ctx.enter_context(nc.semaphore(name))
            return sems[name]

        arena = ctx.enter_context(nc.sbuf_tensor("arena", [P, 53100], F32))
        top = [0]

        def take_words(n):
            top[0] += n
            assert top[0] <= 53100, top[0]
            return top[0] - n

        def view(at, *dims):
            n = int(np.prod(dims))
            v = arena[:, at:at + n]
            if len(dims) == 2:
                v = v.rearrange("p (a b) -> p a b", a=dims[0])
            if len(dims) == 3:
                v = v.rearrange("p (a b c) -> p a b c", a=dims[0], b=dims[1])
            return v

        TAB = view(take_words(tw), tw)

        def tab(name, lo=0, hi=None):
            s, e = lay[name]
            return TAB[:, s + lo:(e if hi is None else s + hi)]

        IDENT, ONES = tab("ident"), tab("ones")
        VEC = view(take_words(256), 256)
        MOD = view(take_words(96), 2, 24, 2)
        SC = view(take_words(16), KD, 2)
        SM = view(take_words(512), 512)
        BC = view(take_words(2 * D), 2, D)
        gt_at = take_words(2 * D)
        GT = view(gt_at, 2, D)
        x_at = take_words(6 * D)
        X = view(x_at, 6, D)
        ht_at = take_words(KD * LT)
        HT = view(ht_at, KD, LT)
        WR = view(take_words(WSLOTS * KD * WC), WSLOTS, KD, WC)
        work = top[0]
        free = 53100 - work

        ring = [ctx.enter_context(nc.psum_tensor(f"ring{i}", [P, 1024], F32)) for i in range(3)]
        obank = [ctx.enter_context(nc.psum_tensor(f"obank{i}", [P, 512], F32)) for i in range(2)]

        filled = sem("psum_filled")
        emptied = {"v": sem("dve_emptied"), "a": sem("act_emptied")}
        units, order, by_engine = {}, [], {"v": 0, "a": 0}
        chunks = []
        wload = [sem(f"weights{i}") for i in range(WSLOTS)]
        wcount = [0] * WSLOTS
        wused = sem("weights_used")
        released = []

        w = work
        AQ = view(w, 4, LT)
        AKV = view(w + 3072, 2, LT)
        AGA = view(w + 4608, 4, LT)
        AGB = view(w + 7680, 4, LT)
        AU = view(w + 10752, 4, LT + 4)
        AVT = view(w + 13840, 6, P)
        APB = view(w + 14608, 2, 640)
        APT = view(w + 15888, 2, 640)
        AOT = view(w + 17168, 2, AW)
        ACV = view(w + 18192, 2, LT)
        ROT = view(w + 14608, 2, L)
        DG = view(w + 14608, KD, P)
        VR = view(w, 2, P)
        ATMP = view(w, 4, WC)

        CQ = view(w, HH, L)
        CI = view(w + 2048, 6, HH * P)
        CZ = view(w + 5120, HH, LT)
        CT_ = view(w + 8192, HH, LT)
        CK = view(w + 11264, HH, LT)
        CP = view(w + 14336, HH, LT)
        CSC = view(w + 17408, TL * HH, P)
        CKT = view(w + 19456, HH, P)
        CDG = view(w + 19968, 8, P)
        CW = [view(w + 5120, HH, L), view(w + 8192, HH, L)]
        CS = view(gt_at + D, HH, P)
        CG = view(w, TL, D)
        CSQ = view(w + 5120, 1, D)
        CTMP = view(w + 6144, TL, WC)
        co_at = [x_at + 4 * D, x_at + 5 * D, w + 20992, w + 20992 + D]
        CO = [view(at, D) for at in co_at]
        GN = SM[:, 376:504]
        assert w + 20992 + 2 * D <= 53100, free
        EQK = view(w, 8, L)
        EV = view(w + 4096, TL, AW)
        EU = view(w + 6144, 4, L)
        EPB = view(w + 8192, 2, L)
        EPT = view(w + 9216, 2, L)
        EOT = view(w + 10240, 2, AW)
        EROT = view(w + 8192, 2, L)
        EPOS = view(w + 8192, L)
        COSP, SINP = tab("cos_ax"), tab("sin_ax")
        s5 = w + 11264
        SER, SEI = view(s5, 4, L), view(s5 + 2048, 4, L)
        SBR, SBI = view(s5 + 4096, 4, L), view(s5 + 6144, 4, L)
        SHR, SHI = view(gt_at, 4, L), view(x_at + 4 * D, 4, L)
        SBD = [view(s5 + 8192 + 512 * i, 4, P) for i in range(2)]
        SCD = [view(s5 + 9216 + 512 * i, 4, P) for i in range(2)]
        SPR = view(s5 + 10240, 32, 16)
        SP1, SP2 = view(s5 + 10752, L), view(s5 + 11264, L)
        SBRAW = [view(s5 + 4096 + 256 * i, 16, 16) for i in range(2)]
        SBBL = [view(s5 + 4608 + 512 * i, 16, 32) for i in range(2)]
        SCRAW = [view(s5 + 5632 + 256 * i, 4, DH) for i in range(2)]
        SCEX = [view(s5 + 6144 + 512 * i, 4, P) for i in range(2)]
        SROW = view(s5 + 7168, P)
        assert s5 + 11264 + L <= 53100
        XN = view(s5, TL, D)
        MX = view(w, TL, D)
        FH = view(w, KF, L)
        FSG = view(w + 11264, 2, 2, L)
        FX = view(w + 13312, TL, D)
        RXB = view(w, 8, L + 4)
        RZG = view(w + 4128, 8, L)
        RXC = view(w + 8224, 8, L)
        RA = view(w + 12320, 8, L)
        RGI = view(w + 16416, 8, L)
        RTH = view(w, 8, L)
        RM = HT[:, :, 0:L]

        class Chain:

            def __init__(self, eng, name):
                self.eng, self.sem, self.n = eng, sem(name), 0

            def link(self, ins):
                ins.then_inc(self.sem, 1)
                self.n += 1
                self.eng.wait_ge(self.sem, self.n)

        def read_of(label):
            _, e, k = units[label]
            return emptied[e], k

        def fill_of(label):
            return filled, units[label][0] + 1

        def bank(label):
            return ring[units[label][0] % 3]

        block = ctx.enter_context(nc.Block())

        V_C, V_CC, V_BADA, V_CONV, V_NPRE, V_NFFN = 0, 8, 16, 64, 76, 92
        V_D, V_RCW, V_RCB, V_BR, V_BI, V_LAM = 128, 132, 164, 172, 180, 188

        ROWS = [(V_C, a["c"].rearrange("o (r n) -> (o r) n", n=P), 8),
                (V_CC, a["c_ctx"].rearrange("(r n) -> r n", n=P), 8),
                (V_BADA, a["b_ada"].rearrange("l (r n) -> (l r) n", n=P), 48),
                (V_CONV, a["conv_ab"].rearrange("o j (r n) -> (o j r) n", n=P), 12),
                (V_NPRE, a["norm_mix_pre_2"].rearrange("l (r n) -> (l r) n", n=P), 16),
                (V_NFFN, a["norm_ffn_pre_2"].rearrange("l (r n) -> (l r) n", n=P), 16),
                (V_D, a["s5_d_2"].rearrange("o (r g) c -> (o r) (g c)", r=4), 4),
                (V_RCW, a["rg_conv_w_2"].rearrange("o j (r n) -> (o j r) n", n=P), 32),
                (V_RCB, a["rg_conv_b_2"].rearrange("o (r n) -> (o r) n", n=P), 8),
                (V_BR, a["rg_b_r_2"].rearrange("o (r n) -> (o r) n", n=P), 8),
                (V_BI, a["rg_b_i_2"].rearrange("o (r n) -> (o r) n", n=P), 8),
                (V_LAM, a["rg_lam_2"].rearrange("o (r n) -> (o r) n", n=P), 8)]

        def cols(wap, c0, n=WC, k0=0, kt=KD):
            return [(0, n, wap[k0 * P:(k0 + kt) * P, c0:c0 + n].rearrange("(k p) n -> p k n", p=P))]

        def att_blocks(kind, qt):
            if kind == "A":
                b = [(L, TL, None), (L + P, TL + 1, None)]
                if qt < TL:
                    if qt > 0:
                        b.append(((qt - 1) * P, qt - 1, tab("win_lo")))
                    b.append((qt * P, qt, None))
                    if qt < TL - 1:
                        b.append(((qt + 1) * P, qt + 1, tab("win_hi")))
                return b
            off = P * (qt * (qt + 1) // 2)
            return [(k * P, k, tab("dil", off + k * P, off + (k + 1) * P)) for k in range(qt + 1)]

        def att_events(n):
            for i in range(n + 2):
                if i < n:
                    yield "scores", i
                if 0 <= i - 1 < n:
                    yield "turn", i - 1
                if 0 <= i - 2:
                    yield "values", i - 2
                    if (i - 2) % HEADS == HEADS - 1:
                        yield "finish", (i - 2) // HEADS

        NT_ATT = {"A": TL + TC, "E": TL}

        def hg_seq(d):
            c, l = [TL, TL + 1], list(range(TL))
            return c + l if d == 0 else c[::-1] + l[::-1]

        def pos(ap, n, h, side):
            return ap.rearrange("p g (b s h) -> p g b s h", s=2, h=h)[:, :, :, side, :]

        @block.tensor
        def _(pe):
            def take(label, engine):
                n = len(order)
                if n >= 3:
                    e, k = units[order[n - 3]][1:]
                    pe.wait_ge(emptied[e], k)
                by_engine[engine] += 1
                units[label] = (n, engine, by_engine[engine])
                order.append(label)
                return ring[n % 3]

            def chunk(pieces, kt=KD):
                n = len(chunks)
                s = n % WSLOTS
                chunks.append((pieces, kt))
                wcount[s] += 16 * len(pieces)
                pe.wait_ge(wload[s], wcount[s])
                return WR[:, s]

            def used_with_unit():
                released.append((filled, len(order)))

            def used_now(last):
                last.then_inc(wused, 1)
                released.append((wused, 1 + sum(x is wused for x, _ in released)))

            def gemm_f(name, wt, c0, n, ctx_on, eng, lat_on=True, pieces=None, lhs=None, rhs=HT):
                wv = chunk(pieces or cols(wt, c0, n))
                lhs = lhs or (lambda wv, k, m: wv[:, k, m * P:(m + 1) * P])
                mts = n // P
                if lat_on:
                    ps = take(name + ".lat", eng)
                    for m in range(mts):
                        for k in range(KD):
                            last = pe.matmul(ps[:, m * L:(m + 1) * L], lhs(wv, k, m), rhs[:, k, 0:L],
                                             start=k == 0, stop=k == KD - 1)
                    last.then_inc(filled, 1)
                if ctx_on:
                    ps = take(name + ".ctx", eng)
                    for m in range(mts):
                        for k in range(KD):
                            last = pe.matmul(ps[:, m * LC:(m + 1) * LC], lhs(wv, k, m), rhs[:, k, L:LT],
                                             start=k == 0, stop=k == KD - 1)
                    last.then_inc(filled, 1)
                used_with_unit()

            def gemm_t(name, wt, c0, tiles, eng, act=HT, kts=(KD,)):
                groups = [g for g in (range(0, 4), range(4, 6)) if g.start < tiles]
                if len(kts) > 1:
                    ps = take(name + ".t0", eng)
                    k0 = 0
                    for ci, kt in enumerate(kts):
                        wv = chunk(cols(wt, c0, WC, k0, kt), kt)
                        for t in range(4):
                            for k in range(kt):
                                last = pe.matmul(ps[:, t * WC:(t + 1) * WC], act[:, k0 + k, t * P:(t + 1) * P],
                                                 wv[:, k, :], start=ci == 0 and k == 0 and t % 2 == 0,
                                                 stop=ci == len(kts) - 1 and k == kt - 1,
                                                 skip_group_check=True)
                        k0 += kt
                        if ci < len(kts) - 1:
                            used_now(last)
                    last.then_inc(filled, 1)
                    used_with_unit()
                    return
                wv = chunk(cols(wt, c0))
                for gi, g in enumerate(groups):
                    ps = take(f"{name}.t{gi}", eng)
                    for j, t in enumerate(g):
                        for k in range(KD):
                            last = pe.matmul(ps[:, j * WC:(j + 1) * WC], act[:, k, t * P:(t + 1) * P],
                                             wv[:, k, :], start=k == 0, stop=k == KD - 1)
                    last.then_inc(filled, 1)
                used_with_unit()

            def turn_tiles(name, src, tiles, eng, at=None):
                for t in tiles:
                    ps = take(f"{name}{t}", eng)
                    for k in range(KD):
                        x = at(t, k) if at else src[:, t, k * P:(k + 1) * P]
                        last = pe.transpose(ps[:, k * P:(k + 1) * P], x, IDENT)
                    last.then_inc(filled, 1)

            def mod_layer(l):
                for g in range(3):
                    ps = take(f"mod{l}.{g}", "v")
                    for ci in range(4):
                        wv = chunk(cols(a["w_ada"][l], g * D + ci * WC))
                        for m in range(2):
                            o = 4 * ci + 2 * m
                            for k in range(KD):
                                last = pe.matmul(ps[:, o:o + 2], wv[:, k, m * P:(m + 1) * P], SC[:, k, :],
                                                 start=k == 0, stop=k == KD - 1)
                        if ci < 3:
                            used_now(last)
                    last.then_inc(filled, 1)
                    used_with_unit()

            def gate_rows(l, n):
                for j in range(n):
                    pe.wait_ge(sem(f"gate_diag{l}"), j + 1)
                    ps = take(f"gate{l}.{j}", "a")
                    for h in range(2):
                        last = pe.matmul(ps[:, h * 512:(h + 1) * 512], ONES, DG[:, 4 * h:4 * h + 4, :],
                                         start=True, stop=True)
                    last.then_inc(filled, 1)

            def attention(kind, q_of, k_of, v_of, PB, PT, OT, width):
                n = NT_ATT[kind] * HEADS
                for what, i in att_events(n):
                    qt, h = divmod(i, HEADS)
                    if what == "scores":
                        blocks = att_blocks(kind, qt)
                        ps = take(f"{kind}s{i}", "a")
                        for b, (c0, _, mask) in enumerate(blocks):
                            o = ps[:, b * P:(b + 1) * P]
                            last = pe.matmul(o, q_of(h, qt), k_of(h, c0), start=True, stop=mask is None)
                            if mask is not None:
                                last = pe.matmul(o, IDENT, mask, start=False, stop=True)
                        last.then_inc(filled, 1)
                    elif what == "turn":
                        pe.wait_ge(*read_of(f"{kind}s{i}"))
                        ps = take(f"{kind}t{i}", "v" if i % 2 else "a")
                        for b in range(len(att_blocks(kind, qt))):
                            last = pe.transpose(ps[:, b * P:(b + 1) * P], PB[:, i % 2, b * P:(b + 1) * P], IDENT)
                        last.then_inc(filled, 1)
                    elif what == "values":
                        pe.wait_ge(*read_of(f"{kind}t{i}"))
                        if h == 0 and qt >= 2:
                            pe.wait_ge(sem(f"{kind}_normed"), qt - 1)
                        blocks = att_blocks(kind, qt)
                        for b, (_, vt, _) in enumerate(blocks):
                            last = pe.matmul(obank[qt % 2][:, h * DH:(h + 1) * DH], PT[:, i % 2, b * P:(b + 1) * P],
                                             v_of(h, vt), start=b == 0, stop=b == len(blocks) - 1)
                        last.then_inc(sem(f"{kind}_values"), 1)
                    else:
                        qt = i
                        pe.wait_ge(sem(f"{kind}_normed"), qt + 1)
                        ps = take(f"{kind}o{qt}", "v")
                        for f in range(4):
                            last = pe.transpose(ps[:, f * P:(f + 1) * P], OT[:, qt % 2, f * P:(f + 1) * P], IDENT)
                        last.then_inc(filled, 1)

            pe.wait_ge(sem("tables_in"), 16)
            pe.wait_ge(sem("rows_in"), 16 * len(ROWS))
            ps = take("vec", "v")
            pe.transpose(ps[:, 0:108], VR[0:108, 0, :], IDENT[0:108, 0:108])
            pe.transpose(ps[:, 512:512 + 68], VR[0:68, 1, :], IDENT[0:68, 0:68]).then_inc(filled, 1)
            pe.wait_ge(sem("silu_c"), 1)
            mod_layer(0)
            gate_rows(0, 2)
            pe.wait_ge(sem("x_in"), 32)
            turn_tiles("h0.", X, range(6), "v")
            pe.wait_ge(*read_of("h0.5"))
            wab = a["w_in_ab"][0]
            for c in range(2):
                gemm_f(f"q{c}", wab, 0, WC, True, "a",
                       pieces=[(m * P + g * DH, DH, wab[:, (4 * g + 2 * c + m) * DH:(4 * g + 2 * c + m + 1) * DH]
                                .rearrange("(k p) n -> p k n", p=P)) for m in range(2) for g in range(2)])
            gemm_f("kv", wab, 512, WC, True, "a")
            for nm, c0, eng in (("ga", 768, "a"), ("gb", 2816, "a"), ("bg", 1792, "v"), ("xb", 1280, "v"), ("cg", 2304, "v")):
                for c in range(2):
                    gemm_f(f"{nm}{c}", wab, c0 + c * WC, WC, True, eng)
            pe.wait_ge(*read_of("kv.ctx"))
            for c, tl in enumerate(([(AQ, 0), (AQ, 1)], [(AQ, 2), (AQ, 3)], [(AKV, 0)])):
                ps = take(f"rope{c}", "v")
                for j, (src, i) in enumerate(tl):
                    last = pe.matmul(ps[:, j * L:(j + 1) * L], tab("rot_ax"), src[:, i, 0:L], start=True, stop=True)
                last.then_inc(filled, 1)
            ps = take("vtok", "a")
            for t in range(6):
                last = pe.transpose(ps[:, t * P:(t + 1) * P], AKV[:, 1, t * P:(t + 1) * P], IDENT)
            last.then_inc(filled, 1)
            pe.wait_ge(*read_of("vtok"))
            pe.wait_ge(sem("roped"), 3)
            attention("A", lambda h, qt: AQ[64 * (h // 4):64 * (h // 4) + 64, h % 4, qt * P:(qt + 1) * P],
                      lambda h, c0: AKV[64 * (h // 4):64 * (h // 4) + 64, 0, c0:c0 + P],
                      lambda h, vt: AVT[:, vt, 64 * (h // 4):64 * (h // 4) + 64], APB, APT, AOT, 640)
            pe.wait_ge(*read_of("Ao5"))
            pe.wait_ge(sem("conv"), 8)
            for c in range(4):
                gemm_t(f"y0.{c}", a["w_out_ab"][0], c * WC, 6, "v")
            if stop <= 1:
                return
            mod_layer(1)
            gate_rows(1, 1)
            pe.wait_ge(sem("x1_ready"), 6)
            turn_tiles("h1.", X, range(6), "v")
            pe.wait_ge(*read_of("h1.5"))
            wc = a["w_in_c"][0]
            for hh in range(2):
                for c in range(2):
                    gemm_f(f"cq{hh}{c}", wc, hh * 512 + c * WC, WC, False, "a")
                for c in range(2):
                    gemm_t(f"ci{hh}{c}", wc, 3072 + hh * 512 + c * WC, 6, "a")
                for d in range(2):
                    hd = f"{hh}{d}"
                    for c in range(2):
                        gemm_f(f"cz{hd}{c}", wc, 1024 * (1 + d) + hh * 512 + c * WC, WC, True, "v")
                    pe.wait_ge(sem("hg_k"), 2 * hh + d + 1)
                    pe.wait_ge(*read_of(f"cq{hh}1.lat"))
                    for g in range(2):
                        ps = take(f"dg{hd}{g}", "v")
                        for j in range(8):
                            ch, h = divmod(8 * g + j, HH)
                            last = pe.matmul(ps[:, j * P:(j + 1) * P], CK[:, h, ch * P:(ch + 1) * P],
                                             CQ[:, h, ch * P:(ch + 1) * P], start=True, stop=True)
                        last.then_inc(filled, 1)
                    pe.wait_ge(sem("hg_ks"), 2 * hh + d + 1)
                    pe.wait_ge(*read_of(f"ci{hh}1.t1"))
                    seq = hg_seq(d)
                    for i, ch in enumerate(seq):
                        tk = ch * P
                        if ch < TL:
                            if i == 2:
                                pe.wait_ge(sem("hg_qi"), 2 * hh + d + 1)
                            pe.wait_ge(*read_of(f"su{hd}{seq[i - 1]}"))
                            ps = take(f"oi{hd}{ch}", "v")
                            for h in range(HH):
                                last = pe.matmul(ps[:, h * P:(h + 1) * P], CT_[:, h, tk:tk + P], CS[:, h, :],
                                                 start=True, stop=True)
                            last.then_inc(filled, 1)
                        if i < 5:
                            ps = take(f"kt{hd}{ch}", "a")
                            for h in range(HH):
                                last = pe.transpose(ps[:, h * P:(h + 1) * P], CZ[:, h, tk:tk + P], IDENT)
                            last.then_inc(filled, 1)
                            pe.wait_ge(*read_of(f"kt{hd}{ch}"))
                            ps = take(f"su{hd}{ch}", "v")
                            for h in range(HH):
                                last = pe.matmul(ps[:, h * P:(h + 1) * P], CKT[:, h, :], CI[:, ch, h * P:(h + 1) * P],
                                                 start=True, stop=True)
                            last.then_inc(filled, 1)
                    for li, h2 in enumerate(LEVELS):
                        pe.wait_ge(sem("hg_w"), 7 * (2 * hh + d) + li + 1)
                        ps = take(f"lv{hd}{li}", "v")
                        W = CW[li % 2]
                        for j in range(TL * HH):
                            ch, h = divmod(j, HH)
                            rv = W[:, h, ch * P:(ch + 1) * P].rearrange("p (b s h) -> p b s h", s=2, h=h2)
                            last = pe.matmul(ps[:, j * 64:(j + 1) * 64], W[:, h, ch * P:(ch + 1) * P],
                                             rv[:, :, 1 - d, :], start=True, stop=True)
                        last.then_inc(filled, 1)
                pe.wait_ge(*read_of(f"lv{hh}16"))
                for ch in range(TL):
                    ps = take(f"oo{hh}{ch}", "v")
                    for h in range(HH):
                        last = pe.matmul(ps[:, h * P:(h + 1) * P], CSC[:, ch * HH + h, :],
                                         CI[:, ch, h * P:(h + 1) * P], start=True, stop=True)
                    last.then_inc(filled, 1)
            for c in range(4):
                gemm_t(f"cg{c}_", wc, 4096 + c * WC, 4, "a")
            pe.wait_ge(sem("c_y"), 4)
            turn_tiles("cy", None, range(4), "a", lambda t, k: CO[t][:, k * P:(k + 1) * P])
            pe.wait_ge(*read_of("cy3"))
            for c in range(4):
                gemm_t(f"y1.{c}", a["w_out_c"][0], c * WC, 4, "v")
            if stop <= 2:
                return
            def pre_norm(n, eng="v"):
                pe.wait_ge(sem("xn_ready"), 4 * n)
                turn_tiles(f"n{n}.", FX if n in (2, 4) else XN, range(TL), eng)
                pe.wait_ge(*read_of(f"n{n}.3"))

            pre_norm(1)
            we = a["ev_w_in_2"][0]
            for c in range(4):
                gemm_f(f"eqk{c}", we, c * WC, WC, False, "a")
            for c in range(2):
                gemm_t(f"ev{c}", we, 2 * AW + c * WC, TL, "a")
            for c in range(2):
                gemm_f(f"eu{c}", we, 3 * AW + c * WC, WC, False, "a")
            for c in range(4):
                ps = take(f"erope{c}", "v")
                for j in range(2):
                    last = pe.matmul(ps[:, j * L:(j + 1) * L], tab("rot_pt"), EQK[:, 2 * c + j, :], start=True, stop=True)
                last.then_inc(filled, 1)
            pe.wait_ge(sem("s5_rows_in"), 32)
            pe.wait_ge(sem("s5_dt_rows"), 1)
            ps = take("s5rows", "v")
            pe.transpose(ps[:, 0:48], SROW[0:48, :], IDENT[0:48, 0:48]).then_inc(filled, 1)
            pe.wait_ge(sem("s5_cexp"), 1)
            ps = take("s5c", "v")
            for k in range(2):
                for i in range(4):
                    last = pe.transpose(ps[:, (4 * k + i) * P:(4 * k + i + 1) * P], SCEX[k][:, i, :], IDENT)
            last.then_inc(filled, 1)
            pe.wait_ge(sem("s5_bblk"), 1)
            ps = take("s5b", "v")
            for k in range(2):
                for i in range(4):
                    last = pe.transpose(ps[:, (4 * k + i) * P:(4 * k + i + 1) * P],
                                        SBBL[k][:, 4 * i:4 * i + 4, :].rearrange("p j c -> p (j c)"), IDENT)
            last.then_inc(filled, 1)
            pe.wait_ge(*read_of("s5b"))
            for i in range(4):
                for jj in range(4):
                    ps = take(f"bu{4 * i + jj}", "v")
                    for k in range(2):
                        last = pe.matmul(ps[:, k * L:(k + 1) * L], SBD[k][32 * jj:32 * jj + 32, i, :],
                                         EU[32 * jj:32 * jj + 32, i, :], start=True, stop=True,
                                         tile_position=(32 * jj, 0))
                    last.then_inc(filled, 1)
                pe.wait_ge(sem("s5_states"), i + 1)
                ps = take(f"s5y{i}", "v")
                for jj in range(4):
                    for k, H in enumerate((SHR, SHI)):
                        last = pe.matmul(ps[32 * jj:32 * jj + 32, 0:L], SCD[k][:, i, 32 * jj:32 * jj + 32], H[:, jj, :],
                                         start=k == 0, stop=k == 1, tile_position=(0, 32 * jj))
                last.then_inc(filled, 1)
            pe.wait_ge(sem("s5_gelu"), 4)
            for c in range(2):
                wv = chunk(cols(a["s5_w_glu_2"][0], c * WC, WC, 0, 4), 4)
                ps = take(f"glu{c}", "a")
                for m in range(2):
                    for k in range(4):
                        last = pe.matmul(ps[:, m * L:(m + 1) * L], wv[:, k, m * P:(m + 1) * P], HT[:, 4 + k, 0:L],
                                         start=k == 0, stop=k == 3)
                last.then_inc(filled, 1)
                used_with_unit()
            pe.wait_ge(sem("eroped"), 4)
            attention("E", lambda h, qt: EQK[64 * (h % 2):64 * (h % 2) + 64, h // 2, qt * P:(qt + 1) * P],
                      lambda h, c0: EQK[64 * (h % 2):64 * (h % 2) + 64, 4 + h // 2, c0:c0 + P],
                      lambda h, vt: EV[:, vt, h * DH:(h + 1) * DH], EPB, EPT, EOT, L)
            pe.wait_ge(*read_of("Eo3"))
            pe.wait_ge(sem("s5_out"), 4)
            for c in range(4):
                gemm_t(f"em{c}", a["ev_w_out_2"][0], c * WC, TL, "a")
            if stop <= 3:
                return

            def ffn(l, n):
                pre_norm(n)
                for c in range(KF // 2):
                    gemm_f(f"fg{l}.{c}", a["ffn_w_gate_2"][l], c * WC, WC, False, "a")
                    gemm_f(f"fu{l}.{c}", a["ffn_w_up_2"][l], c * WC, WC, False, "v")
                pe.wait_ge(*read_of(f"fu{l}.{KF // 2 - 1}.lat"))
                for c in range(4):
                    gemm_t(f"fm{l}{c}", a["ffn_w_down_2"][l], c * WC, TL, "a", FH, (8, 8, 6))

            ffn(0, 2)
            if stop <= 4:
                return
            pre_norm(3)
            wo = a["od_w_in_2"][0]
            for c in range(4):
                gemm_f(f"rx{c}", wo, c * WC, WC, False, "v")
            for c in range(4):
                gemm_f(f"rz{c}", wo, D + c * WC, WC, False, "a")
            pe.wait_ge(sem("rg_conv"), 8)
            for nm, wt in (("r", a["rg_w_r_2"][0]), ("i", a["rg_w_i_2"][0])):
                wv = chunk([(0, WC, wt.rearrange("h (k p) j -> p (h k) j", p=P))])
                for h in range(4):
                    ps = take(f"rg{nm}{h}", "a")
                    for m in range(2):
                        for k in range(2):
                            last = pe.matmul(ps[:, m * L:(m + 1) * L], wv[:, 2 * h + k, m * P:(m + 1) * P],
                                             RXC[:, 2 * h + k, :], start=k == 0, stop=k == 1)
                    last.then_inc(filled, 1)
                used_with_unit()
            pe.wait_ge(sem("rg_out"), 8)
            for c in range(4):
                gemm_t(f"om{c}", a["od_w_out_2"][0], c * WC, TL, "a")
            if stop <= 5:
                return
            ffn(1, 4)

        @block.sync
        def _(sp):
            sp.dma_start(TAB[:, :], a["tables"]).then_inc(sem("tables_in"), 16)
            for c0, rows, n in ROWS:
                r = c0 % P
                sp.dma_start(VR[r:r + n, c0 // P, :], rows).then_inc(sem("rows_in"), 16)
            for n, (pieces, kt) in enumerate(chunks):
                if n == 4:
                    sp.dma_start(X[:, 0:TL, :], a["x"][0].rearrange("(t p) n -> p t n", p=P)).then_inc(sem("x_in"), 16)
                    sp.dma_start(X[:, TL:6, :], a["ctx"][0].rearrange("(t p) n -> p t n", p=P)).then_inc(sem("x_in"), 16)
                if n >= WSLOTS:
                    sp.wait_ge(*released[n - WSLOTS])
                for c0, m, src in pieces:
                    sp.dma_start(WR[:, n % WSLOTS, 0:kt, c0:c0 + m], src).then_inc(wload[n % WSLOTS], 16)

        @block.scalar
        def _(act):
            ch_ = Chain(act, "act_chain")
            link = ch_.link

            def pair(label, dst, c, ctx_, func=ACT.Copy):
                n, t0 = (LC, L) if ctx_ else (L, 0)
                act.wait_ge(*fill_of(label))
                act.activation(dst[:, 2 * c:2 * c + 2, t0:t0 + n], bank(label)[:, 0:2 * n].rearrange("p (m t) -> p m t", m=2),
                               func).then_inc(emptied["a"], 1)

            def bcast_row(dst, src):
                return act.dma_start(dst, src.partition_broadcast(P))

            bcast_row(BC[:, 0, :], a["ln_g"][0]).then_inc(sem("bc_in"), 16)
            bcast_row(BC[:, 1, :], a["ln_b"][0]).then_inc(sem("bc_in"), 16)
            bcast_row(SM[:, 0:8], a["sink_ab"][0]).then_inc(sem("sink_in"), 16)
            act.wait_ge(*read_of("vec"))
            for j, c0 in enumerate((V_C, V_CC)):
                last = act.activation(SC[:, :, j], VEC[:, c0:c0 + 8], ACT.Silu)
                link(last) if j == 0 else None
            last.then_inc(sem("silu_c"), 1)
            for j in range(2):
                act.wait_ge(*fill_of(f"gate0.{j}"))
                ps = bank(f"gate0.{j}")
                act.activation(GT[:, j, :], ps[:, :], ACT.Copy).then_inc(emptied["a"], 1)
            for c in range(2):
                for x in (0, 1):
                    pair(f"q{c}" + (".lat", ".ctx")[x], AQ, c, x)
            for x in (0, 1):
                pair("kv" + (".lat", ".ctx")[x], AKV, 0, x)
            for nm, dst in (("ga", AGA), ("gb", AGB)):
                for c in range(2):
                    for x in (0, 1):
                        pair(f"{nm}{c}" + (".lat", ".ctx")[x], dst, c, x, ACT.Silu)
            act.wait_ge(*fill_of("vtok"))
            act.activation(AVT[:, :, :], ring[units["vtok"][0] % 3][:, 0:6 * P].rearrange("p (t c) -> p t c", t=6), ACT.Copy).then_inc(emptied["a"], 1)

            def attention(kind, PB, PT, scale, sink):
                n = NT_ATT[kind] * HEADS
                for what, i in att_events(n):
                    qt, h = divmod(i, HEADS)
                    if what == "scores":
                        nb = len(att_blocks(kind, qt))
                        act.wait_ge(*fill_of(f"{kind}s{i}"))
                        ps = bank(f"{kind}s{i}")
                        act.wait_ge(sem(f"{kind}_max"), i + 1)
                        if i >= 2:
                            act.wait_ge(*fill_of(f"{kind}t{i - 2}"))
                        col = 32 + 16 * (qt % 2) + h
                        if h == 0 and qt >= 2:
                            act.wait_ge(sem(f"{kind}_normed"), qt - 1)
                        ins = act.activation(PB[:, i % 2, 0:nb * P], ps[:, 0:nb * P], ACT.Exp,
                                             bias=SM[:, col:col + 1], scale=scale,
                                             accum_out=SM[:, col + 8:col + 9])
                        ins.then_inc(emptied["a"], 1)
                        if h == HEADS - 1 and sink:
                            act.wait_ge(sem(f"{kind}_sinkarg"), qt + 1)
                            s0 = 64 + 8 * (qt % 2)
                            act.activation(SM[:, s0:s0 + 8], SM[:, s0:s0 + 8], ACT.Exp).then_inc(sem(f"{kind}_sink"), 1)
                    elif what == "turn" and i % 2 == 0:
                        nb = len(att_blocks(kind, qt))
                        act.wait_ge(*fill_of(f"{kind}t{i}"))
                        ps = bank(f"{kind}t{i}")
                        if i >= 2:
                            act.wait_ge(sem(f"{kind}_values"), i - 1)
                        act.activation(PT[:, i % 2, 0:nb * P], ps[:, 0:nb * P], ACT.Copy).then_inc(emptied["a"], 1)

            attention("A", APB, APT, 0.125, True)

            def ln_root(k, tiles):
                act.wait_ge(sem("ln_var"), k)
                act.activation(SM[:, 96:96 + tiles], SM[:, 96:96 + tiles], ACT.Sqrt).then_inc(sem("ln_root"), 1)

            ln_root(1, 6)
            act.wait_ge(sem("x1_ready"), 6)
            bcast_row(BC[:, 0, :], a["ln_g"][1]).then_inc(sem("bc_in"), 16)
            bcast_row(BC[:, 1, :], a["ln_b"][1]).then_inc(sem("bc_in"), 16)
            if stop <= 1:
                return
            bcast_row(GN, a["gnorm_c"][0]).then_inc(sem("gn_in"), 16)
            act.wait_ge(*fill_of("gate1.0"))
            ps = bank("gate1.0")
            act.activation(GT[:, 0, :], ps[:, :], ACT.Copy).then_inc(emptied["a"], 1)
            for hh in range(2):
                if hh:
                    act.wait_ge(*read_of("oo03"))
                for c in range(2):
                    pair(f"cq{hh}{c}.lat", CQ, c, 0, ACT.Silu)
                for c in range(2):
                    for g, nt in ((0, 4), (1, 2)):
                        act.wait_ge(*fill_of(f"ci{hh}{c}.t{g}"))
                        ps = bank(f"ci{hh}{c}.t{g}")
                        act.activation(CI[:, 4 * g:4 * g + nt, c * WC:(c + 1) * WC],
                                            ps[:, 0:nt * WC].rearrange("p (t c) -> p t c", t=nt), ACT.Copy).then_inc(emptied["a"], 1)
                for d in range(2):
                    hd = f"{hh}{d}"
                    r = 2 * hh + d + 1
                    act.wait_ge(sem("hg_abs"), r)
                    link(act.activation(CT_[:, :, :], CT_[:, :, :], ACT.Exp, scale=-1.0))
                    act.activation(CT_[:, :, :], CT_[:, :, :], ACT.Ln, bias=ONES[:, 0:1]).then_inc(sem("hg_ln"), 1)
                    act.wait_ge(sem("hg_karg"), r)
                    act.activation(CK[:, :, :], CK[:, :, :], ACT.Exp).then_inc(sem("hg_k"), 1)
                    act.wait_ge(sem("hg_ksarg"), r)
                    act.activation(CZ[:, :, :], CZ[:, :, :], ACT.Exp).then_inc(sem("hg_ksexp"), 1)
                    act.activation(SM[:, 128:152], SM[:, 128:152], ACT.Exp).then_inc(sem("hg_decay"), 1)
                    act.wait_ge(sem("hg_qiarg"), r)
                    act.activation(CT_[:, :, 0:L], CT_[:, :, 0:L], ACT.Exp).then_inc(sem("hg_qiexp"), 1)
                    for i, ch in enumerate(hg_seq(d)):
                        if i < 5:
                            act.wait_ge(*fill_of(f"kt{hd}{ch}"))
                            ps = bank(f"kt{hd}{ch}")
                            if i:
                                act.wait_ge(*fill_of(f"su{hd}{hg_seq(d)[i - 1]}"))
                            act.activation(CKT[:, :, :], ps[:, 0:HH * P].rearrange("p (h c) -> p h c", h=HH), ACT.Copy).then_inc(emptied["a"], 1)
                    for li in range(7):
                        act.wait_ge(sem("hg_warg"), 7 * (r - 1) + li + 1)
                        W = CW[li % 2]
                        act.activation(W[:, :, :], W[:, :, :], ACT.Exp).then_inc(sem("hg_wexp"), 1)
            for c in range(4):
                act.wait_ge(*fill_of(f"cg{c}_.t0"))
                ps = bank(f"cg{c}_.t0")
                if c == 0:
                    act.wait_ge(*read_of("oo13"))
                act.activation(CG[:, :, c * WC:(c + 1) * WC], ps[:, :].rearrange("p (t c) -> p t c", t=4), ACT.Silu).then_inc(emptied["a"], 1)
            act.wait_ge(sem("c_ms"), 1)
            act.activation(SM[:, 160:192], SM[:, 160:192], ACT.Sqrt).then_inc(sem("c_root"), 1)
            for t in range(4):
                act.wait_ge(*fill_of(f"cy{t}"))
                ps = bank(f"cy{t}")
                act.activation(HT[:, :, t * P:(t + 1) * P], ps[:, :].rearrange("p (k c) -> p k c", k=KD), ACT.Copy).then_inc(emptied["a"], 1)
            ln_root(2, 4)
            if stop <= 2:
                return
            def row_stats(name, at, n):
                src, junk = at
                for t in range(TL):
                    ins = act.activation(junk[:, t, :], src[:, t, :], ACT.Square, accum_out=SM[:, 200 + t:201 + t])
                ins.then_inc(sem(name), 1)

            def root(name, n):
                act.wait_ge(sem(name + "_ms"), n)
                act.activation(SM[:, 200:204], SM[:, 200:204], ACT.Sqrt).then_inc(sem(name + "_root"), 1)

            def pre_norm(n, ready, dst):
                act.wait_ge(sem(ready), 4)
                row_stats("rms_sum", (X, dst), n)
                root("rms", 2 * n - 1)
                act.wait_ge(sem("rms_inv"), 2 * n - 1)
                for t in range(TL):
                    act.activation(dst[:, t, :], X[:, t, :], ACT.Copy, scale=SM[:, 200 + t:201 + t]).then_inc(sem("xn_ready"), 1)

            def post_norm(n, name, dst, junk):
                for c in range(4):
                    act.wait_ge(*fill_of(f"{name}{c}.t0"))
                    ps = bank(f"{name}{c}.t0")
                    ins = act.activation(dst[:, :, c * WC:(c + 1) * WC], ps[:, :].rearrange("p (t c) -> p t c", t=4), ACT.Copy)
                    ins.then_inc(emptied["a"], 1)
                act.wait_ge(*read_of(f"{name}3.t0"))
                row_stats("rms_sum", (dst, junk), n)
                root("rms", 2 * n)

            act.wait_ge(sem("x2_ready"), 4)
            bcast_row(BC[:, 0, :], a["norm_mix_post_2"][0]).then_inc(sem("bc_in"), 16)
            bcast_row(BC[:, 1, :], a["norm_ffn_post_2"][0]).then_inc(sem("bc_in"), 16)
            act.dma_start(EPOS.bitcast(I32), a["positions_2"][0].partition_broadcast(P)).then_inc(sem("pos_in"), 16)
            pre_norm(1, "x2_ready", XN)
            act.wait_ge(*fill_of("n1.3"))
            act.dma_start(SROW[0:16, :], a["s5_a_re_2"][0].rearrange("(j g) p -> j (g p)", g=2)).then_inc(sem("s5_rows_in"), 16)
            act.dma_start(SROW[16:32, :], a["s5_a_im_2"][0].rearrange("(j g) p -> j (g p)", g=2)).then_inc(sem("s5_rows_in"), 16)
            act.dma_start(SM[32:48, 240:242], a["s5_log_dt_2"][0].rearrange("(j g) -> j g", g=2)).then_inc(sem("s5_dt_in"), 16)
            for k, nm in enumerate(("re", "im")):
                act.dma_start(SBRAW[k], a[f"s5_b_{nm}_2"][0].rearrange("(j g) p c -> (g p) j c", g=2)).then_inc(sem("s5_b_in"), 16)
                act.dma_start(SCRAW[k], a[f"s5_c_{nm}_2"][0].rearrange("(i g) c p -> (g c) i p", i=4)).then_inc(sem("s5_c_in"), 16)
            for c in range(4):
                pair(f"eqk{c}.lat", EQK, c, 0)
            for c in range(2):
                act.wait_ge(*fill_of(f"ev{c}.t0"))
                ps = bank(f"ev{c}.t0")
                act.activation(EV[:, :, c * WC:(c + 1) * WC], ps[:, :].rearrange("p (t c) -> p t c", t=4), ACT.Copy).then_inc(emptied["a"], 1)
            for c in range(2):
                pair(f"eu{c}.lat", EU, c, 0)
            act.wait_ge(sem("rope_arg"), 1)
            link(act.activation(COSP, COSP, ACT.Sin))
            act.activation(SINP, SINP, ACT.Sin).then_inc(sem("rope_tab"), 1)
            pr = lambda k: SPR[:, k, :]
            act.wait_ge(*read_of("s5rows"))
            act.activation(pr(2), pr(2), ACT.Exp).then_inc(sem("s5_dt"), 1)
            act.wait_ge(sem("s5_ang"), 1)
            link(act.activation(pr(5), pr(3), ACT.Exp))
            link(act.activation(pr(6), pr(6), ACT.Sin))
            act.activation(pr(7), pr(7), ACT.Sin).then_inc(sem("s5_sc"), 1)
            for i in range(4):
                act.wait_ge(*read_of(f"s5y{i}"))
                act.activation(HT[:, 4 + i, 0:L], HT[:, 4 + i, 0:L], ACT.Gelu_apprx_tanh).then_inc(sem("s5_gelu"), 1)
            for c in range(2):
                act.wait_ge(*fill_of(f"glu{c}"))
                ps = bank(f"glu{c}")
                act.activation(EU[:, 2 * c:2 * c + 2, :], ps[:, :].rearrange("p (m t) -> p m t", m=2), ACT.Sigmoid).then_inc(emptied["a"], 1)
            attention("E", EPB, EPT, 0.125, False)
            post_norm(1, "em", MX, XN)
            if stop <= 3:
                return

            def ffn(l, n, ready):
                pre_norm(n, ready, FX)
                for c in range(KF // 2):
                    act.wait_ge(*fill_of(f"fg{l}.{c}.lat"))
                    ps = bank(f"fg{l}.{c}.lat")
                    if c >= 2:
                        act.wait_ge(*read_of(f"fu{l}.{c - 2}.lat"))
                    act.activation(FSG[:, c % 2], ps[:, :].rearrange("p (m t) -> p m t", m=2), ACT.Silu).then_inc(emptied["a"], 1)
                post_norm(n, f"fm{l}", FX, FH[:, 0:8, :].rearrange("p a b -> p (a b)").rearrange("p (t n) -> p t n", t=4))

            ffn(0, 2, "x3_ready")
            if stop <= 4:
                return
            act.wait_ge(sem("x4_ready"), 4)
            bcast_row(BC[:, 0, :], a["norm_mix_post_2"][1]).then_inc(sem("bc_in"), 16)
            bcast_row(BC[:, 1, :], a["norm_ffn_post_2"][1]).then_inc(sem("bc_in"), 16)
            pre_norm(3, "x4_ready", XN)
            act.wait_ge(sem("lam_abs"), 1)
            link(act.activation(SM[:, 216:224], SM[:, 216:224], ACT.Exp, scale=-1.0))
            act.activation(SM[:, 216:224], SM[:, 216:224], ACT.Ln, bias=ONES[:, 0:1]).then_inc(sem("lam_ln"), 1)
            for c in range(4):
                pair(f"rz{c}.lat", RZG, c, 0, ACT.Gelu_apprx_tanh)
            for nm, dst, v0 in (("r", RA, V_BR), ("i", RGI, V_BI)):
                for h in range(4):
                    act.wait_ge(*fill_of(f"rg{nm}{h}"))
                    ps = bank(f"rg{nm}{h}")
                    for m in range(2):
                        t = 2 * h + m
                        last = act.activation(dst[:, t, :], ps[:, m * L:(m + 1) * L], ACT.Sigmoid, bias=VEC[:, v0 + t:v0 + t + 1])
                    last.then_inc(emptied["a"], 1)
            act.wait_ge(*read_of("rgi3"))
            act.wait_ge(sem("rg_sp"), 1)
            for t in range(8):
                link(act.activation(RTH[:, t, :], RA[:, t, :], ACT.Tanh, scale=SM[:, 224 + t:225 + t]))
                act.activation(RA[:, t, :], RA[:, t, :], ACT.Exp, scale=SM[:, 232 + t:233 + t]).then_inc(sem("rg_a"), 1)
            for t in range(8):
                act.wait_ge(sem("rg_msq"), t + 1)
                act.activation(RM[:, t, :], RM[:, t, :], ACT.Sqrt).then_inc(sem("rg_mult"), 1)
            post_norm(3, "om", MX, XN)
            if stop <= 5:
                return
            ffn(1, 4, "x5_ready")

        @block.vector
        def _(dve):
            ch_ = Chain(dve, "dve_chain")
            link = ch_.link

            def mod_layer(l):
                for g in range(3):
                    dve.wait_ge(*fill_of(f"mod{l}.{g}"))
                    ps = bank(f"mod{l}.{g}")
                    b = VEC[:, V_BADA + 24 * l + 8 * g:V_BADA + 24 * l + 8 * g + 8]
                    ins = dve.tensor_tensor(MOD[:, l, 8 * g:8 * g + 8, :], ps[:, 0:16].rearrange("p (m j) -> p m j", j=2),
                                            b.unsqueeze(2).to_broadcast([P, 8, 2]), ALU.add)
                    ins.then_inc(emptied["v"], 1)
                    if g == 1:
                        dve.wait_ge(*read_of(f"mod{l}.{g}"))
                        link(dve.tensor_scalar(MOD[:, l, 8:16, :], MOD[:, l, 8:16, :], 1.0, None, ALU.add))
                dve.wait_ge(*read_of(f"mod{l}.2"))

            def gate_diag(l, n):
                for j in range(n):
                    if j:
                        dve.wait_ge(*fill_of(f"gate{l}.{j - 1}"))
                    dve.tensor_tensor(DG[:, :, :], IDENT.unsqueeze(1).to_broadcast([P, KD, P]),
                                      MOD[:, l, 16:24, j].unsqueeze(2).to_broadcast([P, KD, P]),
                                      ALU.mult).then_inc(sem(f"gate_diag{l}"), 1)

            def modulated(l, name, tiles):
                for t in tiles:
                    dve.wait_ge(*fill_of(f"{name}{t}"))
                    ps = bank(f"{name}{t}")
                    j = 0 if t < TL else 1
                    dst = HT[:, :, t * P:(t + 1) * P]
                    link(dve.tensor_tensor(dst, ps[:, :].rearrange("p (k c) -> p k c", k=KD),
                                           MOD[:, l, 8:16, j].unsqueeze(2).to_broadcast([P, KD, P]), ALU.mult))
                    dve.tensor_tensor(dst, dst, MOD[:, l, 0:8, j].unsqueeze(2).to_broadcast([P, KD, P]), ALU.add).then_inc(emptied["v"], 1)

            def join_gated(name, tiles, tmp):
                for c in range(4):
                    for g, t0, nt in ((0, 0, 4), (1, 4, 2)):
                        if t0 >= tiles:
                            continue
                        dve.wait_ge(*fill_of(f"{name}.{c}.t{g}"))
                        ps = bank(f"{name}.{c}.t{g}")
                        gate = GT[:, g, c * WC:(c + 1) * WC].unsqueeze(1).to_broadcast([P, nt, WC])
                        xs = X[:, t0:t0 + nt, c * WC:(c + 1) * WC]
                        ins = dve.tensor_tensor(tmp[:, 0:nt, :], ps[:, 0:nt * WC].rearrange("p (t c) -> p t c", t=nt), gate, ALU.mult)
                        ins.then_inc(emptied["v"], 1)
                        dve.wait_ge(*read_of(f"{name}.{c}.t{g}"))
                        link(dve.scalar_tensor_tensor(out=xs, in0=xs, scalar=ALPHA, in1=tmp[:, 0:nt, :], op0=ALU.mult, op1=ALU.add))

            def layer_norm(k, tiles, bc_count):
                for t in range(tiles):
                    for h in range(2):
                        last = dve.bn_stats(SM[:, 256 + 12 * t + 6 * h:256 + 12 * t + 6 * h + 6], X[:, t, h * 512:(h + 1) * 512])
                    link(last)
                    link(dve.bn_aggr(SM[:, 104 + 2 * t:106 + 2 * t], SM[:, 256 + 12 * t:268 + 12 * t]))
                mv = SM[:, 104:104 + 2 * tiles].rearrange("p (t m) -> p t m", m=2)
                dve.tensor_scalar(SM[:, 96:96 + tiles], mv[:, :, 1], LN_EPS, None, ALU.add).then_inc(sem("ln_var"), 1)
                dve.wait_ge(sem("ln_root"), k)
                link(dve.reciprocal(SM[:, 96:96 + tiles], SM[:, 96:96 + tiles]))
                dve.wait_ge(sem("bc_in"), bc_count)
                for t in range(tiles):
                    link(dve.tensor_scalar(X[:, t, :], X[:, t, :], SM[:, 104 + 2 * t:105 + 2 * t], SM[:, 96 + t:97 + t],
                                           ALU.subtract, ALU.mult))
                    link(dve.tensor_tensor(X[:, t, :], X[:, t, :], BC[:, 0, :], ALU.mult))
                    dve.tensor_tensor(X[:, t, :], X[:, t, :], BC[:, 1, :], ALU.add).then_inc(sem(f"x{k}_ready"), 1)

            dve.wait_ge(*fill_of("vec"))
            ps = bank("vec")
            link(dve.tensor_copy(VEC[:, 0:108], ps[:, 0:108]))
            ins = dve.tensor_copy(VEC[:, 128:196], ps[:, 512:580])
            ins.then_inc(emptied["v"], 1)
            dve.wait_ge(*read_of("vec"))
            dve.wait_ge(sem("sink_in"), 16)
            link(dve.tensor_scalar(SM[:, 8:16], SM[:, 0:8], -1.0, None, ALU.mult))
            mod_layer(0)
            gate_diag(0, 2)
            modulated(0, "h0.", range(6))
            zero = tab("chunk", 0, 1)
            for i in range(4):
                for e in (0, L + 1, L + 2, LT + 3):
                    dve.memset(AU[:, i, e:e + 1], 0.0)
            lat_u = lambda c: AU[:, 2 * c:2 * c + 2, 1:1 + L]
            ctx_u = lambda c: AU[:, 2 * c:2 * c + 2, L + 3:L + 3 + LC]

            def two(ps, n):
                return ps[:, 0:2 * n].rearrange("p (m t) -> p m t", m=2)

            dve.wait_ge(*read_of("gb1.ctx"))
            for c in range(2):
                dve.wait_ge(*fill_of(f"bg{c}.lat"))
                dve.tensor_tensor(AGB[:, 2 * c:2 * c + 2, 0:L], AGB[:, 2 * c:2 * c + 2, 0:L], two(bank(f"bg{c}.lat"), L), ALU.mult).then_inc(emptied["v"], 1)
                dve.wait_ge(*fill_of(f"bg{c}.ctx"))
                dve.tensor_tensor(AGB[:, 2 * c:2 * c + 2, L:LT], AGB[:, 2 * c:2 * c + 2, L:LT], two(bank(f"bg{c}.ctx"), LC), ALU.mult).then_inc(emptied["v"], 1)
            for c in range(2):
                dve.wait_ge(*fill_of(f"xb{c}.lat"))
                dve.tensor_copy(lat_u(c), two(bank(f"xb{c}.lat"), L)).then_inc(emptied["v"], 1)
                dve.wait_ge(*fill_of(f"xb{c}.ctx"))
                dve.tensor_copy(ctx_u(c), two(bank(f"xb{c}.ctx"), LC)).then_inc(emptied["v"], 1)
            dve.wait_ge(*read_of("xb1.ctx"))
            for c in range(2):
                dve.wait_ge(*fill_of(f"cg{c}.lat"))
                dve.tensor_tensor(lat_u(c), lat_u(c), two(bank(f"cg{c}.lat"), L), ALU.mult).then_inc(emptied["v"], 1)
                dve.wait_ge(*fill_of(f"cg{c}.ctx"))
                dve.tensor_tensor(ctx_u(c), ctx_u(c), two(bank(f"cg{c}.ctx"), LC), ALU.mult).then_inc(emptied["v"], 1)
            cosb = lambda n: tab("cos_ax").unsqueeze(1).to_broadcast([P, n, L])
            sinb = lambda n: tab("sin_ax").unsqueeze(1).to_broadcast([P, n, L])

            def rope(label, x, n, cb, sb_, tmp, name, count):
                dve.wait_ge(*fill_of(label))
                ps = bank(label)
                ins = dve.tensor_tensor(tmp[:, 0:n, :], ps[:, 0:n * L].rearrange("p (m t) -> p m t", m=n), sb_(n), ALU.mult)
                ins.then_inc(emptied["v"], 1)
                dve.wait_ge(*read_of(label))
                link(dve.tensor_tensor(x, x, cb(n), ALU.mult))
                dve.tensor_tensor(x, x, tmp[:, 0:n, :], ALU.add).then_inc(sem(name), 1)
                dve.wait_ge(sem(name), count)

            rope("rope0", AQ[:, 0:2, 0:L], 2, cosb, sinb, ROT, "roped", 1)
            rope("rope1", AQ[:, 2:4, 0:L], 2, cosb, sinb, ROT, "roped", 2)
            rope("rope2", AKV[:, 0:1, 0:L], 1, cosb, sinb, ROT, "roped", 3)

            def conv_tile(i):
                for s0, n, d0 in ((0, L, 0), (L + 2, LC, L)):
                    acc = ACV[:, i % 2, d0:d0 + n]
                    wcol = lambda j: VEC[:, V_CONV + 4 * j + i:V_CONV + 4 * j + i + 1]
                    link(dve.tensor_scalar(acc, AU[:, i, s0:s0 + n], wcol(0), None, ALU.mult))
                    for j in (1, 2):
                        link(dve.scalar_tensor_tensor(out=acc, in0=AU[:, i, s0 + j:s0 + j + n], scalar=wcol(j), in1=acc,
                                                      op0=ALU.mult, op1=ALU.add))
                    dve.tensor_tensor(HT[:, 4 + i, d0:d0 + n], acc, AGB[:, i, d0:d0 + n], ALU.mult).then_inc(sem("conv"), 1)

            def attention(kind, PT, OT, scale, sink, finish, between):
                n = NT_ATT[kind] * HEADS
                for what, i in att_events(n):
                    qt, h = divmod(i, HEADS)
                    if what == "scores":
                        nb = len(att_blocks(kind, qt))
                        nu, e, k = units[f"{kind}s{i}"]
                        dve.wait_ge(filled, nu + 1)
                        col = 32 + 16 * (qt % 2) + h
                        if h == 0 and qt >= 2:
                            dve.wait_ge(*read_of(f"{kind}s{(qt - 1) * HEADS - 1}"))
                            if sink:
                                dve.wait_ge(sem(f"{kind}_sink"), qt - 1)
                        link(dve.tensor_reduce(SM[:, 80:81], ring[nu % 3][:, 0:nb * P], AX.X, ALU.max))
                        ins = dve.tensor_scalar(SM[:, col:col + 1], SM[:, 80:81], -scale,
                                                SM[:, 8 + h:9 + h] if sink else None,
                                                ALU.mult, *([ALU.min] if sink else []))
                        ins.then_inc(sem(f"{kind}_max"), 1)
                        dve.wait_ge(sem(f"{kind}_max"), i + 1)
                        if h == HEADS - 1 and sink:
                            s0, b0 = 64 + 8 * (qt % 2), 32 + 16 * (qt % 2)
                            dve.tensor_tensor(SM[:, s0:s0 + 8], SM[:, 0:8], SM[:, b0:b0 + 8], ALU.add).then_inc(sem(f"{kind}_sinkarg"), 1)
                    elif what == "turn" and i % 2:
                        nb = len(att_blocks(kind, qt))
                        dve.wait_ge(*fill_of(f"{kind}t{i}"))
                        ps = bank(f"{kind}t{i}")
                        if i >= 2:
                            dve.wait_ge(sem(f"{kind}_values"), i - 1)
                        dve.tensor_copy(PT[:, i % 2, 0:nb * P], ps[:, 0:nb * P]).then_inc(emptied["v"], 1)
                    elif what == "finish":
                        qt = i
                        last_s = units[f"{kind}s{qt * HEADS + HEADS - 1}"]
                        dve.wait_ge(emptied["a"], last_s[2])
                        den = SM[:, 32 + 16 * (qt % 2) + 8:32 + 16 * (qt % 2) + 16]
                        if sink:
                            dve.wait_ge(sem(f"{kind}_sink"), qt + 1)
                            s0 = 64 + 8 * (qt % 2)
                            link(dve.tensor_tensor(SM[:, 82:90], den, SM[:, s0:s0 + 8], ALU.add))
                            link(dve.reciprocal(SM[:, 82:90], SM[:, 82:90]))
                        else:
                            link(dve.reciprocal(SM[:, 82:90], den))
                        dve.wait_ge(sem(f"{kind}_values"), (qt + 1) * HEADS)
                        if qt >= 2:
                            dve.wait_ge(*fill_of(f"{kind}o{qt - 2}"))
                        dve.tensor_tensor(OT[:, qt % 2, :].rearrange("p (h c) -> p h c", h=HEADS),
                                          obank[qt % 2][:, :].rearrange("p (h c) -> p h c", h=HEADS),
                                          SM[:, 82:90].unsqueeze(2).to_broadcast([P, HEADS, DH]),
                                          ALU.mult).then_inc(sem(f"{kind}_normed"), 1)
                        dve.wait_ge(sem(f"{kind}_normed"), qt + 1)
                        between(qt)
                        dve.wait_ge(*fill_of(f"{kind}o{qt}"))
                        ps = bank(f"{kind}o{qt}")
                        finish(qt, ps[:, 0:512].rearrange("p (f c) -> p f c", f=4))

            def finish_a(qt, o):
                dve.tensor_tensor(HT[:, 0:4, qt * P:(qt + 1) * P], o, AGA[:, :, qt * P:(qt + 1) * P], ALU.mult).then_inc(emptied["v"], 1)

            attention("A", APT, AOT, 0.125, True, finish_a, lambda qt: conv_tile(qt) if qt < 4 else None)
            join_gated("y0", 6, ATMP)
            layer_norm(1, 6, 32)
            if stop <= 1:
                return

            mod_layer(1)
            gate_diag(1, 1)
            modulated(1, "h1.", range(6))
            QS = 128.0 ** -0.5
            for hh in range(2):
                for d in range(2):
                    hd = f"{hh}{d}"
                    r = 2 * hh + d + 1
                    if r > 1:
                        dve.wait_ge(*fill_of(f"lv{(r - 2) // 2}{(r - 2) % 2}6"))
                    for c in range(2):
                        for x in (0, 1):
                            dve.wait_ge(*fill_of(f"cz{hd}{c}" + (".lat", ".ctx")[x]))
                            ps = bank(f"cz{hd}{c}" + (".lat", ".ctx")[x])
                            n, t0 = (L, 0) if x == 0 else (LC, L)
                            dve.tensor_copy(CZ[:, 2 * c:2 * c + 2, t0:t0 + n], two(ps, n)).then_inc(emptied["v"], 1)
                    dve.wait_ge(*read_of(f"cz{hd}1.ctx"))
                    dve.scalar_tensor_tensor(out=CT_[:, :, :], in0=CZ[:, :, :], scalar=-1.0, in1=CZ[:, :, :],
                                             op0=ALU.mult, op1=ALU.max).then_inc(sem("hg_abs"), 1)
                    dve.wait_ge(sem("hg_ln"), r)
                    link(dve.scalar_tensor_tensor(out=CT_[:, :, :], in0=CZ[:, :, :], scalar=0.0, in1=CT_[:, :, :],
                                                  op0=ALU.min, op1=ALU.subtract))
                    dve.tensor_tensor(CK[:, :, :], CT_[:, :, :], CZ[:, :, :], ALU.subtract).then_inc(sem("hg_karg"), 1)
                    for h in range(HH):
                        dve.tensor_tensor_scan(CP[:, h, 0:L], tab("chunk"), CT_[:, h, 0:L], 0.0, ALU.mult, ALU.add)
                        last = dve.tensor_tensor_scan(CP[:, h, L:LT], tab("chunk", 0, LC), CT_[:, h, L:LT], 0.0, ALU.mult, ALU.add)
                        link(last)
                    plast = CP[:, :, :].rearrange("p h (c t) -> p h c t", t=P)[:, :, :, P - 1]
                    DEC = SM[:, 128:152].rearrange("p (h c) -> p h c", h=HH)
                    PL = SM[:, 352:376].rearrange("p (h c) -> p h c", h=HH)
                    link(dve.tensor_copy(PL, plast))
                    link(dve.tensor_copy(DEC, PL))
                    if d == 1:
                        link(dve.tensor_tensor(CP[:, :, :], CP[:, :, :], CT_[:, :, :], ALU.subtract))
                    ch4 = lambda ap, n: ap.rearrange("p h (c t) -> p h c t", t=P)
                    z4, p4 = ch4(CZ[:, :, :], 6), ch4(CP[:, :, :], 6)
                    plb = PL.unsqueeze(3).to_broadcast([P, HH, 6, P])
                    if d == 0:
                        for h in range(HH):
                            last = dve.tensor_tensor(z4[:, h], plb[:, h], p4[:, h], ALU.subtract)
                    else:
                        last = dve.tensor_copy(CZ[:, :, :], CP[:, :, :])
                    last.then_inc(sem("hg_ksarg"), 1)
                    t4 = ch4(CT_[:, :, 0:L], 4)
                    if d == 0:
                        last = dve.tensor_copy(CT_[:, :, 0:L], CP[:, :, 0:L])
                    else:
                        for h in range(HH):
                            last = dve.tensor_tensor(t4[:, h], plb[:, h, 0:4], ch4(CP[:, :, 0:L], 4)[:, h], ALU.subtract)
                    last.then_inc(sem("hg_qiarg"), 1)
                    dve.wait_ge(sem("hg_ksexp"), r)
                    dve.wait_ge(sem("hg_k"), r)
                    dve.tensor_tensor(CZ[:, :, :], CZ[:, :, :], CK[:, :, :], ALU.mult).then_inc(sem("hg_ks"), 1)
                    dve.wait_ge(sem("hg_qiexp"), r)
                    dve.wait_ge(*read_of(f"cq{hh}1.lat"))
                    dve.tensor_tensor(CT_[:, :, 0:L], CT_[:, :, 0:L], CQ[:, :, :], ALU.mult).then_inc(sem("hg_qi"), 1)
                    for g in range(2):
                        dve.wait_ge(*fill_of(f"dg{hd}{g}"))
                        ps = bank(f"dg{hd}{g}")
                        sc = CSC[:, 8 * g:8 * g + 8, :]
                        src = ps[:, :].rearrange("p (j c) -> p j c", j=8)
                        idb = IDENT.unsqueeze(1).to_broadcast([P, 8, P])
                        if d == 0:
                            dve.tensor_tensor(sc, src, idb, ALU.mult).then_inc(emptied["v"], 1)
                            dve.wait_ge(*read_of(f"dg{hd}{g}"))
                        else:
                            dve.tensor_tensor(CDG[:, :, :], src, idb, ALU.mult).then_inc(emptied["v"], 1)
                            dve.wait_ge(*read_of(f"dg{hd}{g}"))
                            link(dve.tensor_tensor(sc, sc, CDG[:, :, :], ALU.add))
                    dve.wait_ge(sem("hg_decay"), r)
                    for i, ch in enumerate(hg_seq(d)):
                        if ch < TL:
                            dve.wait_ge(*fill_of(f"oi{hd}{ch}"))
                            ps = bank(f"oi{hd}{ch}")
                            o = CO[ch][:, hh * 512:(hh + 1) * 512]
                            if d == 0:
                                dve.tensor_scalar(o, ps[:, 0:512], QS, None, ALU.mult).then_inc(emptied["v"], 1)
                            else:
                                dve.scalar_tensor_tensor(out=o, in0=ps[:, 0:512], scalar=QS, in1=o, op0=ALU.mult, op1=ALU.add).then_inc(emptied["v"], 1)
                            dve.wait_ge(*read_of(f"oi{hd}{ch}"))
                        if i < 5:
                            dve.wait_ge(*fill_of(f"su{hd}{ch}"))
                            ps = bank(f"su{hd}{ch}")
                            if i == 0:
                                ins = dve.tensor_copy(CS[:, :, :], ps[:, 0:512].rearrange("p (h c) -> p h c", h=HH))
                            else:
                                for h in range(HH):
                                    ins = dve.scalar_tensor_tensor(out=CS[:, h, :], in0=CS[:, h, :], scalar=DEC[:, h, ch:ch + 1],
                                                                   in1=ps[:, h * P:(h + 1) * P], op0=ALU.mult, op1=ALU.add)
                            ins.then_inc(emptied["v"], 1)
                            dve.wait_ge(*read_of(f"su{hd}{ch}"))
                    def level_arg(li):
                        h2 = LEVELS[li]
                        W = CW[li % 2]
                        n = L // (2 * h2)
                        if li >= 2:
                            dve.wait_ge(*fill_of(f"lv{hd}{li - 2}"))
                        elif li == 0:
                            dve.wait_ge(*fill_of(f"kt{hd}{hg_seq(d)[4]}"))
                        else:
                            dve.wait_ge(*fill_of(f"oi{hd}{hg_seq(d)[5]}"))
                        for h in range(HH):
                            p_ = CP[:, h, 0:L].rearrange("p (b s h) -> p b s h", s=2, h=h2)
                            w_ = W[:, h, :].rearrange("p (b s h) -> p b s h", s=2, h=h2)
                            ref = p_[:, :, 0, h2 - 1:h2] if d == 0 else p_[:, :, 1, 0:1]
                            ref = ref.to_broadcast([P, n, h2])
                            if d == 0:
                                dve.tensor_tensor(w_[:, :, 0, :], ref, p_[:, :, 0, :], ALU.subtract)
                                last = dve.tensor_tensor(w_[:, :, 1, :], p_[:, :, 1, :], ref, ALU.subtract)
                            else:
                                dve.tensor_tensor(w_[:, :, 0, :], ref, p_[:, :, 0, :], ALU.subtract)
                                last = dve.tensor_tensor(w_[:, :, 1, :], p_[:, :, 1, :], ref, ALU.subtract)
                        last.then_inc(sem("hg_warg"), 1)

                    def level_mul(li):
                        h2 = LEVELS[li]
                        W = CW[li % 2]
                        dve.wait_ge(sem("hg_wexp"), 7 * (r - 1) + li + 1)
                        for side in range(2):
                            for h in range(HH):
                                f = (CK if side == d else CQ)[:, h, 0:L]
                                w_ = W[:, h, :].rearrange("p (b s h) -> p b s h", s=2, h=h2)[:, :, side, :]
                                last = dve.tensor_tensor(w_, w_, f.rearrange("p (b s h) -> p b s h", s=2, h=h2)[:, :, side, :], ALU.mult)
                        last.then_inc(sem("hg_w"), 1)

                    def level_mask(li):
                        h2 = LEVELS[li]
                        dve.wait_ge(*fill_of(f"lv{hd}{li}"))
                        ps = bank(f"lv{hd}{li}")
                        m = tab("lv_f" if d == 0 else "lv_b", 64 * li, 64 * li + 64).bitcast(U32)
                        nb = 64 // h2
                        m = m.rearrange("p (b h) -> p b h", h=h2)
                        for j in range(TL * HH):
                            o = CSC[:, j, :].rearrange("p (b s h) -> p b s h", s=2, h=h2)[:, :, 1 - d, :]
                            last = dve.copy_predicated(o, m, ps[:, j * 64:(j + 1) * 64].rearrange("p (b h) -> p b h", h=h2))
                        last.then_inc(emptied["v"], 1)

                    level_arg(0)
                    for li in range(7):
                        if li + 1 < 7:
                            level_arg(li + 1)
                        level_mul(li)
                        level_mask(li)
                    dve.wait_ge(*read_of(f"lv{hd}6"))
                for ch in range(TL):
                    dve.wait_ge(*fill_of(f"oo{hh}{ch}"))
                    ps = bank(f"oo{hh}{ch}")
                    o = CO[ch][:, hh * 512:(hh + 1) * 512]
                    dve.scalar_tensor_tensor(out=o, in0=ps[:, 0:512], scalar=QS, in1=o, op0=ALU.mult, op1=ALU.add).then_inc(emptied["v"], 1)
                    dve.wait_ge(*read_of(f"oo{hh}{ch}"))
            MS = SM[:, 160:192].rearrange("p (t h) -> p t h", t=4)
            o3 = lambda t: CO[t].rearrange("p (h c) -> p h c", h=HEADS)
            for t in range(TL):
                link(dve.tensor_tensor(CSQ[:, 0, :], CO[t], CO[t], ALU.mult))
                link(dve.tensor_reduce(MS[:, t, :], CSQ[:, 0, :].rearrange("p (h c) -> p h c", h=HEADS), AX.X, ALU.add))
            dve.tensor_scalar(SM[:, 160:192], SM[:, 160:192], 1.0 / P, RMS_EPS, ALU.mult, ALU.add).then_inc(sem("c_ms"), 1)
            dve.wait_ge(sem("c_root"), 1)
            link(dve.reciprocal(SM[:, 160:192], SM[:, 160:192]))
            dve.wait_ge(sem("gn_in"), 16)
            dve.wait_ge(*read_of("cg3_.t0"))
            for t in range(TL):
                link(dve.tensor_tensor(o3(t), o3(t), MS[:, t, :].unsqueeze(2).to_broadcast([P, HEADS, P]), ALU.mult))
                link(dve.tensor_tensor(o3(t), o3(t), GN.unsqueeze(1).to_broadcast([P, HEADS, P]), ALU.mult))
                dve.tensor_tensor(CO[t], CO[t], CG[:, t, :], ALU.mult).then_inc(sem("c_y"), 1)
            join_gated("y1", 4, CTMP)
            layer_norm(2, 4, 64)
            if stop <= 2:
                return
            R4 = SM[:, 200:204]

            def inv_rms(k):
                dve.wait_ge(sem("rms_sum"), k)
                dve.tensor_scalar(R4, R4, 1.0 / D, RMS_EPS, ALU.mult, ALU.add).then_inc(sem("rms_ms"), 1)
                dve.wait_ge(sem("rms_root"), k)
                dve.reciprocal(R4, R4).then_inc(sem("rms_inv"), 1)
                dve.wait_ge(sem("rms_inv"), k)

            def pre_norm(n, v0):
                inv_rms(2 * n - 1)
                for t in range(TL):
                    dve.wait_ge(*fill_of(f"n{n}.{t}"))
                    ps = bank(f"n{n}.{t}")
                    dve.tensor_tensor(HT[:, :, t * P:(t + 1) * P], ps[:, :].rearrange("p (k c) -> p k c", k=KD),
                                           VEC[:, v0:v0 + 8].unsqueeze(2).to_broadcast([P, KD, P]), ALU.mult).then_inc(emptied["v"], 1)

            def post_norm(n, src, b, count):
                inv_rms(2 * n)
                dve.wait_ge(sem("bc_in"), count)
                for t in range(TL):
                    link(dve.scalar_tensor_tensor(out=src[:, t, :], in0=src[:, t, :], scalar=SM[:, 200 + t:201 + t],
                                                  in1=BC[:, b, :], op0=ALU.mult, op1=ALU.mult))
                    dve.tensor_tensor(X[:, t, :], X[:, t, :], src[:, t, :], ALU.add).then_inc(sem(f"x{n + 2}_ready"), 1)

            C1, C2 = 6.28125, 0.0019340515136718750
            C3 = TWO_PI - C1 - C2
            PI_ = 3.1415925

            def sine_args(ang, s_, c_, tmp, ready):
                link(dve.tensor_scalar(tmp, ang, 1.0 / TWO_PI, MAGIC, ALU.mult, ALU.add))
                link(dve.tensor_scalar(tmp, tmp, -MAGIC, None, ALU.add))
                link(dve.scalar_tensor_tensor(out=s_, in0=tmp, scalar=-C1, in1=ang, op0=ALU.mult, op1=ALU.add))
                link(dve.scalar_tensor_tensor(out=s_, in0=tmp, scalar=-C2, in1=s_, op0=ALU.mult, op1=ALU.add))
                link(dve.scalar_tensor_tensor(out=s_, in0=tmp, scalar=-C3, in1=s_, op0=ALU.mult, op1=ALU.add))
                link(dve.tensor_scalar(c_, s_, np.pi / 2, None, ALU.add))
                link(dve.tensor_scalar(tmp, c_, np.pi, TWO_PI, ALU.is_gt, ALU.mult))
                link(dve.tensor_tensor(c_, c_, tmp, ALU.subtract))
                link(dve.tensor_scalar(c_, c_, PI_, -PI_, ALU.min, ALU.max))
                dve.tensor_scalar(s_, s_, PI_, -PI_, ALU.min, ALU.max).then_inc(sem(ready), 1)

            colt = lambda k: tab("cols", k, k + 1)
            pre_norm(1, V_NPRE)
            dve.wait_ge(sem("pos_in"), 16)
            link(dve.tensor_copy(SP1, EPOS.bitcast(I32)))
            link(dve.tensor_scalar(SP1, SP1, colt(0), None, ALU.mult))
            sine_args(SP1, SINP, COSP, SP2, "rope_arg")
            dve.wait_ge(sem("s5_dt_in"), 16)
            dve.tensor_copy(SROW[32:48, :].rearrange("j (g p) -> j g p", g=2),
                            SM[32:48, 240:242].unsqueeze(2).to_broadcast([16, 2, DH])).then_inc(sem("s5_dt_rows"), 1)
            dve.wait_ge(sem("s5_c_in"), 32)
            for k, sg in ((0, 1.0), (1, -1.0)):
                for gg in range(2):
                    ins = dve.tensor_scalar(SCEX[k][:, :, gg * DH:(gg + 1) * DH], SCRAW[k], colt(2 + gg), sg, ALU.mult, ALU.mult)
                    if (k, gg) != (1, 1):
                        link(ins)
            ins.then_inc(sem("s5_cexp"), 1)
            dve.wait_ge(sem("rope_tab"), 1)
            cosb = lambda n: COSP.unsqueeze(1).to_broadcast([P, n, L])
            sinb = lambda n: SINP.unsqueeze(1).to_broadcast([P, n, L])
            for c in range(4):
                rope(f"erope{c}", EQK[:, 2 * c:2 * c + 2, :], 2, cosb, sinb, EROT, "eroped", c + 1)
            pr = lambda k: SPR[:, k, :]
            dve.wait_ge(*fill_of("s5rows"))
            ps = bank("s5rows")
            dve.tensor_copy(SPR[:, 0:3, :], ps[:, 0:48].rearrange("p (k j) -> p k j", k=3)).then_inc(emptied["v"], 1)
            dve.wait_ge(*read_of("s5rows"))
            dve.wait_ge(*fill_of("s5c"))
            ps = bank("s5c")
            for k in range(2):
                ins = dve.tensor_copy(SCD[k], ps[:, 512 * k:512 * k + 512].rearrange("p (i c) -> p i c", i=4))
                link(ins) if k == 0 else ins.then_inc(emptied["v"], 1)
            dve.wait_ge(sem("s5_dt"), 1)
            mul = lambda o, x, y: link(dve.tensor_tensor(o, x, y, ALU.mult))
            add = lambda o, x, y: link(dve.tensor_tensor(o, x, y, ALU.add))
            sub = lambda o, x, y: link(dve.tensor_tensor(o, x, y, ALU.subtract))
            mul(pr(3), pr(0), pr(2))
            mul(pr(4), pr(1), pr(2))
            sine_args(pr(4), pr(6), pr(7), pr(8), "s5_ang")
            dve.wait_ge(sem("s5_ang"), 1)
            mul(pr(8), pr(0), pr(0))
            mul(pr(9), pr(1), pr(1))
            add(pr(8), pr(8), pr(9))
            link(dve.reciprocal(pr(8), pr(8)))
            dve.wait_ge(sem("s5_sc"), 1)
            mul(pr(9), pr(5), pr(7))
            link(dve.tensor_scalar(pr(9), pr(9), -1.0, None, ALU.add))
            mul(pr(10), pr(5), pr(6))
            mul(pr(11), pr(9), pr(0))
            mul(pr(12), pr(10), pr(1))
            add(pr(11), pr(11), pr(12))
            mul(pr(11), pr(11), pr(8))
            mul(pr(12), pr(10), pr(0))
            mul(pr(13), pr(9), pr(1))
            sub(pr(12), pr(12), pr(13))
            mul(pr(12), pr(12), pr(8))
            dve.wait_ge(sem("s5_b_in"), 32)
            wr, wi = (pr(k).unsqueeze(2).to_broadcast([P, 16, 16]) for k in (11, 12))
            q1 = SP1[:, 0:256].rearrange("p (j c) -> p j c", j=16)
            q2 = SP1[:, 256:512].rearrange("p (j c) -> p j c", j=16)
            q3 = SP2[:, 0:256].rearrange("p (j c) -> p j c", j=16)
            mul(q1, SBRAW[0], wr)
            mul(q2, SBRAW[1], wi)
            sub(q1, q1, q2)
            mul(q2, SBRAW[0], wi)
            mul(q3, SBRAW[1], wr)
            add(q2, q2, q3)
            for k, q in ((0, q1), (1, q2)):
                for gg in range(2):
                    ins = dve.tensor_scalar(SBBL[k][:, :, gg * 16:(gg + 1) * 16], q, colt(4 + gg), None, ALU.mult)
                    if (k, gg) != (1, 1):
                        link(ins)
            ins.then_inc(sem("s5_bblk"), 1)
            EC, ES = lambda k: pr(14 + k), lambda k: pr(23 + k)
            link(dve.tensor_copy(EC(0), pr(7)))
            link(dve.tensor_copy(ES(0), pr(6)))
            for k in range(8):
                mul(pr(9), EC(k), EC(k))
                mul(pr(10), ES(k), ES(k))
                sub(EC(k + 1), pr(9), pr(10))
                mul(pr(9), EC(k), ES(k))
                link(dve.tensor_scalar(ES(k + 1), pr(9), 2.0, None, ALU.mult))
            dve.wait_ge(*fill_of("s5b"))
            ps = bank("s5b")
            for k in range(2):
                ins = dve.tensor_copy(SBD[k], ps[:, 512 * k:512 * k + 512].rearrange("p (i c) -> p i c", i=4))
                link(ins) if k == 0 else ins.then_inc(emptied["v"], 1)
            for i in range(4):
                js = slice(4 * i, 4 * i + 4)
                link(dve.memset(SER[:, :, 0:1], 1.0))
                link(dve.memset(SEI[:, :, 0:1], 0.0))
                for k in range(9):
                    n = 1 << k
                    cb = EC(k)[:, js].unsqueeze(2).to_broadcast([P, 4, n])
                    sb_ = ES(k)[:, js].unsqueeze(2).to_broadcast([P, 4, n])
                    t1, t2 = SBR[:, :, 0:n], SBI[:, :, 0:n]
                    mul(t1, SER[:, :, 0:n], cb)
                    mul(t2, SEI[:, :, 0:n], sb_)
                    sub(SER[:, :, n:2 * n], t1, t2)
                    mul(t1, SER[:, :, 0:n], sb_)
                    mul(t2, SEI[:, :, 0:n], cb)
                    add(SEI[:, :, n:2 * n], t1, t2)
                if i:
                    dve.wait_ge(*fill_of(f"s5y{i - 1}"))
                for jj in range(4):
                    j = 4 * i + jj
                    dve.wait_ge(*fill_of(f"bu{j}"))
                    ps = bank(f"bu{j}")
                    er, ei, br, bi = SER[:, jj, :], SEI[:, jj, :], SBR[:, jj, :], SBI[:, jj, :]
                    ur, ui = ps[:, 0:L], ps[:, L:2 * L]
                    mul(SP1, er, ur)
                    mul(SP2, ei, ui)
                    add(br, SP1, SP2)
                    mul(SP1, er, ui)
                    dve.tensor_tensor(SP2, ei, ur, ALU.mult).then_inc(emptied["v"], 1)
                    dve.wait_ge(*read_of(f"bu{j}"))
                    sub(bi, SP1, SP2)
                    rho = pr(5)[:, j:j + 1].to_broadcast([P, L])
                    link(dve.tensor_tensor_scan(br, rho, br, 0.0, ALU.mult, ALU.add))
                    link(dve.tensor_tensor_scan(bi, rho, bi, 0.0, ALU.mult, ALU.add))
                    mul(SP1, er, br)
                    mul(SP2, ei, bi)
                    sub(SHR[:, jj, :], SP1, SP2)
                    mul(SP1, er, bi)
                    mul(SP2, ei, br)
                    ins = dve.tensor_tensor(SHI[:, jj, :], SP1, SP2, ALU.add)
                    if jj < 3:
                        link(ins)
                ins.then_inc(sem("s5_states"), 1)
                dve.wait_ge(sem("s5_states"), i + 1)
                dve.wait_ge(*fill_of(f"s5y{i}"))
                ps = bank(f"s5y{i}")
                dve.scalar_tensor_tensor(out=HT[:, 4 + i, 0:L], in0=EU[:, i, :], scalar=VEC[:, V_D + i:V_D + i + 1],
                                              in1=ps[:, 0:L], op0=ALU.mult, op1=ALU.add).then_inc(emptied["v"], 1)
            dve.wait_ge(*fill_of("glu1"))
            dve.wait_ge(*read_of("glu1"))
            for m in range(4):
                dve.tensor_tensor(HT[:, 4 + m, 0:L], HT[:, 4 + m, 0:L], EU[:, m, :], ALU.mult).then_inc(sem("s5_out"), 1)

            def finish_e(qt, o):
                dve.tensor_copy(HT[:, 0:4, qt * P:(qt + 1) * P], o).then_inc(emptied["v"], 1)

            attention("E", EPT, EOT, 0.125, False, finish_e, lambda qt: None)
            post_norm(1, MX, 0, 96)
            if stop <= 3:
                return

            def ffn(l, n, count):
                pre_norm(n, V_NFFN + 8 * l)
                for c in range(KF // 2):
                    dve.wait_ge(*fill_of(f"fu{l}.{c}.lat"))
                    ps = bank(f"fu{l}.{c}.lat")
                    dve.wait_ge(*read_of(f"fg{l}.{c}.lat"))
                    dve.tensor_tensor(FH[:, 2 * c:2 * c + 2, :], FSG[:, c % 2], ps[:, :].rearrange("p (m t) -> p m t", m=2), ALU.mult).then_inc(emptied["v"], 1)
                post_norm(n, FX, 1, count)

            ffn(0, 2, 96)
            if stop <= 4:
                return
            lam, sp = VEC[:, V_LAM:V_LAM + 8], SM[:, 216:224]
            dve.scalar_tensor_tensor(out=sp, in0=lam, scalar=-1.0, in1=lam, op0=ALU.mult, op1=ALU.max).then_inc(sem("lam_abs"), 1)
            pre_norm(3, V_NPRE + 8)
            dve.wait_ge(sem("lam_ln"), 1)
            link(dve.tensor_scalar(SM[:, 224:232], lam, -1.0, 0.0, ALU.mult, ALU.max))
            link(dve.tensor_tensor(sp, sp, SM[:, 224:232], ALU.add))
            link(dve.tensor_scalar(SM[:, 224:232], sp, 8.0, None, ALU.mult))
            dve.tensor_scalar(SM[:, 232:240], sp, -8.0, None, ALU.mult).then_inc(sem("rg_sp"), 1)
            link(dve.memset(RXB[:, :, 0:3], 0.0))
            for c in range(4):
                dve.wait_ge(*fill_of(f"rx{c}.lat"))
                dve.tensor_copy(RXB[:, 2 * c:2 * c + 2, 3:3 + L], two(bank(f"rx{c}.lat"), L)).then_inc(emptied["v"], 1)
            dve.wait_ge(*read_of("rx3.lat"))
            for t in range(8):
                wcol = lambda j: VEC[:, V_RCW + 8 * j + t:V_RCW + 8 * j + t + 1]
                link(dve.tensor_scalar(RXC[:, t, :], RXB[:, t, 0:L], wcol(0), VEC[:, V_RCB + t:V_RCB + t + 1], ALU.mult, ALU.add))
                for j in (1, 2, 3):
                    ins = dve.scalar_tensor_tensor(out=RXC[:, t, :], in0=RXB[:, t, j:j + L], scalar=wcol(j), in1=RXC[:, t, :],
                                                   op0=ALU.mult, op1=ALU.add)
                    if j < 3:
                        link(ins)
                ins.then_inc(sem("rg_conv"), 1)
            dve.wait_ge(*read_of("rgi3"))
            dve.wait_ge(sem("rg_conv"), 8)
            for t in range(8):
                dve.wait_ge(sem("rg_a"), t + 1)
                dve.tensor_tensor(RGI[:, t, :], RGI[:, t, :], RXC[:, t, :], ALU.mult)
                link(dve.tensor_tensor(RM[:, t, :], RA[:, t, :], RA[:, t, :], ALU.mult))
                dve.scalar_tensor_tensor(out=RM[:, t, :], in0=RM[:, t, :], scalar=1.0, in1=RTH[:, t, :],
                                         op0=ALU.add, op1=ALU.mult).then_inc(sem("rg_msq"), 1)
            dve.wait_ge(*read_of("rz3.lat"))
            for t in range(8):
                dve.wait_ge(sem("rg_mult"), t + 1)
                link(dve.tensor_tensor(RGI[:, t, :], RGI[:, t, :], RM[:, t, :], ALU.mult))
                link(dve.tensor_tensor_scan(RXC[:, t, :], RA[:, t, :], RGI[:, t, :], 0.0, ALU.mult, ALU.add))
                dve.tensor_tensor(RM[:, t, :], RXC[:, t, :], RZG[:, t, :], ALU.mult).then_inc(sem("rg_out"), 1)
            post_norm(3, MX, 0, 128)
            if stop <= 5:
                return
            ffn(1, 4, 128)

        @block.gpsimd
        def _(pool):
            last = min(stop, 6)
            pool.wait_ge(sem(f"x{last}_ready"), 6 if last == 1 else 4)
            pool.dma_start(out[0].rearrange("(t p) n -> p t n", p=P), X[:, 0:TL, :]).then_inc(sem("out_written"), 16)
            pool.wait_ge(sem("out_written"), 16)
            if last <= 2:
                pool.wait_ge(sem("bc_in"), 64)


SHAPES = None


def kernel(**inputs):
    import numpy as _np
    import concourse.bacc as _bacc
    from concourse import mybir as _mybir
    from concourse.bass_utils import run_bass_kernel_spmd as _run

    nc = _bacc.Bacc("TRN2", target_bir_lowering=False, num_devices=1)
    arrays, aps = {}, {}
    for name, x in list(inputs.items()) + [("tables", make_tables())]:
        x = _np.ascontiguousarray(x)
        arrays[f"in_{name}"] = x
        aps[name] = nc.dram_tensor(f"in_{name}", x.shape, _mybir.dt.from_np(x.dtype), kind="ExternalInput").ap()
    out = nc.dram_tensor("out_0", (1, L, D), F32, kind="ExternalOutput").ap()
    program(nc, aps, out)
    r = _run(nc, [arrays], core_ids=[0])
    return r.results[0]["out_0"]
```

```python
from contextlib import ExitStack

import numpy as np

import concourse.bass as bass
from concourse import mybir

F32 = mybir.dt.float32
U32 = mybir.dt.uint32
I32 = mybir.dt.int32
ALU = mybir.AluOpType
ACT = mybir.ActivationFunctionType
AX = mybir.AxisListType

P = 128
D = 1024
KD = D // P
L = 512
LC = 256
TL = L // P
TC = LC // P
LT = L + LC
HEADS = 8
DH = 64
AW = HEADS * DH
NEG = -1e30
ALPHA = 4.0 ** 0.25
LN_EPS = 1e-5
RMS_EPS = 1e-6
FFN = 2816
KF = FFN // P
WC = 256
WSLOTS = 3
HH = 2
LEVELS = (64, 32, 16, 8, 4, 2, 1)
TWO_PI = 2.0 * np.pi
MAGIC = 12582912.0


def table_layout():
    sizes = [("ident", P), ("ones", P), ("win_lo", P), ("win_hi", P), ("dil", 1280),
             ("lv_f", 64 * len(LEVELS)), ("lv_b", 64 * len(LEVELS)), ("rot_ax", P), ("rot_pt", P),
             ("cos_ax", L), ("sin_ax", L), ("chunk", L), ("cols", 8)]
    at, out = 0, {}
    for name, n in sizes:
        out[name] = (at, at + n)
        at += n
    return out, at


def make_tables():
    lay, width = table_layout()
    t = np.zeros((P, width), np.float32)

    def put(name, a):
        t[:, lay[name][0]:lay[name][1]] = a

    i = np.arange(P)
    put("ident", np.eye(P))
    put("ones", 1.0)
    put("win_lo", np.where(i[None, :] >= i[:, None], 0.0, NEG))
    put("win_hi", np.where(i[None, :] <= i[:, None], 0.0, NEG))
    off = 0
    for qt in range(TL):
        q = qt * P + i[:, None]
        k = np.arange((qt + 1) * P)[None, :]
        d = q - k
        n = ((d >= 0) & (d <= 128)).astype(int) + ((d >= 0) & (d % 4 == 0)) + ((d >= 0) & (d % 16 == 0))
        b = np.where(n > 0, 8.0 * np.log(np.maximum(n, 1)), NEG)
        t[:, lay["dil"][0] + off:lay["dil"][0] + off + (qt + 1) * P] = b
        off += (qt + 1) * P
    for li, h in enumerate(LEVELS):
        right = np.array([c for c in range(P) if (c // h) % 2 == 1])
        left = np.array([c for c in range(P) if (c // h) % 2 == 0])
        f = (i[:, None] // (2 * h) == right[None, :] // (2 * h)) & ((i[:, None] // h) % 2 == 0)
        b = (i[:, None] // (2 * h) == left[None, :] // (2 * h)) & ((i[:, None] // h) % 2 == 1)
        t[:, lay["lv_f"][0] + 64 * li:lay["lv_f"][0] + 64 * li + 64] = f
        t[:, lay["lv_b"][0] + 64 * li:lay["lv_b"][0] + 64 * li + 64] = b

    def rotation(period, half, used):
        r = np.zeros((P, P), np.float32)
        for m in range(P):
            o = m % period
            if o < used:
                if o < half:
                    r[m + half, m] = -1.0
                else:
                    r[m - half, m] = 1.0
        return r

    put("rot_ax", rotation(32, 16, 32))
    put("rot_pt", rotation(64, 8, 16))
    freqs = (np.float32(10000.0) ** (-np.arange(16, dtype=np.float32) / np.float32(16))).astype(np.float32)
    tok = np.arange(L)
    for p in range(P):
        o = p % DH
        pos = (tok // 64 if o < 32 else tok % 64).astype(np.float32)
        ang = pos * freqs[o % 16]
        t[p, lay["cos_ax"][0]:lay["cos_ax"][1]] = np.cos(ang)
        t[p, lay["sin_ax"][0]:lay["sin_ax"][1]] = np.sin(ang)
    put("chunk", (np.arange(L) % P != 0).astype(np.float32)[None, :])
    inv = (np.float32(500000.0) ** -(np.arange(8, dtype=np.float32) * np.float32(2.0) / np.float32(16))).astype(np.float32)
    c0 = lay["cols"][0]
    for p in range(P):
        o = p % DH
        t[p, c0] = inv[o % 8] if o < 16 else 0.0
    t[:, c0 + 2] = (i // 16) % 2 == 0
    t[:, c0 + 3] = (i // 16) % 2 == 1
    t[:, c0 + 4] = i // DH == 0
    t[:, c0 + 5] = i // DH == 1
    return t


def program(nc, a, out, stop=99, dumps=()):
    lay, tw = table_layout()
    ctx = ExitStack()
    with ctx:
        sems = {}

        def sem(name):
            if name not in sems:
                sems[name] = ctx.enter_context(nc.semaphore(name))
            return sems[name]

        arena = ctx.enter_context(nc.sbuf_tensor("arena", [P, 53100], F32))
        top = [0]

        def take_words(n):
            top[0] += n
            assert top[0] <= 53100, top[0]
            return top[0] - n

        def view(at, *dims):
            n = int(np.prod(dims))
            v = arena[:, at:at + n]
            if len(dims) == 2:
                v = v.rearrange("p (a b) -> p a b", a=dims[0])
            if len(dims) == 3:
                v = v.rearrange("p (a b c) -> p a b c", a=dims[0], b=dims[1])
            return v

        TAB = view(take_words(tw), tw)

        def tab(name, lo=0, hi=None):
            s, e = lay[name]
            return TAB[:, s + lo:(e if hi is None else s + hi)]

        IDENT, ONES = tab("ident"), tab("ones")
        VEC = view(take_words(256), 256)
        MOD = view(take_words(96), 2, 24, 2)
        SC = view(take_words(16), KD, 2)
        SM = view(take_words(512), 512)
        BC = view(take_words(2 * D), 2, D)
        gt_at = take_words(2 * D)
        GT = view(gt_at, 2, D)
        x_at = take_words(6 * D)
        X = view(x_at, 6, D)
        ht_at = take_words(KD * LT)
        HT = view(ht_at, KD, LT)
        WR = view(take_words(WSLOTS * KD * WC), WSLOTS, KD, WC)
        hi_at = take_words(2 * KD * WC)
        work = top[0]
        free = 53100 - work

        ring = [ctx.enter_context(nc.psum_tensor(f"ring{i}", [P, 1024], F32)) for i in range(3)]
        obank = [ctx.enter_context(nc.psum_tensor(f"obank{i}", [P, 512], F32)) for i in range(2)]

        filled = sem("psum_filled")
        emptied = {"v": sem("dve_emptied"), "a": sem("act_emptied")}
        units, order, by_engine = {}, [], {"v": 0, "a": 0}
        chunks = []
        wload = [sem(f"weights{i}") for i in range(WSLOTS)]
        wcount = [0] * WSLOTS
        wused = sem("weights_used")
        released = []

        w = work
        AQ = view(w, 4, LT)
        AKV = view(w + 3072, 2, LT)
        AGA = view(w + 4608, 4, LT)
        AGB = view(w + 7680, 4, LT)
        AU = view(w + 10752, 4, LT + 4)
        AVT = view(w + 13840, 6, P)
        APB = view(w + 14608, 2, 640)
        APT = view(w + 15888, 2, 640)
        AOT = view(w + 17168, 2, AW)
        ACV = view(w + 18192, 2, LT)
        ROT = view(w + 14608, 2, L)
        DG = view(w + 14608, KD, P)
        VR = view(w, 2, P)
        ATMP = view(w, 4, WC)

        hg = [[view(w + 6144 * b + 1536 * k, HH, LT) for b in range(2)] for k in range(4)]
        HZ, HT_, HK, HP = hg
        HW = [view(w + 12288 + 1024 * b, HH, L) for b in range(2)]
        HQ = [view(w + 14336 + 1024 * b, HH, L) for b in range(2)]
        HI = [view(w + 16384 + 1536 * b, 6, HH * P) for b in range(2)]
        HSC = view(w + 19456, TL * HH, P)
        xc = x_at + 4 * D
        HS = view(xc, HH, P)
        HKT = [view(xc + 256 + 256 * b, HH, P) for b in range(2)]
        HDG = view(xc + 768, TL * HH, P)
        HO = view(hi_at, TL, D)
        CG = view(w, TL, D)
        CSQ = view(w + 12288, D)
        CTMP = view(w + 13312, TL, WC)
        GN = SM[:, 376:504]
        assert w + 20480 <= 53100, free
        STEPS = [(hb, d) for hb in range(HEADS // HH) for d in range(2)]
        rounds = {}
        EQK = view(w, 8, L)
        EV = view(w + 4096, TL, AW)
        EU = view(w + 6144, 4, L)
        EPB = view(w + 8192, 2, L)
        EPT = view(w + 9216, 2, L)
        EOT = view(w + 10240, 2, AW)
        EROT = view(w + 8192, 2, L)
        EPOS = view(w + 8192, L)
        COSP, SINP = tab("cos_ax"), tab("sin_ax")
        s5 = w + 11264
        buffers = lambda at: [view(at + 1024 * b, 2, L) for b in range(2)]
        SER, SEI = buffers(s5), buffers(s5 + 2048)
        SBR, SBI = buffers(s5 + 4096), buffers(s5 + 6144)
        SHR, SHI = buffers(gt_at), buffers(x_at + 4 * D)
        SBD = [view(hi_at + 512 * i, 4, P) for i in range(2)]
        SCD = [view(hi_at + 1024 + 512 * i, 4, P) for i in range(2)]
        SPR = view(hi_at + 2048, 32, 16)
        SE0 = [view(hi_at + 2560 + 512 * i, 16, 32) for i in range(2)]
        SROW = view(hi_at + 3584, P)
        SP1, SP2 = view(w + 9216, 2, L), view(w + 10240, 2, L)
        SP3 = view(w + 19456, 2, L)
        SBRAW = [view(s5 + 4096 + 256 * i, 16, 16) for i in range(2)]
        SBBL = [view(s5 + 4608 + 512 * i, 16, 32) for i in range(2)]
        SCRAW = [view(s5 + 5632 + 256 * i, 4, DH) for i in range(2)]
        SCEX = [view(s5 + 6144 + 512 * i, 4, P) for i in range(2)]
        S5_STEPS = 8
        assert w + 20480 <= 53100
        XN = view(s5, TL, D)
        MX = view(w, TL, D)
        FH = view(w, KF, L)
        FSG = view(w + 11264, 2, 2, L)
        FX = view(w + 13312, TL, D)
        RXB = view(w, 8, L + 4)
        RZG = view(w + 4128, 8, L)
        RXC = view(w + 8224, 8, L)
        RA = view(w + 12320, 8, L)
        RGI = view(w + 16416, 8, L)
        RTH = view(w, 8, L)
        RM = HT[:, :, 0:L]

        class Chain:

            def __init__(self, eng, name):
                self.eng, self.sem, self.n = eng, sem(name), 0

            def link(self, ins):
                ins.then_inc(self.sem, 1)
                self.n += 1
                self.eng.wait_ge(self.sem, self.n)

        def read_of(label):
            _, e, k = units[label]
            return emptied[e], k

        def fill_of(label):
            return filled, units[label][0] + 1

        def bank(label):
            return ring[units[label][0] % 3]

        block = ctx.enter_context(nc.Block())

        V_C, V_CC, V_BADA, V_CONV, V_NPRE, V_NFFN = 0, 8, 16, 64, 76, 92
        V_D, V_RCW, V_RCB, V_BR, V_BI, V_LAM = 128, 132, 164, 172, 180, 188

        ROWS = [(V_C, a["c"].rearrange("o (r n) -> (o r) n", n=P), 8),
                (V_CC, a["c_ctx"].rearrange("(r n) -> r n", n=P), 8),
                (V_BADA, a["b_ada"].rearrange("l (r n) -> (l r) n", n=P), 48),
                (V_CONV, a["conv_ab"].rearrange("o j (r n) -> (o j r) n", n=P), 12),
                (V_NPRE, a["norm_mix_pre_2"].rearrange("l (r n) -> (l r) n", n=P), 16),
                (V_NFFN, a["norm_ffn_pre_2"].rearrange("l (r n) -> (l r) n", n=P), 16),
                (V_D, a["s5_d_2"].rearrange("o (r g) c -> (o r) (g c)", r=4), 4),
                (V_RCW, a["rg_conv_w_2"].rearrange("o j (r n) -> (o j r) n", n=P), 32),
                (V_RCB, a["rg_conv_b_2"].rearrange("o (r n) -> (o r) n", n=P), 8),
                (V_BR, a["rg_b_r_2"].rearrange("o (r n) -> (o r) n", n=P), 8),
                (V_BI, a["rg_b_i_2"].rearrange("o (r n) -> (o r) n", n=P), 8),
                (V_LAM, a["rg_lam_2"].rearrange("o (r n) -> (o r) n", n=P), 8)]

        def cols(wap, c0, n=WC, k0=0, kt=KD):
            return [(0, n, wap[k0 * P:(k0 + kt) * P, c0:c0 + n].rearrange("(k p) n -> p k n", p=P))]

        def att_blocks(kind, qt):
            if kind == "A":
                b = [(L, TL, None), (L + P, TL + 1, None)]
                if qt < TL:
                    if qt > 0:
                        b.append(((qt - 1) * P, qt - 1, tab("win_lo")))
                    b.append((qt * P, qt, None))
                    if qt < TL - 1:
                        b.append(((qt + 1) * P, qt + 1, tab("win_hi")))
                return b
            off = P * (qt * (qt + 1) // 2)
            return [(k * P, k, tab("dil", off + k * P, off + (k + 1) * P)) for k in range(qt + 1)]

        def att_events(n):
            for i in range(n + 2):
                if i < n:
                    yield "scores", i
                if 0 <= i - 1 < n:
                    yield "turn", i - 1
                if 0 <= i - 2:
                    yield "values", i - 2
                    if (i - 2) % HEADS == HEADS - 1:
                        yield "finish", (i - 2) // HEADS

        NT_ATT = {"A": TL + TC, "E": TL}

        def hg_seq(d):
            c, l = [TL, TL + 1], list(range(TL))
            return c + l if d == 0 else c[::-1] + l[::-1]

        def pos(ap, n, h, side):
            return ap.rearrange("p g (b s h) -> p g b s h", s=2, h=h)[:, :, :, side, :]

        @block.tensor
        def _(pe):
            def take(label, engine):
                n = len(order)
                if n >= 3:
                    e, k = units[order[n - 3]][1:]
                    pe.wait_ge(emptied[e], k)
                by_engine[engine] += 1
                units[label] = (n, engine, by_engine[engine])
                order.append(label)
                return ring[n % 3]

            def chunk(pieces, kt=KD):
                n = len(chunks)
                s = n % WSLOTS
                chunks.append((pieces, kt))
                wcount[s] += 16 * len(pieces)
                pe.wait_ge(wload[s], wcount[s])
                return WR[:, s]

            def used_with_unit():
                released.append((filled, len(order)))

            def used_now(last):
                last.then_inc(wused, 1)
                released.append((wused, 1 + sum(x is wused for x, _ in released)))

            def gemm_f(name, wt, c0, n, ctx_on, eng, lat_on=True, pieces=None, lhs=None, rhs=HT):
                wv = chunk(pieces or cols(wt, c0, n))
                lhs = lhs or (lambda wv, k, m: wv[:, k, m * P:(m + 1) * P])
                mts = n // P
                if lat_on:
                    ps = take(name + ".lat", eng)
                    for m in range(mts):
                        for k in range(KD):
                            last = pe.matmul(ps[:, m * L:(m + 1) * L], lhs(wv, k, m), rhs[:, k, 0:L],
                                             start=k == 0, stop=k == KD - 1)
                    last.then_inc(filled, 1)
                if ctx_on:
                    ps = take(name + ".ctx", eng)
                    for m in range(mts):
                        for k in range(KD):
                            last = pe.matmul(ps[:, m * LC:(m + 1) * LC], lhs(wv, k, m), rhs[:, k, L:LT],
                                             start=k == 0, stop=k == KD - 1)
                    last.then_inc(filled, 1)
                used_with_unit()

            def gemm_t(name, wt, c0, tiles, eng, act=HT, kts=(KD,)):
                groups = [g for g in (range(0, 4), range(4, 6)) if g.start < tiles]
                if len(kts) > 1:
                    ps = take(name + ".t0", eng)
                    k0 = 0
                    for ci, kt in enumerate(kts):
                        wv = chunk(cols(wt, c0, WC, k0, kt), kt)
                        for t in range(4):
                            for k in range(kt):
                                last = pe.matmul(ps[:, t * WC:(t + 1) * WC], act[:, k0 + k, t * P:(t + 1) * P],
                                                 wv[:, k, :], start=ci == 0 and k == 0 and t % 2 == 0,
                                                 stop=ci == len(kts) - 1 and k == kt - 1,
                                                 skip_group_check=True)
                        k0 += kt
                        if ci < len(kts) - 1:
                            used_now(last)
                    last.then_inc(filled, 1)
                    used_with_unit()
                    return
                wv = chunk(cols(wt, c0))
                for gi, g in enumerate(groups):
                    ps = take(f"{name}.t{gi}", eng)
                    for j, t in enumerate(g):
                        for k in range(KD):
                            last = pe.matmul(ps[:, j * WC:(j + 1) * WC], act[:, k, t * P:(t + 1) * P],
                                             wv[:, k, :], start=k == 0, stop=k == KD - 1)
                    last.then_inc(filled, 1)
                used_with_unit()

            def turn_tiles(name, src, tiles, eng, at=None):
                for t in tiles:
                    ps = take(f"{name}{t}", eng)
                    for k in range(KD):
                        x = at(t, k) if at else src[:, t, k * P:(k + 1) * P]
                        last = pe.transpose(ps[:, k * P:(k + 1) * P], x, IDENT)
                    last.then_inc(filled, 1)

            def mod_layer(l):
                for g in range(3):
                    ps = take(f"mod{l}.{g}", "v")
                    for ci in range(4):
                        wv = chunk(cols(a["w_ada"][l], g * D + ci * WC))
                        for m in range(2):
                            o = 4 * ci + 2 * m
                            for k in range(KD):
                                last = pe.matmul(ps[:, o:o + 2], wv[:, k, m * P:(m + 1) * P], SC[:, k, :],
                                                 start=k == 0, stop=k == KD - 1)
                        if ci < 3:
                            used_now(last)
                    last.then_inc(filled, 1)
                    used_with_unit()

            def gate_rows(l, n):
                for j in range(n):
                    pe.wait_ge(sem(f"gate_diag{l}"), j + 1)
                    ps = take(f"gate{l}.{j}", "a")
                    for h in range(2):
                        last = pe.matmul(ps[:, h * 512:(h + 1) * 512], ONES, DG[:, 4 * h:4 * h + 4, :],
                                         start=True, stop=True)
                    last.then_inc(filled, 1)

            def attention(kind, q_of, k_of, v_of, PB, PT, OT, width):
                n = NT_ATT[kind] * HEADS
                for what, i in att_events(n):
                    qt, h = divmod(i, HEADS)
                    if what == "scores":
                        blocks = att_blocks(kind, qt)
                        ps = take(f"{kind}s{i}", "a")
                        for b, (c0, _, mask) in enumerate(blocks):
                            o = ps[:, b * P:(b + 1) * P]
                            last = pe.matmul(o, q_of(h, qt), k_of(h, c0), start=True, stop=mask is None)
                            if mask is not None:
                                last = pe.matmul(o, IDENT, mask, start=False, stop=True)
                        last.then_inc(filled, 1)
                    elif what == "turn":
                        pe.wait_ge(*read_of(f"{kind}s{i}"))
                        ps = take(f"{kind}t{i}", "v" if i % 2 else "a")
                        for b in range(len(att_blocks(kind, qt))):
                            last = pe.transpose(ps[:, b * P:(b + 1) * P], PB[:, i % 2, b * P:(b + 1) * P], IDENT)
                        last.then_inc(filled, 1)
                    elif what == "values":
                        pe.wait_ge(*read_of(f"{kind}t{i}"))
                        if h == 0 and qt >= 2:
                            pe.wait_ge(sem(f"{kind}_normed"), qt - 1)
                        blocks = att_blocks(kind, qt)
                        for b, (_, vt, _) in enumerate(blocks):
                            last = pe.matmul(obank[qt % 2][:, h * DH:(h + 1) * DH], PT[:, i % 2, b * P:(b + 1) * P],
                                             v_of(h, vt), start=b == 0, stop=b == len(blocks) - 1)
                        last.then_inc(sem(f"{kind}_values"), 1)
                    else:
                        qt = i
                        pe.wait_ge(sem(f"{kind}_normed"), qt + 1)
                        ps = take(f"{kind}o{qt}", "v")
                        for f in range(4):
                            last = pe.transpose(ps[:, f * P:(f + 1) * P], OT[:, qt % 2, f * P:(f + 1) * P], IDENT)
                        last.then_inc(filled, 1)

            pe.wait_ge(sem("tables_in"), 16)
            pe.wait_ge(sem("rows_in"), 16 * len(ROWS))
            ps = take("vec", "v")
            pe.transpose(ps[:, 0:108], VR[0:108, 0, :], IDENT[0:108, 0:108])
            pe.transpose(ps[:, 512:512 + 68], VR[0:68, 1, :], IDENT[0:68, 0:68]).then_inc(filled, 1)
            pe.wait_ge(sem("silu_c"), 1)
            mod_layer(0)
            gate_rows(0, 2)
            pe.wait_ge(sem("x_in"), 32)
            turn_tiles("h0.", X, range(6), "v")
            pe.wait_ge(*read_of("h0.5"))
            wab = a["w_in_ab"][0]
            for c in range(2):
                gemm_f(f"q{c}", wab, 0, WC, True, "a",
                       pieces=[(m * P + g * DH, DH, wab[:, (4 * g + 2 * c + m) * DH:(4 * g + 2 * c + m + 1) * DH]
                                .rearrange("(k p) n -> p k n", p=P)) for m in range(2) for g in range(2)])
            gemm_f("kv", wab, 512, WC, True, "a")
            for nm, c0, eng in (("ga", 768, "a"), ("gb", 2816, "a"), ("bg", 1792, "v"), ("xb", 1280, "v"), ("cg", 2304, "v")):
                for c in range(2):
                    gemm_f(f"{nm}{c}", wab, c0 + c * WC, WC, True, eng)
            pe.wait_ge(*read_of("kv.ctx"))
            for c, tl in enumerate(([(AQ, 0), (AQ, 1)], [(AQ, 2), (AQ, 3)], [(AKV, 0)])):
                ps = take(f"rope{c}", "v")
                for j, (src, i) in enumerate(tl):
                    last = pe.matmul(ps[:, j * L:(j + 1) * L], tab("rot_ax"), src[:, i, 0:L], start=True, stop=True)
                last.then_inc(filled, 1)
            ps = take("vtok", "a")
            for t in range(6):
                last = pe.transpose(ps[:, t * P:(t + 1) * P], AKV[:, 1, t * P:(t + 1) * P], IDENT)
            last.then_inc(filled, 1)
            pe.wait_ge(*read_of("vtok"))
            pe.wait_ge(sem("roped"), 3)
            attention("A", lambda h, qt: AQ[64 * (h // 4):64 * (h // 4) + 64, h % 4, qt * P:(qt + 1) * P],
                      lambda h, c0: AKV[64 * (h // 4):64 * (h // 4) + 64, 0, c0:c0 + P],
                      lambda h, vt: AVT[:, vt, 64 * (h // 4):64 * (h // 4) + 64], APB, APT, AOT, 640)
            pe.wait_ge(*read_of("Ao5"))
            pe.wait_ge(sem("conv"), 8)
            for c in range(4):
                gemm_t(f"y0.{c}", a["w_out_ab"][0], c * WC, 6, "v")
            if stop <= 1:
                return
            mod_layer(1)
            gate_rows(1, 1)
            pe.wait_ge(sem("x1_ready"), 6)
            turn_tiles("h1.", X, range(6), "v")
            pe.wait_ge(*read_of("h1.5"))
            wc = a["w_in_c"][0]

            def product(kind, key, wv, part):
                label = f"c{kind}{key}.{part}"
                ps = take(label, "v" if kind == "z" else "a")
                if kind in "zq":
                    if part < 2:
                        for k in range(KD):
                            last = pe.matmul(ps[:, 0:L], wv[:, k, part * P:(part + 1) * P], HT[:, k, 0:L],
                                             start=k == 0, stop=k == KD - 1)
                    else:
                        for m in range(HH):
                            for k in range(KD):
                                last = pe.matmul(ps[:, m * LC:(m + 1) * LC], wv[:, k, m * P:(m + 1) * P], HT[:, k, L:LT],
                                                 start=k == 0, stop=k == KD - 1)
                else:
                    for j in range(2):
                        t = 2 * part + j
                        for k in range(KD):
                            last = pe.matmul(ps[:, j * WC:(j + 1) * WC], HT[:, k, t * P:(t + 1) * P], wv[:, k, :],
                                             start=k == 0, stop=k == KD - 1)
                last.then_inc(filled, 1)
                return (kind, key, part, label)

            def products(st):
                if st == len(STEPS):
                    for c in range(4):
                        wv = chunk(cols(wc, 4096 + c * WC))
                        for g in range(2):
                            yield product("g", c, wv, g)
                        used_with_unit()
                    return
                hb, d = STEPS[st]
                wv = chunk(cols(wc, 1024 * (1 + d) + hb * WC))
                for part in range(3):
                    yield product("z", st, wv, part)
                used_with_unit()
                if d == 0:
                    wv = chunk(cols(wc, hb * WC))
                    for part in range(2):
                        yield product("q", hb, wv, part)
                    used_with_unit()
                    wv = chunk(cols(wc, 3072 + hb * WC))
                    for part in range(3):
                        yield product("i", hb, wv, part)
                    used_with_unit()

            rounds[-1, 0] = list(products(0))
            for st, (hb, d) in enumerate(STEPS):
                b, q = st % 2, hb % 2
                K_, Q_, I_ = HK[b], HQ[q], HI[q]
                coming = products(st + 1)
                pe.wait_ge(sem("hg_k"), st + 1)
                pe.wait_ge(*read_of(f"cq{hb}.1"))
                ps = take(f"dg{st}", "v")
                for j in range(TL * HH):
                    ch, h = divmod(j, HH)
                    last = pe.matmul(ps[:, j * P:(j + 1) * P], K_[:, h, ch * P:(ch + 1) * P],
                                     Q_[:, h, ch * P:(ch + 1) * P], start=True, stop=True)
                last.then_inc(filled, 1)
                pe.wait_ge(sem("hg_ks"), st + 1)
                pe.wait_ge(sem("hg_qi"), st + 1)
                pe.wait_ge(*read_of(f"ci{hb}.2"))
                seq = hg_seq(d)
                for i in range(7):
                    ch = seq[i] if i < 6 else None
                    if i < 6 and ch < TL:
                        pe.wait_ge(*read_of(f"su{st}.{i - 1}"))
                        ps = take(f"oi{st}.{i}", "v")
                        for h in range(HH):
                            last = pe.matmul(ps[:, h * P:(h + 1) * P], HT_[b][:, h, ch * P:(ch + 1) * P], HS[:, h, :],
                                             start=True, stop=True)
                        last.then_inc(filled, 1)
                    if i < 5:
                        ps = take(f"kt{st}.{i}", "a")
                        for h in range(HH):
                            last = pe.transpose(ps[:, h * P:(h + 1) * P], HZ[b][:, h, ch * P:(ch + 1) * P], IDENT)
                        last.then_inc(filled, 1)
                    pe.wait_ge(sem("hg_w"), 7 * st + i + 1)
                    ps = take(f"lv{st}.{i}", "v")
                    W = HW[(7 * st + i) % 2]
                    for j in range(TL * HH):
                        c4, h = divmod(j, HH)
                        wt = W[:, h, c4 * P:(c4 + 1) * P]
                        rv = wt.rearrange("p (b s h) -> p b s h", s=2, h=LEVELS[i])
                        last = pe.matmul(ps[:, j * 64:(j + 1) * 64], wt, rv[:, :, 1 - d, :], start=True, stop=True)
                    last.then_inc(filled, 1)
                    done = next(coming, None)
                    rounds[st, i] = [done] if done else []
                    if i < 5:
                        pe.wait_ge(*read_of(f"kt{st}.{i}"))
                        ps = take(f"su{st}.{i}", "v")
                        for h in range(HH):
                            last = pe.matmul(ps[:, h * P:(h + 1) * P], HKT[i % 2][:, h, :], I_[:, ch, h * P:(h + 1) * P],
                                             start=True, stop=True)
                        last.then_inc(filled, 1)
                rounds[st, 7] = list(coming)
                if d == 1:
                    pe.wait_ge(*read_of(f"lv{st}.6"))
                    ps = take(f"oo{hb}", "v")
                    for j in range(TL * HH):
                        ch, h = divmod(j, HH)
                        last = pe.matmul(ps[:, j * P:(j + 1) * P], HSC[:, j, :], I_[:, ch, h * P:(h + 1) * P],
                                         start=True, stop=True)
                    last.then_inc(filled, 1)
            pe.wait_ge(sem("c_y"), 4)
            turn_tiles("cy", HO, range(4), "a")
            pe.wait_ge(*read_of("cy3"))
            for c in range(4):
                gemm_t(f"y1.{c}", a["w_out_c"][0], c * WC, 4, "v")
            if stop <= 2:
                return
            def pre_norm(n, eng="v"):
                pe.wait_ge(sem("xn_ready"), 4 * n)
                turn_tiles(f"n{n}.", FX if n in (2, 4) else XN, range(TL), eng)
                pe.wait_ge(*read_of(f"n{n}.3"))

            pre_norm(1)
            we = a["ev_w_in_2"][0]
            def s5_input(st):
                for jj in range(2):
                    j = 2 * st + jj
                    at = 32 * (j % 4)
                    ps = take(f"bu{j}", "v")
                    for k in range(2):
                        last = pe.matmul(ps[:, k * L:(k + 1) * L], SBD[k][at:at + 32, j // 4, :], EU[at:at + 32, j // 4, :],
                                         start=True, stop=True, tile_position=(at, 0))
                    last.then_inc(filled, 1)

            def s5_output(st):
                pe.wait_ge(sem("s5_hr"), st + 1)
                pe.wait_ge(sem("s5_hi"), st + 1)
                ps = take(f"s5y{st}", "v")
                for jj in range(2):
                    at = 32 * ((2 * st + jj) % 4)
                    for k, H in enumerate((SHR, SHI)):
                        last = pe.matmul(ps[at:at + 32, 0:L], SCD[k][:, st // 2, at:at + 32], H[st % 2][:, jj, :],
                                         start=k == 0, stop=k == 1, tile_position=(0, at))
                last.then_inc(filled, 1)

            gemm_f("eu0", we, 3 * AW, WC, False, "a")
            pe.wait_ge(sem("s5_rows_in"), 32)
            pe.wait_ge(sem("s5_dt_rows"), 1)
            ps = take("s5rows", "v")
            pe.transpose(ps[:, 0:48], SROW[0:48, :], IDENT[0:48, 0:48]).then_inc(filled, 1)
            gemm_f("eu1", we, 3 * AW + WC, WC, False, "a")
            pe.wait_ge(sem("s5_cexp"), 1)
            ps = take("s5c", "v")
            for k in range(2):
                for i in range(4):
                    last = pe.transpose(ps[:, (4 * k + i) * P:(4 * k + i + 1) * P], SCEX[k][:, i, :], IDENT)
            last.then_inc(filled, 1)
            pe.wait_ge(sem("s5_bblk"), 1)
            ps = take("s5b", "v")
            for k in range(2):
                for i in range(4):
                    last = pe.transpose(ps[:, (4 * k + i) * P:(4 * k + i + 1) * P],
                                        SBBL[k][:, 4 * i:4 * i + 4, :].rearrange("p j c -> p (j c)"), IDENT)
            last.then_inc(filled, 1)
            pe.wait_ge(*read_of("s5b"))
            pe.wait_ge(*read_of("eu1.lat"))
            for st in range(S5_STEPS):
                s5_input(st)
                if st < 4:
                    gemm_f(f"eqk{st}", we, st * WC, WC, False, "a")
                elif st < 6:
                    gemm_t(f"ev{st - 4}", we, 2 * AW + (st - 4) * WC, TL, "a")
                if st:
                    s5_output(st - 1)
                if 1 <= st < 5:
                    c = st - 1
                    pe.wait_ge(*read_of(f"eqk{c}.lat"))
                    ps = take(f"erope{c}", "v")
                    for j in range(2):
                        last = pe.matmul(ps[:, j * L:(j + 1) * L], tab("rot_pt"), EQK[:, 2 * c + j, :], start=True, stop=True)
                    last.then_inc(filled, 1)
            s5_output(S5_STEPS - 1)
            pe.wait_ge(sem("s5_gelu"), 4)
            for c in range(2):
                wv = chunk(cols(a["s5_w_glu_2"][0], c * WC, WC, 0, 4), 4)
                ps = take(f"glu{c}", "a")
                for m in range(2):
                    for k in range(4):
                        last = pe.matmul(ps[:, m * L:(m + 1) * L], wv[:, k, m * P:(m + 1) * P], HT[:, 4 + k, 0:L],
                                         start=k == 0, stop=k == 3)
                last.then_inc(filled, 1)
                used_with_unit()
            pe.wait_ge(sem("eroped"), 4)
            pe.wait_ge(*read_of("ev1.t0"))
            attention("E", lambda h, qt: EQK[64 * (h % 2):64 * (h % 2) + 64, h // 2, qt * P:(qt + 1) * P],
                      lambda h, c0: EQK[64 * (h % 2):64 * (h % 2) + 64, 4 + h // 2, c0:c0 + P],
                      lambda h, vt: EV[:, vt, h * DH:(h + 1) * DH], EPB, EPT, EOT, L)
            pe.wait_ge(*read_of("Eo3"))
            pe.wait_ge(sem("s5_out"), 4)
            for c in range(4):
                gemm_t(f"em{c}", a["ev_w_out_2"][0], c * WC, TL, "a")
            if stop <= 3:
                return

            def ffn(l, n):
                pre_norm(n)
                for c in range(KF // 2):
                    gemm_f(f"fg{l}.{c}", a["ffn_w_gate_2"][l], c * WC, WC, False, "a")
                    gemm_f(f"fu{l}.{c}", a["ffn_w_up_2"][l], c * WC, WC, False, "v")
                pe.wait_ge(*read_of(f"fu{l}.{KF // 2 - 1}.lat"))
                for c in range(4):
                    gemm_t(f"fm{l}{c}", a["ffn_w_down_2"][l], c * WC, TL, "a", FH, (8, 8, 6))

            ffn(0, 2)
            if stop <= 4:
                return
            pre_norm(3)
            wo = a["od_w_in_2"][0]
            for c in range(4):
                gemm_f(f"rx{c}", wo, c * WC, WC, False, "v")
            for c in range(4):
                gemm_f(f"rz{c}", wo, D + c * WC, WC, False, "a")
            pe.wait_ge(sem("rg_conv"), 8)
            for nm, wt in (("r", a["rg_w_r_2"][0]), ("i", a["rg_w_i_2"][0])):
                wv = chunk([(0, WC, wt.rearrange("h (k p) j -> p (h k) j", p=P))])
                for h in range(4):
                    ps = take(f"rg{nm}{h}", "a")
                    for m in range(2):
                        for k in range(2):
                            last = pe.matmul(ps[:, m * L:(m + 1) * L], wv[:, 2 * h + k, m * P:(m + 1) * P],
                                             RXC[:, 2 * h + k, :], start=k == 0, stop=k == 1)
                    last.then_inc(filled, 1)
                used_with_unit()
            pe.wait_ge(sem("rg_out"), 8)
            for c in range(4):
                gemm_t(f"om{c}", a["od_w_out_2"][0], c * WC, TL, "a")
            if stop <= 5:
                return
            ffn(1, 4)

        @block.sync
        def _(sp):
            sp.dma_start(TAB[:, :], a["tables"]).then_inc(sem("tables_in"), 16)
            for c0, rows, n in ROWS:
                r = c0 % P
                sp.dma_start(VR[r:r + n, c0 // P, :], rows).then_inc(sem("rows_in"), 16)
            for n, (pieces, kt) in enumerate(chunks):
                if n == 4:
                    sp.dma_start(X[:, 0:TL, :], a["x"][0].rearrange("(t p) n -> p t n", p=P)).then_inc(sem("x_in"), 16)
                    sp.dma_start(X[:, TL:6, :], a["ctx"][0].rearrange("(t p) n -> p t n", p=P)).then_inc(sem("x_in"), 16)
                if n >= WSLOTS:
                    sp.wait_ge(*released[n - WSLOTS])
                for c0, m, src in pieces:
                    sp.dma_start(WR[:, n % WSLOTS, 0:kt, c0:c0 + m], src).then_inc(wload[n % WSLOTS], 16)

        @block.scalar
        def _(act):
            ch_ = Chain(act, "act_chain")
            link = ch_.link

            def pair(label, dst, c, ctx_, func=ACT.Copy):
                n, t0 = (LC, L) if ctx_ else (L, 0)
                act.wait_ge(*fill_of(label))
                act.activation(dst[:, 2 * c:2 * c + 2, t0:t0 + n], bank(label)[:, 0:2 * n].rearrange("p (m t) -> p m t", m=2),
                               func).then_inc(emptied["a"], 1)

            def bcast_row(dst, src):
                return act.dma_start(dst, src.partition_broadcast(P))

            bcast_row(BC[:, 0, :], a["ln_g"][0]).then_inc(sem("bc_in"), 16)
            bcast_row(BC[:, 1, :], a["ln_b"][0]).then_inc(sem("bc_in"), 16)
            bcast_row(SM[:, 0:8], a["sink_ab"][0]).then_inc(sem("sink_in"), 16)
            act.wait_ge(*read_of("vec"))
            for j, c0 in enumerate((V_C, V_CC)):
                last = act.activation(SC[:, :, j], VEC[:, c0:c0 + 8], ACT.Silu)
                link(last) if j == 0 else None
            last.then_inc(sem("silu_c"), 1)
            for j in range(2):
                act.wait_ge(*fill_of(f"gate0.{j}"))
                ps = bank(f"gate0.{j}")
                act.activation(GT[:, j, :], ps[:, :], ACT.Copy).then_inc(emptied["a"], 1)
            for c in range(2):
                for x in (0, 1):
                    pair(f"q{c}" + (".lat", ".ctx")[x], AQ, c, x)
            for x in (0, 1):
                pair("kv" + (".lat", ".ctx")[x], AKV, 0, x)
            for nm, dst in (("ga", AGA), ("gb", AGB)):
                for c in range(2):
                    for x in (0, 1):
                        pair(f"{nm}{c}" + (".lat", ".ctx")[x], dst, c, x, ACT.Silu)
            act.wait_ge(*fill_of("vtok"))
            act.activation(AVT[:, :, :], ring[units["vtok"][0] % 3][:, 0:6 * P].rearrange("p (t c) -> p t c", t=6), ACT.Copy).then_inc(emptied["a"], 1)

            def attention(kind, PB, PT, scale, sink):
                n = NT_ATT[kind] * HEADS
                for what, i in att_events(n):
                    qt, h = divmod(i, HEADS)
                    if what == "scores":
                        nb = len(att_blocks(kind, qt))
                        act.wait_ge(*fill_of(f"{kind}s{i}"))
                        ps = bank(f"{kind}s{i}")
                        act.wait_ge(sem(f"{kind}_max"), i + 1)
                        if i >= 2:
                            act.wait_ge(*fill_of(f"{kind}t{i - 2}"))
                        col = 32 + 16 * (qt % 2) + h
                        if h == 0 and qt >= 2:
                            act.wait_ge(sem(f"{kind}_normed"), qt - 1)
                        ins = act.activation(PB[:, i % 2, 0:nb * P], ps[:, 0:nb * P], ACT.Exp,
                                             bias=SM[:, col:col + 1], scale=scale,
                                             accum_out=SM[:, col + 8:col + 9])
                        ins.then_inc(emptied["a"], 1)
                        if h == HEADS - 1 and sink:
                            act.wait_ge(sem(f"{kind}_sinkarg"), qt + 1)
                            s0 = 64 + 8 * (qt % 2)
                            act.activation(SM[:, s0:s0 + 8], SM[:, s0:s0 + 8], ACT.Exp).then_inc(sem(f"{kind}_sink"), 1)
                    elif what == "turn" and i % 2 == 0:
                        nb = len(att_blocks(kind, qt))
                        act.wait_ge(*fill_of(f"{kind}t{i}"))
                        ps = bank(f"{kind}t{i}")
                        if i >= 2:
                            act.wait_ge(sem(f"{kind}_values"), i - 1)
                        act.activation(PT[:, i % 2, 0:nb * P], ps[:, 0:nb * P], ACT.Copy).then_inc(emptied["a"], 1)

            attention("A", APB, APT, 0.125, True)

            def ln_root(k, tiles):
                act.wait_ge(sem("ln_var"), k)
                act.activation(SM[:, 96:96 + tiles], SM[:, 96:96 + tiles], ACT.Sqrt).then_inc(sem("ln_root"), 1)

            ln_root(1, 6)
            act.wait_ge(sem("x1_ready"), 6)
            bcast_row(BC[:, 0, :], a["ln_g"][1]).then_inc(sem("bc_in"), 16)
            bcast_row(BC[:, 1, :], a["ln_b"][1]).then_inc(sem("bc_in"), 16)
            if stop <= 1:
                return
            bcast_row(GN, a["gnorm_c"][0]).then_inc(sem("gn_in"), 16)
            act.wait_ge(*fill_of("gate1.0"))
            ps = bank("gate1.0")
            act.activation(GT[:, 0, :], ps[:, :], ACT.Copy).then_inc(emptied["a"], 1)

            def take_products(key):
                for kind, k, part, label in rounds[key]:
                    if kind == "z":
                        continue
                    act.wait_ge(*fill_of(label))
                    two = bank(label)[:, 0:512].rearrange("p (t c) -> p t c", t=2)
                    if kind == "q":
                        act.activation(HQ[k % 2][:, part, :], bank(label)[:, 0:L], ACT.Silu).then_inc(emptied["a"], 1)
                    elif kind == "i":
                        act.activation(HI[k % 2][:, 2 * part:2 * part + 2, :], two, ACT.Copy).then_inc(emptied["a"], 1)
                    else:
                        act.activation(CG[:, 2 * part:2 * part + 2, k * WC:(k + 1) * WC], two, ACT.Silu).then_inc(emptied["a"], 1)

            DEC = [SM[:, 128 + 12 * b:140 + 12 * b] for b in range(2)]

            def log1p_exp(st):
                t = HT_[st % 2]
                act.wait_ge(sem("hg_abs"), st + 1)
                link(act.activation(t[:, :, :], t[:, :, :], ACT.Exp, scale=-1.0))
                act.activation(t[:, :, :], t[:, :, :], ACT.Ln, bias=ONES[:, 0:1]).then_inc(sem("hg_ln"), 1)

            def keys(st):
                act.wait_ge(sem("hg_karg"), st + 1)
                k = HK[st % 2]
                act.activation(k[:, :, :], k[:, :, :], ACT.Exp).then_inc(sem("hg_k"), 1)

            def state_factors(st):
                b, d = st % 2, STEPS[st][1]
                act.wait_ge(sem("hg_arg"), st + 1)
                act.activation(DEC[b], DEC[b], ACT.Exp)
                act.activation(HZ[b][:, :, :], (HP if d else HZ)[b][:, :, :], ACT.Exp)
                act.activation(HT_[b][:, :, 0:L], (HT_ if d else HP)[b][:, :, 0:L], ACT.Exp).then_inc(sem("hg_exps"), 1)

            def level_exp(g):
                act.wait_ge(sem("hg_warg"), g + 1)
                act.activation(HW[g % 2][:, :, :], HW[g % 2][:, :, :], ACT.Exp).then_inc(sem("hg_wexp"), 1)

            take_products((-1, 0))
            log1p_exp(0)
            keys(0)
            state_factors(0)
            for st in range(len(STEPS)):
                more = st + 1 < len(STEPS)
                level_exp(7 * st)
                level_exp(7 * st + 1)
                for i in range(7):
                    if i < 5:
                        act.wait_ge(*fill_of(f"kt{st}.{i}"))
                        act.activation(HKT[i % 2][:, :, :], bank(f"kt{st}.{i}")[:, 0:HH * P].rearrange("p (h c) -> p h c", h=HH),
                                       ACT.Copy).then_inc(emptied["a"], 1)
                        level_exp(7 * st + i + 2)
                    take_products((st, i))
                    if more and i == 3:
                        log1p_exp(st + 1)
                    if more and i == 5:
                        keys(st + 1)
                    if more and i == 6:
                        state_factors(st + 1)
                take_products((st, 7))
            act.wait_ge(sem("c_ms"), 1)
            act.activation(SM[:, 160:192], SM[:, 160:192], ACT.Sqrt).then_inc(sem("c_root"), 1)
            for t in range(4):
                act.wait_ge(*fill_of(f"cy{t}"))
                ps = bank(f"cy{t}")
                act.activation(HT[:, :, t * P:(t + 1) * P], ps[:, :].rearrange("p (k c) -> p k c", k=KD), ACT.Copy).then_inc(emptied["a"], 1)
            ln_root(2, 4)
            if stop <= 2:
                return
            def row_stats(name, at, n):
                src, junk = at
                for t in range(TL):
                    ins = act.activation(junk[:, t, :], src[:, t, :], ACT.Square, accum_out=SM[:, 200 + t:201 + t])
                ins.then_inc(sem(name), 1)

            def root(name, n):
                act.wait_ge(sem(name + "_ms"), n)
                act.activation(SM[:, 200:204], SM[:, 200:204], ACT.Sqrt).then_inc(sem(name + "_root"), 1)

            def pre_norm(n, ready, dst):
                act.wait_ge(sem(ready), 4)
                row_stats("rms_sum", (X, dst), n)
                root("rms", 2 * n - 1)
                act.wait_ge(sem("rms_inv"), 2 * n - 1)
                for t in range(TL):
                    act.activation(dst[:, t, :], X[:, t, :], ACT.Copy, scale=SM[:, 200 + t:201 + t]).then_inc(sem("xn_ready"), 1)

            def post_norm(n, name, dst, junk):
                for c in range(4):
                    act.wait_ge(*fill_of(f"{name}{c}.t0"))
                    ps = bank(f"{name}{c}.t0")
                    ins = act.activation(dst[:, :, c * WC:(c + 1) * WC], ps[:, :].rearrange("p (t c) -> p t c", t=4), ACT.Copy)
                    ins.then_inc(emptied["a"], 1)
                act.wait_ge(*read_of(f"{name}3.t0"))
                row_stats("rms_sum", (dst, junk), n)
                root("rms", 2 * n)

            act.wait_ge(sem("x2_ready"), 4)
            bcast_row(BC[:, 0, :], a["norm_mix_post_2"][0]).then_inc(sem("bc_in"), 16)
            bcast_row(BC[:, 1, :], a["norm_ffn_post_2"][0]).then_inc(sem("bc_in"), 16)
            act.dma_start(EPOS.bitcast(I32), a["positions_2"][0].partition_broadcast(P)).then_inc(sem("pos_in"), 16)
            act.dma_start(SROW[0:16, :], a["s5_a_re_2"][0].rearrange("(j g) p -> j (g p)", g=2)).then_inc(sem("s5_rows_in"), 16)
            act.dma_start(SROW[16:32, :], a["s5_a_im_2"][0].rearrange("(j g) p -> j (g p)", g=2)).then_inc(sem("s5_rows_in"), 16)
            act.dma_start(SM[32:48, 240:242], a["s5_log_dt_2"][0].rearrange("(j g) -> j g", g=2)).then_inc(sem("s5_dt_in"), 16)
            for k, nm in enumerate(("re", "im")):
                act.dma_start(SBRAW[k], a[f"s5_b_{nm}_2"][0].rearrange("(j g) p c -> (g p) j c", g=2)).then_inc(sem("s5_b_in"), 16)
                act.dma_start(SCRAW[k], a[f"s5_c_{nm}_2"][0].rearrange("(i g) c p -> (g c) i p", i=4)).then_inc(sem("s5_c_in"), 16)
            pre_norm(1, "x2_ready", XN)
            pair("eu0.lat", EU, 0, 0)
            act.wait_ge(sem("rope_arg"), 1)
            link(act.activation(COSP, COSP, ACT.Sin))
            act.activation(SINP, SINP, ACT.Sin).then_inc(sem("rope_tab"), 1)
            pr = lambda k: SPR[:, k, :]
            act.wait_ge(*read_of("s5rows"))
            act.activation(pr(2), pr(2), ACT.Exp).then_inc(sem("s5_dt"), 1)
            act.wait_ge(sem("s5_ang"), 1)
            link(act.activation(pr(5), pr(3), ACT.Exp))
            link(act.activation(pr(6), pr(6), ACT.Sin))
            act.activation(pr(7), pr(7), ACT.Sin).then_inc(sem("s5_sc"), 1)
            pair("eu1.lat", EU, 1, 0)
            for c in range(4):
                pair(f"eqk{c}.lat", EQK, c, 0)
            for c in range(2):
                act.wait_ge(*fill_of(f"ev{c}.t0"))
                ps = bank(f"ev{c}.t0")
                act.activation(EV[:, :, c * WC:(c + 1) * WC], ps[:, :].rearrange("p (t c) -> p t c", t=4), ACT.Copy).then_inc(emptied["a"], 1)
            for i in range(4):
                act.wait_ge(*read_of(f"s5y{2 * i + 1}"))
                act.activation(HT[:, 4 + i, 0:L], EU[:, i, :], ACT.Gelu_apprx_tanh).then_inc(sem("s5_gelu"), 1)
            for c in range(2):
                act.wait_ge(*fill_of(f"glu{c}"))
                ps = bank(f"glu{c}")
                act.activation(EU[:, 2 * c:2 * c + 2, :], ps[:, :].rearrange("p (m t) -> p m t", m=2), ACT.Sigmoid).then_inc(emptied["a"], 1)
            attention("E", EPB, EPT, 0.125, False)
            post_norm(1, "em", MX, XN)
            if stop <= 3:
                return

            def ffn(l, n, ready):
                pre_norm(n, ready, FX)
                for c in range(KF // 2):
                    act.wait_ge(*fill_of(f"fg{l}.{c}.lat"))
                    ps = bank(f"fg{l}.{c}.lat")
                    if c >= 2:
                        act.wait_ge(*read_of(f"fu{l}.{c - 2}.lat"))
                    act.activation(FSG[:, c % 2], ps[:, :].rearrange("p (m t) -> p m t", m=2), ACT.Silu).then_inc(emptied["a"], 1)
                post_norm(n, f"fm{l}", FX, FH[:, 0:8, :].rearrange("p a b -> p (a b)").rearrange("p (t n) -> p t n", t=4))

            ffn(0, 2, "x3_ready")
            if stop <= 4:
                return
            act.wait_ge(sem("x4_ready"), 4)
            bcast_row(BC[:, 0, :], a["norm_mix_post_2"][1]).then_inc(sem("bc_in"), 16)
            bcast_row(BC[:, 1, :], a["norm_ffn_post_2"][1]).then_inc(sem("bc_in"), 16)
            pre_norm(3, "x4_ready", XN)
            act.wait_ge(sem("lam_abs"), 1)
            link(act.activation(SM[:, 216:224], SM[:, 216:224], ACT.Exp, scale=-1.0))
            act.activation(SM[:, 216:224], SM[:, 216:224], ACT.Ln, bias=ONES[:, 0:1]).then_inc(sem("lam_ln"), 1)
            for c in range(4):
                pair(f"rz{c}.lat", RZG, c, 0, ACT.Gelu_apprx_tanh)
            for nm, dst, v0 in (("r", RA, V_BR), ("i", RGI, V_BI)):
                for h in range(4):
                    act.wait_ge(*fill_of(f"rg{nm}{h}"))
                    ps = bank(f"rg{nm}{h}")
                    for m in range(2):
                        t = 2 * h + m
                        last = act.activation(dst[:, t, :], ps[:, m * L:(m + 1) * L], ACT.Sigmoid, bias=VEC[:, v0 + t:v0 + t + 1])
                    last.then_inc(emptied["a"], 1)
            act.wait_ge(*read_of("rgi3"))
            act.wait_ge(sem("rg_sp"), 1)
            for t in range(8):
                link(act.activation(RTH[:, t, :], RA[:, t, :], ACT.Tanh, scale=SM[:, 224 + t:225 + t]))
                act.activation(RA[:, t, :], RA[:, t, :], ACT.Exp, scale=SM[:, 232 + t:233 + t]).then_inc(sem("rg_a"), 1)
            for t in range(8):
                act.wait_ge(sem("rg_msq"), t + 1)
                act.activation(RM[:, t, :], RM[:, t, :], ACT.Sqrt).then_inc(sem("rg_mult"), 1)
            post_norm(3, "om", MX, XN)
            if stop <= 5:
                return
            ffn(1, 4, "x5_ready")

        @block.vector
        def _(dve):
            ch_ = Chain(dve, "dve_chain")
            link = ch_.link

            def mod_layer(l):
                for g in range(3):
                    dve.wait_ge(*fill_of(f"mod{l}.{g}"))
                    ps = bank(f"mod{l}.{g}")
                    b = VEC[:, V_BADA + 24 * l + 8 * g:V_BADA + 24 * l + 8 * g + 8]
                    ins = dve.tensor_tensor(MOD[:, l, 8 * g:8 * g + 8, :], ps[:, 0:16].rearrange("p (m j) -> p m j", j=2),
                                            b.unsqueeze(2).to_broadcast([P, 8, 2]), ALU.add)
                    ins.then_inc(emptied["v"], 1)
                    if g == 1:
                        dve.wait_ge(*read_of(f"mod{l}.{g}"))
                        link(dve.tensor_scalar(MOD[:, l, 8:16, :], MOD[:, l, 8:16, :], 1.0, None, ALU.add))
                dve.wait_ge(*read_of(f"mod{l}.2"))

            def gate_diag(l, n):
                for j in range(n):
                    if j:
                        dve.wait_ge(*fill_of(f"gate{l}.{j - 1}"))
                    dve.tensor_tensor(DG[:, :, :], IDENT.unsqueeze(1).to_broadcast([P, KD, P]),
                                      MOD[:, l, 16:24, j].unsqueeze(2).to_broadcast([P, KD, P]),
                                      ALU.mult).then_inc(sem(f"gate_diag{l}"), 1)

            def modulated(l, name, tiles):
                for t in tiles:
                    dve.wait_ge(*fill_of(f"{name}{t}"))
                    ps = bank(f"{name}{t}")
                    j = 0 if t < TL else 1
                    dst = HT[:, :, t * P:(t + 1) * P]
                    link(dve.tensor_tensor(dst, ps[:, :].rearrange("p (k c) -> p k c", k=KD),
                                           MOD[:, l, 8:16, j].unsqueeze(2).to_broadcast([P, KD, P]), ALU.mult))
                    dve.tensor_tensor(dst, dst, MOD[:, l, 0:8, j].unsqueeze(2).to_broadcast([P, KD, P]), ALU.add).then_inc(emptied["v"], 1)

            def join_gated(name, tiles, tmp):
                for c in range(4):
                    for g, t0, nt in ((0, 0, 4), (1, 4, 2)):
                        if t0 >= tiles:
                            continue
                        dve.wait_ge(*fill_of(f"{name}.{c}.t{g}"))
                        ps = bank(f"{name}.{c}.t{g}")
                        gate = GT[:, g, c * WC:(c + 1) * WC].unsqueeze(1).to_broadcast([P, nt, WC])
                        xs = X[:, t0:t0 + nt, c * WC:(c + 1) * WC]
                        ins = dve.tensor_tensor(tmp[:, 0:nt, :], ps[:, 0:nt * WC].rearrange("p (t c) -> p t c", t=nt), gate, ALU.mult)
                        ins.then_inc(emptied["v"], 1)
                        dve.wait_ge(*read_of(f"{name}.{c}.t{g}"))
                        link(dve.scalar_tensor_tensor(out=xs, in0=xs, scalar=ALPHA, in1=tmp[:, 0:nt, :], op0=ALU.mult, op1=ALU.add))

            def layer_norm(k, tiles, bc_count):
                for t in range(tiles):
                    for h in range(2):
                        last = dve.bn_stats(SM[:, 256 + 12 * t + 6 * h:256 + 12 * t + 6 * h + 6], X[:, t, h * 512:(h + 1) * 512])
                    link(last)
                    link(dve.bn_aggr(SM[:, 104 + 2 * t:106 + 2 * t], SM[:, 256 + 12 * t:268 + 12 * t]))
                mv = SM[:, 104:104 + 2 * tiles].rearrange("p (t m) -> p t m", m=2)
                dve.tensor_scalar(SM[:, 96:96 + tiles], mv[:, :, 1], LN_EPS, None, ALU.add).then_inc(sem("ln_var"), 1)
                dve.wait_ge(sem("ln_root"), k)
                link(dve.reciprocal(SM[:, 96:96 + tiles], SM[:, 96:96 + tiles]))
                dve.wait_ge(sem("bc_in"), bc_count)
                for t in range(tiles):
                    link(dve.tensor_scalar(X[:, t, :], X[:, t, :], SM[:, 104 + 2 * t:105 + 2 * t], SM[:, 96 + t:97 + t],
                                           ALU.subtract, ALU.mult))
                    link(dve.tensor_tensor(X[:, t, :], X[:, t, :], BC[:, 0, :], ALU.mult))
                    dve.tensor_tensor(X[:, t, :], X[:, t, :], BC[:, 1, :], ALU.add).then_inc(sem(f"x{k}_ready"), 1)

            dve.wait_ge(*fill_of("vec"))
            ps = bank("vec")
            link(dve.tensor_copy(VEC[:, 0:108], ps[:, 0:108]))
            ins = dve.tensor_copy(VEC[:, 128:196], ps[:, 512:580])
            ins.then_inc(emptied["v"], 1)
            dve.wait_ge(*read_of("vec"))
            dve.wait_ge(sem("sink_in"), 16)
            link(dve.tensor_scalar(SM[:, 8:16], SM[:, 0:8], -1.0, None, ALU.mult))
            mod_layer(0)
            gate_diag(0, 2)
            modulated(0, "h0.", range(6))
            zero = tab("chunk", 0, 1)
            for i in range(4):
                for e in (0, L + 1, L + 2, LT + 3):
                    dve.memset(AU[:, i, e:e + 1], 0.0)
            lat_u = lambda c: AU[:, 2 * c:2 * c + 2, 1:1 + L]
            ctx_u = lambda c: AU[:, 2 * c:2 * c + 2, L + 3:L + 3 + LC]

            def two(ps, n):
                return ps[:, 0:2 * n].rearrange("p (m t) -> p m t", m=2)

            dve.wait_ge(*read_of("gb1.ctx"))
            for c in range(2):
                dve.wait_ge(*fill_of(f"bg{c}.lat"))
                dve.tensor_tensor(AGB[:, 2 * c:2 * c + 2, 0:L], AGB[:, 2 * c:2 * c + 2, 0:L], two(bank(f"bg{c}.lat"), L), ALU.mult).then_inc(emptied["v"], 1)
                dve.wait_ge(*fill_of(f"bg{c}.ctx"))
                dve.tensor_tensor(AGB[:, 2 * c:2 * c + 2, L:LT], AGB[:, 2 * c:2 * c + 2, L:LT], two(bank(f"bg{c}.ctx"), LC), ALU.mult).then_inc(emptied["v"], 1)
            for c in range(2):
                dve.wait_ge(*fill_of(f"xb{c}.lat"))
                dve.tensor_copy(lat_u(c), two(bank(f"xb{c}.lat"), L)).then_inc(emptied["v"], 1)
                dve.wait_ge(*fill_of(f"xb{c}.ctx"))
                dve.tensor_copy(ctx_u(c), two(bank(f"xb{c}.ctx"), LC)).then_inc(emptied["v"], 1)
            dve.wait_ge(*read_of("xb1.ctx"))
            for c in range(2):
                dve.wait_ge(*fill_of(f"cg{c}.lat"))
                dve.tensor_tensor(lat_u(c), lat_u(c), two(bank(f"cg{c}.lat"), L), ALU.mult).then_inc(emptied["v"], 1)
                dve.wait_ge(*fill_of(f"cg{c}.ctx"))
                dve.tensor_tensor(ctx_u(c), ctx_u(c), two(bank(f"cg{c}.ctx"), LC), ALU.mult).then_inc(emptied["v"], 1)
            cosb = lambda n: tab("cos_ax").unsqueeze(1).to_broadcast([P, n, L])
            sinb = lambda n: tab("sin_ax").unsqueeze(1).to_broadcast([P, n, L])

            def rope(label, x, n, cb, sb_, tmp, name, count):
                dve.wait_ge(*fill_of(label))
                ps = bank(label)
                ins = dve.tensor_tensor(tmp[:, 0:n, :], ps[:, 0:n * L].rearrange("p (m t) -> p m t", m=n), sb_(n), ALU.mult)
                ins.then_inc(emptied["v"], 1)
                dve.wait_ge(*read_of(label))
                link(dve.tensor_tensor(x, x, cb(n), ALU.mult))
                dve.tensor_tensor(x, x, tmp[:, 0:n, :], ALU.add).then_inc(sem(name), 1)
                dve.wait_ge(sem(name), count)

            rope("rope0", AQ[:, 0:2, 0:L], 2, cosb, sinb, ROT, "roped", 1)
            rope("rope1", AQ[:, 2:4, 0:L], 2, cosb, sinb, ROT, "roped", 2)
            rope("rope2", AKV[:, 0:1, 0:L], 1, cosb, sinb, ROT, "roped", 3)

            def conv_tile(i):
                for s0, n, d0 in ((0, L, 0), (L + 2, LC, L)):
                    acc = ACV[:, i % 2, d0:d0 + n]
                    wcol = lambda j: VEC[:, V_CONV + 4 * j + i:V_CONV + 4 * j + i + 1]
                    link(dve.tensor_scalar(acc, AU[:, i, s0:s0 + n], wcol(0), None, ALU.mult))
                    for j in (1, 2):
                        link(dve.scalar_tensor_tensor(out=acc, in0=AU[:, i, s0 + j:s0 + j + n], scalar=wcol(j), in1=acc,
                                                      op0=ALU.mult, op1=ALU.add))
                    dve.tensor_tensor(HT[:, 4 + i, d0:d0 + n], acc, AGB[:, i, d0:d0 + n], ALU.mult).then_inc(sem("conv"), 1)

            def attention(kind, PT, OT, scale, sink, finish, between):
                n = NT_ATT[kind] * HEADS
                for what, i in att_events(n):
                    qt, h = divmod(i, HEADS)
                    if what == "scores":
                        nb = len(att_blocks(kind, qt))
                        nu, e, k = units[f"{kind}s{i}"]
                        dve.wait_ge(filled, nu + 1)
                        col = 32 + 16 * (qt % 2) + h
                        if h == 0 and qt >= 2:
                            dve.wait_ge(*read_of(f"{kind}s{(qt - 1) * HEADS - 1}"))
                            if sink:
                                dve.wait_ge(sem(f"{kind}_sink"), qt - 1)
                        link(dve.tensor_reduce(SM[:, 80:81], ring[nu % 3][:, 0:nb * P], AX.X, ALU.max))
                        ins = dve.tensor_scalar(SM[:, col:col + 1], SM[:, 80:81], -scale,
                                                SM[:, 8 + h:9 + h] if sink else None,
                                                ALU.mult, *([ALU.min] if sink else []))
                        ins.then_inc(sem(f"{kind}_max"), 1)
                        dve.wait_ge(sem(f"{kind}_max"), i + 1)
                        if h == HEADS - 1 and sink:
                            s0, b0 = 64 + 8 * (qt % 2), 32 + 16 * (qt % 2)
                            dve.tensor_tensor(SM[:, s0:s0 + 8], SM[:, 0:8], SM[:, b0:b0 + 8], ALU.add).then_inc(sem(f"{kind}_sinkarg"), 1)
                    elif what == "turn" and i % 2:
                        nb = len(att_blocks(kind, qt))
                        dve.wait_ge(*fill_of(f"{kind}t{i}"))
                        ps = bank(f"{kind}t{i}")
                        if i >= 2:
                            dve.wait_ge(sem(f"{kind}_values"), i - 1)
                        dve.tensor_copy(PT[:, i % 2, 0:nb * P], ps[:, 0:nb * P]).then_inc(emptied["v"], 1)
                    elif what == "finish":
                        qt = i
                        last_s = units[f"{kind}s{qt * HEADS + HEADS - 1}"]
                        dve.wait_ge(emptied["a"], last_s[2])
                        den = SM[:, 32 + 16 * (qt % 2) + 8:32 + 16 * (qt % 2) + 16]
                        if sink:
                            dve.wait_ge(sem(f"{kind}_sink"), qt + 1)
                            s0 = 64 + 8 * (qt % 2)
                            link(dve.tensor_tensor(SM[:, 82:90], den, SM[:, s0:s0 + 8], ALU.add))
                            link(dve.reciprocal(SM[:, 82:90], SM[:, 82:90]))
                        else:
                            link(dve.reciprocal(SM[:, 82:90], den))
                        dve.wait_ge(sem(f"{kind}_values"), (qt + 1) * HEADS)
                        if qt >= 2:
                            dve.wait_ge(*fill_of(f"{kind}o{qt - 2}"))
                        dve.tensor_tensor(OT[:, qt % 2, :].rearrange("p (h c) -> p h c", h=HEADS),
                                          obank[qt % 2][:, :].rearrange("p (h c) -> p h c", h=HEADS),
                                          SM[:, 82:90].unsqueeze(2).to_broadcast([P, HEADS, DH]),
                                          ALU.mult).then_inc(sem(f"{kind}_normed"), 1)
                        dve.wait_ge(sem(f"{kind}_normed"), qt + 1)
                        between(qt)
                        dve.wait_ge(*fill_of(f"{kind}o{qt}"))
                        ps = bank(f"{kind}o{qt}")
                        finish(qt, ps[:, 0:512].rearrange("p (f c) -> p f c", f=4))

            def finish_a(qt, o):
                dve.tensor_tensor(HT[:, 0:4, qt * P:(qt + 1) * P], o, AGA[:, :, qt * P:(qt + 1) * P], ALU.mult).then_inc(emptied["v"], 1)

            attention("A", APT, AOT, 0.125, True, finish_a, lambda qt: conv_tile(qt) if qt < 4 else None)
            join_gated("y0", 6, ATMP)
            layer_norm(1, 6, 32)
            if stop <= 1:
                return

            mod_layer(1)
            gate_diag(1, 1)
            modulated(1, "h1.", range(6))
            QS = 128.0 ** -0.5

            def take_products(key):
                for kind, k, part, label in rounds[key]:
                    if kind == "z":
                        z = HZ[k % 2]
                        dve.wait_ge(*fill_of(label))
                        if part < 2:
                            dve.tensor_copy(z[:, part, 0:L], bank(label)[:, 0:L]).then_inc(emptied["v"], 1)
                        else:
                            dve.tensor_copy(z[:, :, L:LT], two(bank(label), LC)).then_inc(emptied["v"], 1)

            DEC = [SM[:, 128 + 12 * b:140 + 12 * b].rearrange("p (h c) -> p h c", h=HH) for b in range(2)]
            PL = [SM[:, 352 + 12 * b:364 + 12 * b].rearrange("p (h c) -> p h c", h=HH) for b in range(2)]

            def abs_z(st):
                z = HZ[st % 2]
                dve.wait_ge(*read_of(f"cz{st}.2"))
                dve.scalar_tensor_tensor(out=HT_[st % 2][:, :, :], in0=z[:, :, :], scalar=-1.0, in1=z[:, :, :],
                                         op0=ALU.mult, op1=ALU.max).then_inc(sem("hg_abs"), 1)

            def log_f_and_sums(st):
                b = st % 2
                dve.wait_ge(sem("hg_ln"), st + 1)
                dve.scalar_tensor_tensor(out=HT_[b][:, :, :], in0=HZ[b][:, :, :], scalar=0.0, in1=HT_[b][:, :, :],
                                         op0=ALU.min, op1=ALU.subtract).then_inc(sem("hg_lf"), 1)
                dve.wait_ge(sem("hg_lf"), st + 1)
                for h in range(HH):
                    dve.tensor_tensor_scan(HP[b][:, h, 0:L], tab("chunk"), HT_[b][:, h, 0:L], 0.0, ALU.mult, ALU.add)
                    last = dve.tensor_tensor_scan(HP[b][:, h, L:LT], tab("chunk", 0, LC), HT_[b][:, h, L:LT], 0.0, ALU.mult, ALU.add)
                link(last)
                link(dve.tensor_copy(PL[b], HP[b][:, :, :].rearrange("p h (c t) -> p h c t", t=P)[:, :, :, P - 1]))
                dve.tensor_copy(DEC[b], PL[b]).then_inc(sem("hg_sums"), 1)

            def state_operands(st):
                b, q = st % 2, STEPS[st][0] % 2
                dve.wait_ge(sem("hg_k"), st + 1)
                dve.wait_ge(sem("hg_exps"), st + 1)
                dve.tensor_tensor(HZ[b][:, :, :], HZ[b][:, :, :], HK[b][:, :, :], ALU.mult).then_inc(sem("hg_ks"), 1)
                dve.wait_ge(*read_of(f"cq{STEPS[st][0]}.1"))
                dve.tensor_tensor(HT_[b][:, :, 0:L], HT_[b][:, :, 0:L], HQ[q][:, :, :], ALU.mult).then_inc(sem("hg_qi"), 1)

            def level_operand(g):
                st, li = divmod(g, 7)
                hb, d = STEPS[st]
                dve.wait_ge(sem("hg_wexp"), g + 1)
                w4 = HW[g % 2][:, :, :].rearrange("p g (b s h) -> p g b s h", s=2, h=LEVELS[li])
                for side in range(2):
                    f = (HK[st % 2] if side == d else HQ[hb % 2])[:, :, 0:L]
                    f4 = f.rearrange("p g (b s h) -> p g b s h", s=2, h=LEVELS[li])
                    last = dve.tensor_tensor(w4[:, :, :, side, :], w4[:, :, :, side, :], f4[:, :, :, side, :], ALU.mult)
                last.then_inc(sem("hg_w"), 1)

            take_products((-1, 0))
            abs_z(0)
            log_f_and_sums(0)
            state_operands(0)
            for st, (hb, d) in enumerate(STEPS):
                more = st + 1 < len(STEPS)
                b = st % 2
                level_operand(7 * st)
                dve.wait_ge(*fill_of(f"dg{st}"))
                src = bank(f"dg{st}")[:, :].rearrange("p (j c) -> p j c", j=TL * HH)
                idb = IDENT.unsqueeze(1).to_broadcast([P, TL * HH, P])
                if d == 0:
                    dve.tensor_tensor(HSC[:, :, :], src, idb, ALU.mult).then_inc(emptied["v"], 1)
                    dve.wait_ge(*read_of(f"dg{st}"))
                else:
                    dve.tensor_tensor(HDG[:, :, :], src, idb, ALU.mult).then_inc(emptied["v"], 1)
                    dve.wait_ge(*read_of(f"dg{st}"))
                    link(dve.tensor_tensor(HSC[:, :, :], HSC[:, :, :], HDG[:, :, :], ALU.add))
                seq = hg_seq(d)
                for i in range(7):
                    ch = seq[i] if i < 6 else None
                    if i < 6 and ch < TL:
                        dve.wait_ge(*fill_of(f"oi{st}.{i}"))
                        o = HO[:, ch, hb * WC:(hb + 1) * WC]
                        ps = bank(f"oi{st}.{i}")[:, 0:WC]
                        if d == 0:
                            dve.tensor_scalar(o, ps, QS, None, ALU.mult).then_inc(emptied["v"], 1)
                        else:
                            dve.scalar_tensor_tensor(out=o, in0=ps, scalar=QS, in1=o, op0=ALU.mult, op1=ALU.add).then_inc(emptied["v"], 1)
                    if i < 6:
                        level_operand(7 * st + i + 1)
                    dve.wait_ge(*fill_of(f"lv{st}.{i}"))
                    h2 = LEVELS[i]
                    nb = 64 // h2
                    m = tab("lv_f" if d == 0 else "lv_b", 64 * i, 64 * i + 64).bitcast(U32)
                    m = m.rearrange("p (b h) -> p b h", h=h2).unsqueeze(1).to_broadcast([P, TL * HH, nb, h2])
                    o = HSC[:, :, :].rearrange("p j (b s h) -> p j b s h", s=2, h=h2)[:, :, :, 1 - d, :]
                    ps = bank(f"lv{st}.{i}")[:, 0:512].rearrange("p (j b h) -> p j b h", j=TL * HH, h=h2)
                    dve.copy_predicated(o, m, ps).then_inc(emptied["v"], 1)
                    dve.wait_ge(*read_of(f"lv{st}.{i}"))
                    take_products((st, i))
                    if more and i == 2:
                        abs_z(st + 1)
                    if more and i == 4:
                        log_f_and_sums(st + 1)
                    if i < 5:
                        dve.wait_ge(*fill_of(f"su{st}.{i}"))
                        ps = bank(f"su{st}.{i}")
                        if i == 0:
                            dve.tensor_copy(HS[:, :, :], ps[:, 0:WC].rearrange("p (h c) -> p h c", h=HH)).then_inc(emptied["v"], 1)
                        else:
                            for h in range(HH):
                                ins = dve.scalar_tensor_tensor(out=HS[:, h, :], in0=HS[:, h, :], scalar=DEC[b][:, h, ch:ch + 1],
                                                               in1=ps[:, h * P:(h + 1) * P], op0=ALU.mult, op1=ALU.add)
                            ins.then_inc(emptied["v"], 1)
                        dve.wait_ge(*read_of(f"su{st}.{i}"))
                    if more and i == 6:
                        state_operands(st + 1)
                take_products((st, 7))
                if d == 1:
                    dve.wait_ge(*fill_of(f"oo{hb}"))
                    o = HO[:, :, hb * WC:(hb + 1) * WC]
                    dve.scalar_tensor_tensor(out=o, in0=bank(f"oo{hb}")[:, :].rearrange("p (t c) -> p t c", t=TL), scalar=QS, in1=o,
                                             op0=ALU.mult, op1=ALU.add).then_inc(emptied["v"], 1)
                    dve.wait_ge(*read_of(f"oo{hb}"))
            MS = SM[:, 160:192].rearrange("p (t h) -> p t h", t=4)
            o3 = lambda t: HO[:, t, :].rearrange("p (h c) -> p h c", h=HEADS)
            for t in range(TL):
                link(dve.tensor_tensor(CSQ, HO[:, t, :], HO[:, t, :], ALU.mult))
                link(dve.tensor_reduce(MS[:, t, :], CSQ.rearrange("p (h c) -> p h c", h=HEADS), AX.X, ALU.add))
            dve.tensor_scalar(SM[:, 160:192], SM[:, 160:192], 1.0 / P, RMS_EPS, ALU.mult, ALU.add).then_inc(sem("c_ms"), 1)
            dve.wait_ge(sem("c_root"), 1)
            link(dve.reciprocal(SM[:, 160:192], SM[:, 160:192]))
            dve.wait_ge(sem("gn_in"), 16)
            dve.wait_ge(*read_of("cg3.1"))
            for t in range(TL):
                link(dve.tensor_tensor(o3(t), o3(t), MS[:, t, :].unsqueeze(2).to_broadcast([P, HEADS, P]), ALU.mult))
                link(dve.tensor_tensor(o3(t), o3(t), GN.unsqueeze(1).to_broadcast([P, HEADS, P]), ALU.mult))
                dve.tensor_tensor(HO[:, t, :], HO[:, t, :], CG[:, t, :], ALU.mult).then_inc(sem("c_y"), 1)
            join_gated("y1", 4, CTMP)
            layer_norm(2, 4, 64)
            if stop <= 2:
                return
            R4 = SM[:, 200:204]

            def inv_rms(k):
                dve.wait_ge(sem("rms_sum"), k)
                dve.tensor_scalar(R4, R4, 1.0 / D, RMS_EPS, ALU.mult, ALU.add).then_inc(sem("rms_ms"), 1)
                dve.wait_ge(sem("rms_root"), k)
                dve.reciprocal(R4, R4).then_inc(sem("rms_inv"), 1)
                dve.wait_ge(sem("rms_inv"), k)

            def pre_norm(n, v0):
                inv_rms(2 * n - 1)
                for t in range(TL):
                    dve.wait_ge(*fill_of(f"n{n}.{t}"))
                    ps = bank(f"n{n}.{t}")
                    dve.tensor_tensor(HT[:, :, t * P:(t + 1) * P], ps[:, :].rearrange("p (k c) -> p k c", k=KD),
                                           VEC[:, v0:v0 + 8].unsqueeze(2).to_broadcast([P, KD, P]), ALU.mult).then_inc(emptied["v"], 1)

            def post_norm(n, src, b, count):
                inv_rms(2 * n)
                dve.wait_ge(sem("bc_in"), count)
                for t in range(TL):
                    link(dve.scalar_tensor_tensor(out=src[:, t, :], in0=src[:, t, :], scalar=SM[:, 200 + t:201 + t],
                                                  in1=BC[:, b, :], op0=ALU.mult, op1=ALU.mult))
                    dve.tensor_tensor(X[:, t, :], X[:, t, :], src[:, t, :], ALU.add).then_inc(sem(f"x{n + 2}_ready"), 1)

            C1, C2 = 6.28125, 0.0019340515136718750
            C3 = TWO_PI - C1 - C2
            PI_ = 3.1415925

            def sine_args(ang, s_, c_, tmp, ready):
                link(dve.tensor_scalar(tmp, ang, 1.0 / TWO_PI, MAGIC, ALU.mult, ALU.add))
                link(dve.tensor_scalar(tmp, tmp, -MAGIC, None, ALU.add))
                link(dve.scalar_tensor_tensor(out=s_, in0=tmp, scalar=-C1, in1=ang, op0=ALU.mult, op1=ALU.add))
                link(dve.scalar_tensor_tensor(out=s_, in0=tmp, scalar=-C2, in1=s_, op0=ALU.mult, op1=ALU.add))
                link(dve.scalar_tensor_tensor(out=s_, in0=tmp, scalar=-C3, in1=s_, op0=ALU.mult, op1=ALU.add))
                link(dve.tensor_scalar(c_, s_, np.pi / 2, None, ALU.add))
                link(dve.tensor_scalar(tmp, c_, np.pi, TWO_PI, ALU.is_gt, ALU.mult))
                link(dve.tensor_tensor(c_, c_, tmp, ALU.subtract))
                link(dve.tensor_scalar(c_, c_, PI_, -PI_, ALU.min, ALU.max))
                dve.tensor_scalar(s_, s_, PI_, -PI_, ALU.min, ALU.max).then_inc(sem(ready), 1)

            colt = lambda k: tab("cols", k, k + 1)
            pre_norm(1, V_NPRE)
            dve.wait_ge(sem("pos_in"), 16)
            A1, A2 = SP1[:, 0, :], SP2[:, 0, :]
            link(dve.tensor_copy(A1, EPOS.bitcast(I32)))
            link(dve.tensor_scalar(A1, A1, colt(0), None, ALU.mult))
            sine_args(A1, SINP, COSP, A2, "rope_arg")
            dve.wait_ge(sem("s5_dt_in"), 16)
            dve.tensor_copy(SROW[32:48, :].rearrange("j (g p) -> j g p", g=2),
                            SM[32:48, 240:242].unsqueeze(2).to_broadcast([16, 2, DH])).then_inc(sem("s5_dt_rows"), 1)
            dve.wait_ge(sem("s5_c_in"), 32)
            for k, sg in ((0, 1.0), (1, -1.0)):
                for gg in range(2):
                    ins = dve.tensor_scalar(SCEX[k][:, :, gg * DH:(gg + 1) * DH], SCRAW[k], colt(2 + gg), sg, ALU.mult, ALU.mult)
                    if (k, gg) != (1, 1):
                        link(ins)
            ins.then_inc(sem("s5_cexp"), 1)
            pr = lambda k: SPR[:, k, :]
            dve.wait_ge(*fill_of("s5rows"))
            ps = bank("s5rows")
            dve.tensor_copy(SPR[:, 0:3, :], ps[:, 0:48].rearrange("p (k j) -> p k j", k=3)).then_inc(emptied["v"], 1)
            dve.wait_ge(*read_of("s5rows"))
            dve.wait_ge(sem("s5_dt"), 1)
            mul = lambda o, x, y: link(dve.tensor_tensor(o, x, y, ALU.mult))
            add = lambda o, x, y: link(dve.tensor_tensor(o, x, y, ALU.add))
            sub = lambda o, x, y: link(dve.tensor_tensor(o, x, y, ALU.subtract))
            mul(pr(3), pr(0), pr(2))
            mul(pr(4), pr(1), pr(2))
            sine_args(pr(4), pr(6), pr(7), pr(8), "s5_ang")
            dve.wait_ge(sem("s5_ang"), 1)
            mul(pr(8), pr(0), pr(0))
            mul(pr(9), pr(1), pr(1))
            add(pr(8), pr(8), pr(9))
            link(dve.reciprocal(pr(8), pr(8)))
            dve.wait_ge(sem("s5_sc"), 1)
            mul(pr(9), pr(5), pr(7))
            link(dve.tensor_scalar(pr(9), pr(9), -1.0, None, ALU.add))
            mul(pr(10), pr(5), pr(6))
            mul(pr(11), pr(9), pr(0))
            mul(pr(12), pr(10), pr(1))
            add(pr(11), pr(11), pr(12))
            mul(pr(11), pr(11), pr(8))
            mul(pr(12), pr(10), pr(0))
            mul(pr(13), pr(9), pr(1))
            sub(pr(12), pr(12), pr(13))
            mul(pr(12), pr(12), pr(8))
            dve.wait_ge(sem("s5_b_in"), 32)
            wr, wi = (pr(k).unsqueeze(2).to_broadcast([P, 16, 16]) for k in (11, 12))
            q1 = A1[:, 0:256].rearrange("p (j c) -> p j c", j=16)
            q2 = A1[:, 256:512].rearrange("p (j c) -> p j c", j=16)
            q3 = A2[:, 0:256].rearrange("p (j c) -> p j c", j=16)
            mul(q1, SBRAW[0], wr)
            mul(q2, SBRAW[1], wi)
            sub(q1, q1, q2)
            mul(q2, SBRAW[0], wi)
            mul(q3, SBRAW[1], wr)
            add(q2, q2, q3)
            for k, q in ((0, q1), (1, q2)):
                for gg in range(2):
                    ins = dve.tensor_scalar(SBBL[k][:, :, gg * 16:(gg + 1) * 16], q, colt(4 + gg), None, ALU.mult)
                    if (k, gg) != (1, 1):
                        link(ins)
            ins.then_inc(sem("s5_bblk"), 1)
            dve.wait_ge(*fill_of("s5c"))
            ps = bank("s5c")
            for k in range(2):
                ins = dve.tensor_copy(SCD[k], ps[:, 512 * k:512 * k + 512].rearrange("p (i c) -> p i c", i=4))
                link(ins) if k == 0 else ins.then_inc(emptied["v"], 1)
            dve.wait_ge(*fill_of("s5b"))
            ps = bank("s5b")
            for k in range(2):
                ins = dve.tensor_copy(SBD[k], ps[:, 512 * k:512 * k + 512].rearrange("p (i c) -> p i c", i=4))
                link(ins) if k == 0 else ins.then_inc(emptied["v"], 1)

            def s5_step(st):
                b = st % 2
                er, ei, br, bi = SER[b], SEI[b], SBR[b], SBI[b]
                dve.wait_ge(sem("s5_tables"), st + 1)
                if st >= 2:
                    dve.wait_ge(sem("s5_hi"), st - 1)
                if st:
                    dve.wait_ge(sem("s5_hr"), st)
                for jj in range(2):
                    label = f"bu{2 * st + jj}"
                    dve.wait_ge(*fill_of(label))
                    ur, ui = bank(label)[:, 0:L], bank(label)[:, L:2 * L]
                    dve.tensor_tensor(br[:, jj, :], er[:, jj, :], ur, ALU.mult)
                    dve.tensor_tensor(bi[:, jj, :], er[:, jj, :], ui, ALU.mult)
                    dve.tensor_tensor(SP1[:, jj, :], ei[:, jj, :], ui, ALU.mult)
                    dve.tensor_tensor(SP2[:, jj, :], ei[:, jj, :], ur, ALU.mult).then_inc(emptied["v"], 1)
                dve.wait_ge(*read_of(f"bu{2 * st + 1}"))
                dve.tensor_tensor(br, br, SP1, ALU.add)
                link(dve.tensor_tensor(bi, bi, SP2, ALU.subtract))
                for jj in range(2):
                    rho = pr(5)[:, 2 * st + jj:2 * st + jj + 1].to_broadcast([P, L])
                    dve.tensor_tensor_scan(br[:, jj, :], rho, br[:, jj, :], 0.0, ALU.mult, ALU.add)
                    last = dve.tensor_tensor_scan(bi[:, jj, :], rho, bi[:, jj, :], 0.0, ALU.mult, ALU.add)
                last.then_inc(sem("s5_sums"), 1)
                dve.wait_ge(sem("s5_sums"), st + 1)
                if st >= 2:
                    dve.wait_ge(*fill_of(f"s5y{st - 2}"))
                dve.tensor_tensor(SHR[b], er, br, ALU.mult)
                link(dve.tensor_tensor(SP1, ei, bi, ALU.mult))
                dve.tensor_tensor(SHR[b], SHR[b], SP1, ALU.subtract).then_inc(sem("s5_hr"), 1)

            def s5_skip(st):
                label, i, half = f"s5y{st}", st // 2, slice(64 * (st % 2), 64 * (st % 2) + 64)
                dve.wait_ge(*fill_of(label))
                dve.scalar_tensor_tensor(out=EU[half, i, :], in0=EU[half, i, :], scalar=VEC[half, V_D + i:V_D + i + 1],
                                         in1=bank(label)[half, 0:L], op0=ALU.mult, op1=ALU.add).then_inc(emptied["v"], 1)

            dve.wait_ge(sem("rope_tab"), 1)
            cosb = lambda n: COSP.unsqueeze(1).to_broadcast([P, n, L])
            sinb = lambda n: SINP.unsqueeze(1).to_broadcast([P, n, L])
            for st in range(S5_STEPS):
                s5_step(st)
                if st:
                    s5_skip(st - 1)
                if 1 <= st < 5:
                    c = st - 1
                    rope(f"erope{c}", EQK[:, 2 * c:2 * c + 2, :], 2, cosb, sinb, EROT, "eroped", c + 1)
            s5_skip(S5_STEPS - 1)

            def gate_s5(qt):
                if qt == 0:
                    dve.wait_ge(*read_of("glu1"))
                    for m in range(4):
                        dve.tensor_tensor(HT[:, 4 + m, 0:L], HT[:, 4 + m, 0:L], EU[:, m, :], ALU.mult).then_inc(sem("s5_out"), 1)

            def finish_e(qt, o):
                dve.tensor_copy(HT[:, 0:4, qt * P:(qt + 1) * P], o).then_inc(emptied["v"], 1)

            attention("E", EPT, EOT, 0.125, False, finish_e, gate_s5)
            post_norm(1, MX, 0, 96)
            if stop <= 3:
                return

            def ffn(l, n, count):
                pre_norm(n, V_NFFN + 8 * l)
                for c in range(KF // 2):
                    dve.wait_ge(*fill_of(f"fu{l}.{c}.lat"))
                    ps = bank(f"fu{l}.{c}.lat")
                    dve.wait_ge(*read_of(f"fg{l}.{c}.lat"))
                    dve.tensor_tensor(FH[:, 2 * c:2 * c + 2, :], FSG[:, c % 2], ps[:, :].rearrange("p (m t) -> p m t", m=2), ALU.mult).then_inc(emptied["v"], 1)
                post_norm(n, FX, 1, count)

            ffn(0, 2, 96)
            if stop <= 4:
                return
            lam, sp = VEC[:, V_LAM:V_LAM + 8], SM[:, 216:224]
            dve.scalar_tensor_tensor(out=sp, in0=lam, scalar=-1.0, in1=lam, op0=ALU.mult, op1=ALU.max).then_inc(sem("lam_abs"), 1)
            pre_norm(3, V_NPRE + 8)
            dve.wait_ge(sem("lam_ln"), 1)
            link(dve.tensor_scalar(SM[:, 224:232], lam, -1.0, 0.0, ALU.mult, ALU.max))
            link(dve.tensor_tensor(sp, sp, SM[:, 224:232], ALU.add))
            link(dve.tensor_scalar(SM[:, 224:232], sp, 8.0, None, ALU.mult))
            dve.tensor_scalar(SM[:, 232:240], sp, -8.0, None, ALU.mult).then_inc(sem("rg_sp"), 1)
            link(dve.memset(RXB[:, :, 0:3], 0.0))
            for c in range(4):
                dve.wait_ge(*fill_of(f"rx{c}.lat"))
                dve.tensor_copy(RXB[:, 2 * c:2 * c + 2, 3:3 + L], two(bank(f"rx{c}.lat"), L)).then_inc(emptied["v"], 1)
            dve.wait_ge(*read_of("rx3.lat"))
            for t in range(8):
                wcol = lambda j: VEC[:, V_RCW + 8 * j + t:V_RCW + 8 * j + t + 1]
                link(dve.tensor_scalar(RXC[:, t, :], RXB[:, t, 0:L], wcol(0), VEC[:, V_RCB + t:V_RCB + t + 1], ALU.mult, ALU.add))
                for j in (1, 2, 3):
                    ins = dve.scalar_tensor_tensor(out=RXC[:, t, :], in0=RXB[:, t, j:j + L], scalar=wcol(j), in1=RXC[:, t, :],
                                                   op0=ALU.mult, op1=ALU.add)
                    if j < 3:
                        link(ins)
                ins.then_inc(sem("rg_conv"), 1)
            dve.wait_ge(*read_of("rgi3"))
            dve.wait_ge(sem("rg_conv"), 8)
            for t in range(8):
                dve.wait_ge(sem("rg_a"), t + 1)
                dve.tensor_tensor(RGI[:, t, :], RGI[:, t, :], RXC[:, t, :], ALU.mult)
                link(dve.tensor_tensor(RM[:, t, :], RA[:, t, :], RA[:, t, :], ALU.mult))
                dve.scalar_tensor_tensor(out=RM[:, t, :], in0=RM[:, t, :], scalar=1.0, in1=RTH[:, t, :],
                                         op0=ALU.add, op1=ALU.mult).then_inc(sem("rg_msq"), 1)
            dve.wait_ge(*read_of("rz3.lat"))
            for t in range(8):
                dve.wait_ge(sem("rg_mult"), t + 1)
                link(dve.tensor_tensor(RGI[:, t, :], RGI[:, t, :], RM[:, t, :], ALU.mult))
                link(dve.tensor_tensor_scan(RXC[:, t, :], RA[:, t, :], RGI[:, t, :], 0.0, ALU.mult, ALU.add))
                dve.tensor_tensor(RM[:, t, :], RXC[:, t, :], RZG[:, t, :], ALU.mult).then_inc(sem("rg_out"), 1)
            post_norm(3, MX, 0, 128)
            if stop <= 5:
                return
            ffn(1, 4, 128)

        @block.gpsimd
        def _(pool):
            PL = [SM[:, 352 + 12 * b:364 + 12 * b].rearrange("p (h c) -> p h c", h=HH) for b in range(2)]

            def key_args(st):
                b = st % 2
                pool.wait_ge(sem("hg_lf"), st + 1)
                pool.tensor_tensor(HK[b][:, :, :], HT_[b][:, :, :], HZ[b][:, :, :], ALU.subtract).then_inc(sem("hg_karg"), 1)

            def state_args(st):
                b, d = st % 2, STEPS[st][1]
                pool.wait_ge(sem("hg_sums"), st + 1)
                if d == 1:
                    pool.tensor_tensor(HP[b][:, :, :], HP[b][:, :, :], HT_[b][:, :, :], ALU.subtract).then_inc(sem("hg_excl"), 1)
                    pool.wait_ge(sem("hg_excl"), STEPS[st][0] + 1)
                pool.wait_ge(sem("hg_karg"), st + 1)
                n = 4 if d else 6
                dst = (HT_ if d else HZ)[b]
                for h in range(HH):
                    c3 = lambda ap: ap[:, h, 0:n * P].rearrange("p (c t) -> p c t", t=P)
                    last = pool.tensor_tensor(c3(dst), PL[b][:, h, 0:n].unsqueeze(2).to_broadcast([P, n, P]), c3(HP[b]), ALU.subtract)
                last.then_inc(sem("hg_arg"), 1)

            def level_args(g):
                st, li = divmod(g, 7)
                d, h2 = STEPS[st][1], LEVELS[li]
                if g >= 2:
                    pool.wait_ge(*fill_of(f"lv{(g - 2) // 7}.{(g - 2) % 7}"))
                n = L // (2 * h2)
                p4 = HP[st % 2][:, :, 0:L].rearrange("p g (b s h) -> p g b s h", s=2, h=h2)
                w4 = HW[g % 2][:, :, :].rearrange("p g (b s h) -> p g b s h", s=2, h=h2)
                ref = p4[:, :, :, 0, h2 - 1:h2] if d == 0 else p4[:, :, :, 1, 0:1]
                ref = ref.to_broadcast([P, HH, n, h2])
                pool.tensor_tensor(w4[:, :, :, 0, :], ref, p4[:, :, :, 0, :], ALU.subtract)
                pool.tensor_tensor(w4[:, :, :, 1, :], p4[:, :, :, 1, :], ref, ALU.subtract).then_inc(sem("hg_warg"), 1)

            if stop >= 2:
                key_args(0)
                state_args(0)
                for st in range(len(STEPS)):
                    level_args(7 * st)
                    level_args(7 * st + 1)
                    for i in range(7):
                        if i < 5:
                            level_args(7 * st + i + 2)
                        if st + 1 < len(STEPS) and i == 4:
                            key_args(st + 1)
                        if st + 1 < len(STEPS) and i == 5:
                            state_args(st + 1)

            def s5_tables():
                link = Chain(pool, "pool_chain").link
                tt = pool.tensor_tensor
                EC, ES = lambda k: SPR[:, 14 + k, :], lambda k: SPR[:, 23 + k, :]

                def doubled(R, I, T, c, s_, n):
                    lo, hi = slice(0, n), slice(n, 2 * n)
                    tt(R[:, :, hi], R[:, :, lo], c, ALU.mult)
                    tt(T, R[:, :, lo], s_, ALU.mult)
                    link(tt(I[:, :, hi], I[:, :, lo], s_, ALU.mult))
                    link(tt(R[:, :, hi], R[:, :, hi], I[:, :, hi], ALU.subtract))
                    link(tt(I[:, :, hi], I[:, :, lo], c, ALU.mult))
                    ins = tt(I[:, :, hi], I[:, :, hi], T, ALU.add)
                    if n < L // 2:
                        link(ins)
                    return ins

                pool.wait_ge(sem("s5_sc"), 1)
                pool.tensor_copy(EC(0), SPR[:, 7, :])
                link(pool.tensor_copy(ES(0), SPR[:, 6, :]))
                t1, t2 = SP3[:, 0, 0:16], SP3[:, 0, 16:32]
                for k in range(8):
                    tt(t1, EC(k), EC(k), ALU.mult)
                    tt(ES(k + 1), EC(k), ES(k), ALU.mult)
                    link(tt(t2, ES(k), ES(k), ALU.mult))
                    tt(EC(k + 1), t1, t2, ALU.subtract)
                    link(tt(ES(k + 1), ES(k + 1), ES(k + 1), ALU.add))
                pool.memset(SE0[0][:, :, 0:1], 1.0)
                link(pool.memset(SE0[1][:, :, 0:1], 0.0))
                for k in range(5):
                    n = 1 << k
                    at = lambda v: v.unsqueeze(2).to_broadcast([P, 16, n])
                    T = SP3[:, 0, 0:16 * n].rearrange("p (j t) -> p j t", j=16)
                    doubled(SE0[0], SE0[1], T, at(EC(k)), at(ES(k)), n)

                def tables(st):
                    b, js = st % 2, slice(2 * st, 2 * st + 2)
                    if st >= 2:
                        pool.wait_ge(sem("s5_hr"), st - 1)
                    pool.tensor_copy(SER[b][:, :, 0:32], SE0[0][:, js, :])
                    link(pool.tensor_copy(SEI[b][:, :, 0:32], SE0[1][:, js, :]))
                    for k in range(5, 9):
                        n = 1 << k
                        at = lambda v: v[:, js].unsqueeze(2).to_broadcast([P, 2, n])
                        last = doubled(SER[b], SEI[b], SP3[:, :, 0:n], at(EC(k)), at(ES(k)), n)
                    last.then_inc(sem("s5_tables"), 1)
                    pool.wait_ge(sem("s5_tables"), st + 1)

                tables(0)
                tables(1)
                for st in range(S5_STEPS):
                    b = st % 2
                    pool.wait_ge(sem("s5_sums"), st + 1)
                    if st >= 2:
                        pool.wait_ge(*fill_of(f"s5y{st - 2}"))
                    tt(SHI[b], SER[b], SBI[b], ALU.mult)
                    link(tt(SP3, SEI[b], SBR[b], ALU.mult))
                    tt(SHI[b], SHI[b], SP3, ALU.add).then_inc(sem("s5_hi"), 1)
                    pool.wait_ge(sem("s5_hi"), st + 1)
                    if st + 2 < S5_STEPS:
                        tables(st + 2)

            if stop >= 3:
                s5_tables()

            last = min(stop, 6)
            pool.wait_ge(sem(f"x{last}_ready"), 6 if last == 1 else 4)
            pool.dma_start(out[0].rearrange("(t p) n -> p t n", p=P), X[:, 0:TL, :]).then_inc(sem("out_written"), 16)
            pool.wait_ge(sem("out_written"), 16)
            if last <= 2:
                pool.wait_ge(sem("bc_in"), 64)


SHAPES = None


def kernel(**inputs):
    import numpy as _np
    import concourse.bacc as _bacc
    from concourse import mybir as _mybir
    from concourse.bass_utils import run_bass_kernel_spmd as _run

    nc = _bacc.Bacc("TRN2", target_bir_lowering=False, num_devices=1)
    arrays, aps = {}, {}
    for name, x in list(inputs.items()) + [("tables", make_tables())]:
        x = _np.ascontiguousarray(x)
        arrays[f"in_{name}"] = x
        aps[name] = nc.dram_tensor(f"in_{name}", x.shape, _mybir.dt.from_np(x.dtype), kind="ExternalInput").ap()
    out = nc.dram_tensor("out_0", (1, L, D), F32, kind="ExternalOutput").ap()
    program(nc, aps, out)
    r = _run(nc, [arrays], core_ids=[0])
    return r.results[0]["out_0"]
```

```python
from contextlib import ExitStack

import numpy as np

import concourse.bass as bass
from concourse import mybir

F32 = mybir.dt.float32
U32 = mybir.dt.uint32
I32 = mybir.dt.int32
ALU = mybir.AluOpType
ACT = mybir.ActivationFunctionType
AX = mybir.AxisListType

P = 128
D = 1024
KD = D // P
L = 512
LC = 256
TL = L // P
TC = LC // P
LT = L + LC
HEADS = 8
DH = 64
AW = HEADS * DH
NEG = -1e30
ALPHA = 4.0 ** 0.25
LN_EPS = 1e-5
RMS_EPS = 1e-6
FFN = 2816
KF = FFN // P
WC = 256
WSLOTS = 3
HH = 2
LEVELS = (64, 32, 16, 8, 4, 2, 1)
TWO_PI = 2.0 * np.pi
MAGIC = 12582912.0


def table_layout():
    sizes = [("ident", P), ("ones", P), ("win_lo", P), ("win_hi", P), ("dil", 1280),
             ("lv_f", 64 * len(LEVELS)), ("lv_b", 64 * len(LEVELS)), ("rot_ax", P), ("rot_pt", P),
             ("cos_ax", L), ("sin_ax", L), ("chunk", L), ("cols", 8)]
    at, out = 0, {}
    for name, n in sizes:
        out[name] = (at, at + n)
        at += n
    return out, at


def make_tables():
    lay, width = table_layout()
    t = np.zeros((P, width), np.float32)

    def put(name, a):
        t[:, lay[name][0]:lay[name][1]] = a

    i = np.arange(P)
    put("ident", np.eye(P))
    put("ones", 1.0)
    put("win_lo", np.where(i[None, :] >= i[:, None], 0.0, NEG))
    put("win_hi", np.where(i[None, :] <= i[:, None], 0.0, NEG))
    off = 0
    for qt in range(TL):
        q = qt * P + i[:, None]
        k = np.arange((qt + 1) * P)[None, :]
        d = q - k
        n = ((d >= 0) & (d <= 128)).astype(int) + ((d >= 0) & (d % 4 == 0)) + ((d >= 0) & (d % 16 == 0))
        b = np.where(n > 0, 8.0 * np.log(np.maximum(n, 1)), NEG)
        t[:, lay["dil"][0] + off:lay["dil"][0] + off + (qt + 1) * P] = b
        off += (qt + 1) * P
    for li, h in enumerate(LEVELS):
        right = np.array([c for c in range(P) if (c // h) % 2 == 1])
        left = np.array([c for c in range(P) if (c // h) % 2 == 0])
        f = (i[:, None] // (2 * h) == right[None, :] // (2 * h)) & ((i[:, None] // h) % 2 == 0)
        b = (i[:, None] // (2 * h) == left[None, :] // (2 * h)) & ((i[:, None] // h) % 2 == 1)
        t[:, lay["lv_f"][0] + 64 * li:lay["lv_f"][0] + 64 * li + 64] = f
        t[:, lay["lv_b"][0] + 64 * li:lay["lv_b"][0] + 64 * li + 64] = b

    def rotation(period, half, used):
        r = np.zeros((P, P), np.float32)
        for m in range(P):
            o = m % period
            if o < used:
                if o < half:
                    r[m + half, m] = -1.0
                else:
                    r[m - half, m] = 1.0
        return r

    put("rot_ax", rotation(32, 16, 32))
    put("rot_pt", rotation(64, 8, 16))
    freqs = (np.float32(10000.0) ** (-np.arange(16, dtype=np.float32) / np.float32(16))).astype(np.float32)
    tok = np.arange(L)
    for p in range(P):
        o = p % DH
        pos = (tok // 64 if o < 32 else tok % 64).astype(np.float32)
        ang = pos * freqs[o % 16]
        t[p, lay["cos_ax"][0]:lay["cos_ax"][1]] = np.cos(ang)
        t[p, lay["sin_ax"][0]:lay["sin_ax"][1]] = np.sin(ang)
    put("chunk", (np.arange(L) % P != 0).astype(np.float32)[None, :])
    inv = (np.float32(500000.0) ** -(np.arange(8, dtype=np.float32) * np.float32(2.0) / np.float32(16))).astype(np.float32)
    c0 = lay["cols"][0]
    for p in range(P):
        o = p % DH
        t[p, c0] = inv[o % 8] if o < 16 else 0.0
    t[:, c0 + 2] = (i // 16) % 2 == 0
    t[:, c0 + 3] = (i // 16) % 2 == 1
    t[:, c0 + 4] = i // DH == 0
    t[:, c0 + 5] = i // DH == 1
    return t


def program(nc, a, out, stop=99):
    lay, tw = table_layout()
    ctx = ExitStack()
    with ctx:
        sems = {}

        def sem(name):
            if name not in sems:
                sems[name] = ctx.enter_context(nc.semaphore(name))
            return sems[name]

        base = (nc.sbuf_base + 31) // 32 * 32
        arena = nc.alloc_sbuf_tensor_at("arena", [P, 53100], F32, offset=base)
        top = [0]

        def take_words(n):
            top[0] += n
            assert top[0] <= 53100, top[0]
            return top[0] - n

        def view(at, *dims):
            n = int(np.prod(dims))
            v = arena[:, at:at + n]
            if len(dims) == 2:
                v = v.rearrange("p (a b) -> p a b", a=dims[0])
            if len(dims) == 3:
                v = v.rearrange("p (a b c) -> p a b c", a=dims[0], b=dims[1])
            return v

        TAB = view(take_words(tw), tw)

        def tab(name, lo=0, hi=None):
            s, e = lay[name]
            return TAB[:, s + lo:(e if hi is None else s + hi)]

        IDENT, ONES = tab("ident"), tab("ones")
        VEC = view(take_words(256), 256)
        MOD = view(take_words(96), 2, 24, 2)
        SC = view(take_words(16), KD, 2)
        SM = view(take_words(512), 512)
        BC = view(take_words(2 * D), 2, D)
        gt_at = take_words(2 * D)
        GT = view(gt_at, 2, D)
        x_at = take_words(6 * D)
        X = view(x_at, 6, D)
        ht_at = take_words(KD * LT)
        HT = view(ht_at, KD, LT)
        wr_at = take_words(WSLOTS * KD * WC)
        WR = view(wr_at, WSLOTS, KD, WC)
        hi_at = take_words(2 * KD * WC)
        work = top[0]
        free = 53100 - work

        ring = [ctx.enter_context(nc.psum_tensor(f"ring{i}", [P, 1024], F32)) for i in range(3)]
        obank = [ctx.enter_context(nc.psum_tensor(f"obank{i}", [P, 512], F32)) for i in range(2)]

        filled = sem("psum_filled")
        emptied = {"v": sem("dve_emptied"), "a": sem("act_emptied")}
        units, order, by_engine = {}, [], {"v": 0, "a": 0}
        chunks = []
        wload = [sem(f"weights{i}") for i in range(WSLOTS)]
        wcount = [0] * WSLOTS
        wused = sem("weights_used")
        released = []

        w = work
        AQ = view(w, 4, LT)
        AKV = view(w + 3072, 2, LT)
        AGA = view(w + 4608, 4, LT)
        AGB = view(w + 7680, 4, LT)
        AU = view(w + 10752, 4, LT + 4)
        AVT = view(w + 13840, 6, P)
        APB = view(w + 14608, 2, 640)
        APT = view(w + 15888, 2, 640)
        AOT = view(w + 17168, 2, AW)
        ACV = view(w + 18192, 2, LT)
        ROT = view(w + 14608, 2, L)
        MR = view(w + 4096, 3, D)
        MOD_STEPS = (("rows", 0), ("rows", 1), ("turn", 0), ("rows", 2), ("turn", 1), ("turn", 2))
        DG = view(w + 14608, KD, P)
        VR = view(w, 2, P)
        ATMP = view(w, 4, WC)

        hg = [[view(w + 6144 * b + 1536 * k, HH, LT) for b in range(2)] for k in range(4)]
        HZ, HT_, HK, HP = hg
        HW = [view(w + 12288 + 1024 * b, HH, L) for b in range(2)]
        HQ = [view(w + 14336 + 1024 * b, HH, L) for b in range(2)]
        HI = [view(w + 16384 + 1536 * b, 6, HH * P) for b in range(2)]
        HSC = view(w + 19456, TL * HH, P)
        xc = x_at + 4 * D
        HS = view(xc, HH, P)
        HKT = [view(xc + 256 + 256 * b, HH, P) for b in range(2)]
        HDG = view(xc + 768, TL * HH, P)
        HO = view(hi_at, TL, D)
        CG = view(w, TL, D)
        HSQ = view(xc + 768, TL, WC)
        CTMP = view(w + 13312, TL, WC)
        GN = SM[:, 376:504]
        assert w + 20480 <= 53100, free
        STEPS = [(hb, d) for hb in range(HEADS // HH) for d in range(2)]
        rounds = {}
        EQK = view(w, 8, L)
        EV = view(w + 4096, TL, AW)
        EU = view(w + 6144, 4, L)
        EPB = view(w + 8192, 2, L)
        EPT = view(w + 9216, 2, L)
        EOT = view(w + 10240, 2, AW)
        EROT = view(w + 8192, 2, L)
        EPOS = view(w + 8192, L)
        COSP, SINP = tab("cos_ax"), tab("sin_ax")
        s5 = w + 11264
        buffers = lambda at: [view(at + 1024 * b, 2, L) for b in range(2)]
        SER, SEI = buffers(s5), buffers(s5 + 2048)
        SBR, SBI = buffers(s5 + 4096), buffers(s5 + 6144)
        SHR, SHI = buffers(gt_at), buffers(x_at + 4 * D)
        SBD = [view(hi_at + 512 * i, 4, P) for i in range(2)]
        SCD = [view(hi_at + 1024 + 512 * i, 4, P) for i in range(2)]
        SPR = view(hi_at + 2048, 32, 16)
        SE0 = [view(hi_at + 2560 + 512 * i, 16, 32) for i in range(2)]
        SROW = view(hi_at + 3584, P)
        SP1, SP2 = view(w + 9216, 2, L), view(w + 10240, 2, L)
        SP3 = view(w + 19456, 2, L)
        SBRAW = [view(s5 + 4096 + 256 * i, 16, 16) for i in range(2)]
        SBBL = [view(s5 + 4608 + 512 * i, 16, 32) for i in range(2)]
        SCRAW = [view(s5 + 5632 + 256 * i, 4, DH) for i in range(2)]
        SCEX = [view(s5 + 6144 + 512 * i, 4, P) for i in range(2)]
        S5_STEPS = 8
        assert w + 20480 <= 53100
        XN = view(s5, TL, D)
        MX = view(w, TL, D)
        def parts(name, at, *dims):
            return nc.alloc_sbuf_tensor_at(name, [P, *dims], mybir.dt.float32r, offset=base + 4 * at)

        LOW_BITS_OFF = -(1 << 13)
        W_HI = parts("weights_hi", hi_at, 2, KD, WC)
        W_LO = [parts(f"weights_lo{i}", wr_at + i * KD * WC, KD, WC) for i in range(WSLOTS)]
        WM = view(gt_at, KD, WC)
        X_HI = parts("input_hi", x_at + 4 * D, KD, L)
        X_LO = parts("input_lo", x_at + 4 * D + KD * L, KD, L)
        NT, NM = view(w, KD, L), view(w + 4096, KD, L)
        HALVES = ((0, 6), (6, KF // 2))
        F_HI = [parts(f"hidden_hi{i}", w + 2 * i * L, 2, L) for i in range(6)]
        F_LO = [parts(f"hidden_lo{i}", w + (12 + 2 * i) * L, 2, L) for i in range(6)]
        FX = view(w + 24 * L, TL, D)
        FM = view(w + 24 * L + TL * D, 2, L)
        FSG = view(w + 26 * L + TL * D, 2, 2, L)
        FG = view(w + 24 * L + TL * D, TL, D)
        assert w + 24 * L + 2 * TL * D <= 53100
        splits = []

        def ffn_steps(l):
            at = FIRST[l]
            for half, (c0, c1) in enumerate(HALVES):
                for c in range(c0, c1):
                    yield "pair", half, c, at
                    at += 2
                for c in range(4):
                    yield "down", half, c, at
                    at += 2

        made = {"masked": 0, "hi": 0, "lo": 0}
        split_chunks = []

        FIRST = (0, 2 * (KF // 2 + 8) + 8)

        def ffn_end(l):
            return FIRST[l] + 2 * (KF // 2 + 8)

        RG0, RG_END = ffn_end(0), FIRST[1]

        RXB = view(w, 8, L + 4)
        RZG = view(w + 4128, 8, L)
        RXC = view(w + 8224, 8, L)
        RA = view(w + 12320, 8, L)
        RGI = view(w + 16416, 8, L)
        RTH = view(w, 8, L)
        RM = RTH
        RA2 = (COSP, SINP)
        MX3, RJ, G3 = view(w + 8224, TL, D), view(w + 12320, TL, D), view(w + 4128, TL, D)

        class Chain:

            def __init__(self, eng, name):
                self.eng, self.sem, self.n = eng, sem(name), 0

            def link(self, ins):
                ins.then_inc(self.sem, 1)
                self.n += 1
                self.eng.wait_ge(self.sem, self.n)

        def read_of(label):
            _, e, k = units[label]
            return emptied[e], k

        def fill_of(label):
            return filled, units[label][0] + 1

        def bank(label):
            return ring[units[label][0] % 3]

        block = ctx.enter_context(nc.Block())

        V_C, V_CC, V_BADA, V_CONV, V_NPRE, V_NFFN = 0, 8, 16, 64, 76, 92
        V_D, V_RCW, V_RCB, V_BR, V_BI, V_LAM = 128, 132, 164, 172, 180, 188

        ROWS = [(V_C, a["c"].rearrange("o (r n) -> (o r) n", n=P), 8),
                (V_CC, a["c_ctx"].rearrange("(r n) -> r n", n=P), 8),
                (V_BADA, a["b_ada"].rearrange("l (r n) -> (l r) n", n=P), 48),
                (V_CONV, a["conv_ab"].rearrange("o j (r n) -> (o j r) n", n=P), 12),
                (V_NPRE, a["norm_mix_pre_2"].rearrange("l (r n) -> (l r) n", n=P), 16),
                (V_NFFN, a["norm_ffn_pre_2"].rearrange("l (r n) -> (l r) n", n=P), 16),
                (V_D, a["s5_d_2"].rearrange("o (r g) c -> (o r) (g c)", r=4), 4),
                (V_RCW, a["rg_conv_w_2"].rearrange("o j (r n) -> (o j r) n", n=P), 32),
                (V_RCB, a["rg_conv_b_2"].rearrange("o (r n) -> (o r) n", n=P), 8),
                (V_BR, a["rg_b_r_2"].rearrange("o (r n) -> (o r) n", n=P), 8),
                (V_BI, a["rg_b_i_2"].rearrange("o (r n) -> (o r) n", n=P), 8),
                (V_LAM, a["rg_lam_2"].rearrange("o (r n) -> (o r) n", n=P), 8)]

        def cols(wap, c0, n=WC, k0=0, kt=KD):
            return [(0, n, wap[k0 * P:(k0 + kt) * P, c0:c0 + n].rearrange("(k p) n -> p k n", p=P))]

        def att_blocks(kind, qt):
            if kind == "A":
                b = [(L, TL, None), (L + P, TL + 1, None)]
                if qt < TL:
                    if qt > 0:
                        b.append(((qt - 1) * P, qt - 1, tab("win_lo")))
                    b.append((qt * P, qt, None))
                    if qt < TL - 1:
                        b.append(((qt + 1) * P, qt + 1, tab("win_hi")))
                return b
            off = P * (qt * (qt + 1) // 2)
            return [(k * P, k, tab("dil", off + k * P, off + (k + 1) * P)) for k in range(qt + 1)]

        def att_events(n):
            for i in range(n + 2):
                if i < n:
                    yield "scores", i
                if 0 <= i - 1 < n:
                    yield "turn", i - 1
                if 0 <= i - 2:
                    yield "values", i - 2
                    if (i - 2) % HEADS == HEADS - 1:
                        yield "finish", (i - 2) // HEADS

        NT_ATT = {"A": TL + TC, "E": TL}

        def hg_seq(d):
            c, l = [TL, TL + 1], list(range(TL))
            return c + l if d == 0 else c[::-1] + l[::-1]

        def pos(ap, n, h, side):
            return ap.rearrange("p g (b s h) -> p g b s h", s=2, h=h)[:, :, :, side, :]

        @block.tensor
        def _(pe):
            def take(label, engine):
                n = len(order)
                if n >= 3:
                    e, k = units[order[n - 3]][1:]
                    pe.wait_ge(emptied[e], k)
                by_engine[engine] += 1
                units[label] = (n, engine, by_engine[engine])
                order.append(label)
                return ring[n % 3]

            def chunk(pieces, kt=KD):
                n = len(chunks)
                s = n % WSLOTS
                chunks.append((pieces, kt))
                wcount[s] += 16 * len(pieces)
                pe.wait_ge(wload[s], wcount[s])
                return WR[:, s]

            def used_with_unit():
                released.append((filled, len(order)))

            def used_now(last):
                last.then_inc(wused, 1)
                released.append((wused, 1 + sum(x is wused for x, _ in released)))

            def gemm_f(name, wt, c0, n, ctx_on, eng, lat_on=True, pieces=None, lhs=None, rhs=HT):
                wv = chunk(pieces or cols(wt, c0, n))
                lhs = lhs or (lambda wv, k, m: wv[:, k, m * P:(m + 1) * P])
                mts = n // P
                if lat_on:
                    ps = take(name + ".lat", eng)
                    for m in range(mts):
                        for k in range(KD):
                            last = pe.matmul(ps[:, m * L:(m + 1) * L], lhs(wv, k, m), rhs[:, k, 0:L],
                                             start=k == 0, stop=k == KD - 1)
                    last.then_inc(filled, 1)
                if ctx_on:
                    ps = take(name + ".ctx", eng)
                    for m in range(mts):
                        for k in range(KD):
                            last = pe.matmul(ps[:, m * LC:(m + 1) * LC], lhs(wv, k, m), rhs[:, k, L:LT],
                                             start=k == 0, stop=k == KD - 1)
                    last.then_inc(filled, 1)
                used_with_unit()

            def gemm_t(name, wt, c0, tiles, eng, act=HT, kts=(KD,)):
                groups = [g for g in (range(0, 4), range(4, 6)) if g.start < tiles]
                if len(kts) > 1:
                    ps = take(name + ".t0", eng)
                    k0 = 0
                    for ci, kt in enumerate(kts):
                        wv = chunk(cols(wt, c0, WC, k0, kt), kt)
                        for t in range(4):
                            for k in range(kt):
                                last = pe.matmul(ps[:, t * WC:(t + 1) * WC], act[:, k0 + k, t * P:(t + 1) * P],
                                                 wv[:, k, :], start=ci == 0 and k == 0 and t % 2 == 0,
                                                 stop=ci == len(kts) - 1 and k == kt - 1,
                                                 skip_group_check=True)
                        k0 += kt
                        if ci < len(kts) - 1:
                            used_now(last)
                    last.then_inc(filled, 1)
                    used_with_unit()
                    return
                wv = chunk(cols(wt, c0))
                for gi, g in enumerate(groups):
                    ps = take(f"{name}.t{gi}", eng)
                    for j, t in enumerate(g):
                        for k in range(KD):
                            last = pe.matmul(ps[:, j * WC:(j + 1) * WC], act[:, k, t * P:(t + 1) * P],
                                             wv[:, k, :], start=k == 0, stop=k == KD - 1)
                    last.then_inc(filled, 1)
                used_with_unit()

            def turn_tiles(name, src, tiles, eng, at=None):
                for t in tiles:
                    ps = take(f"{name}{t}", eng)
                    for k in range(KD):
                        x = at(t, k) if at else src[:, t, k * P:(k + 1) * P]
                        last = pe.transpose(ps[:, k * P:(k + 1) * P], x, IDENT)
                    last.then_inc(filled, 1)

            def mod_layer(l):
                for what, g in MOD_STEPS:
                    ps = take(f"mod_{what}{l}.{g}", "v")
                    if what == "turn":
                        pe.wait_ge(*read_of(f"mod_rows{l}.{g}"))
                        for m in range(KD):
                            last = pe.transpose(ps[:, 2 * m:2 * m + 2], MR[0:2, g, m * P:(m + 1) * P], IDENT[0:2, 0:2])
                        last.then_inc(filled, 1)
                        continue
                    for ci in range(4):
                        wv = chunk(cols(a["w_ada"][l], g * D + ci * WC))
                        for k in range(KD):
                            last = pe.matmul(ps[0:2, ci * WC:(ci + 1) * WC], SC[:, k, :], wv[:, k, :],
                                             start=k == 0, stop=k == KD - 1)
                        if ci < 3:
                            used_now(last)
                    last.then_inc(filled, 1)
                    used_with_unit()

            def gate_rows(l, n):
                for j in range(n):
                    pe.wait_ge(sem(f"gate_diag{l}"), j + 1)
                    ps = take(f"gate{l}.{j}", "a")
                    for h in range(2):
                        last = pe.matmul(ps[:, h * 512:(h + 1) * 512], ONES, DG[:, 4 * h:4 * h + 4, :],
                                         start=True, stop=True)
                    last.then_inc(filled, 1)

            def attention(kind, q_of, k_of, v_of, PB, PT, OT, width):
                n = NT_ATT[kind] * HEADS
                for what, i in att_events(n):
                    qt, h = divmod(i, HEADS)
                    if what == "scores":
                        blocks = att_blocks(kind, qt)
                        ps = take(f"{kind}s{i}", "a")
                        for b, (c0, _, mask) in enumerate(blocks):
                            o = ps[:, b * P:(b + 1) * P]
                            last = pe.matmul(o, q_of(h, qt), k_of(h, c0), start=True, stop=mask is None)
                            if mask is not None:
                                last = pe.matmul(o, IDENT, mask, start=False, stop=True)
                        last.then_inc(filled, 1)
                    elif what == "turn":
                        pe.wait_ge(*read_of(f"{kind}s{i}"))
                        ps = take(f"{kind}t{i}", "v" if i % 2 else "a")
                        for b in range(len(att_blocks(kind, qt))):
                            last = pe.transpose(ps[:, b * P:(b + 1) * P], PB[:, i % 2, b * P:(b + 1) * P], IDENT)
                        last.then_inc(filled, 1)
                    elif what == "values":
                        pe.wait_ge(*read_of(f"{kind}t{i}"))
                        if h == 0 and qt >= 2:
                            pe.wait_ge(sem(f"{kind}_normed"), qt - 1)
                        blocks = att_blocks(kind, qt)
                        for b, (_, vt, _) in enumerate(blocks):
                            last = pe.matmul(obank[qt % 2][:, h * DH:(h + 1) * DH], PT[:, i % 2, b * P:(b + 1) * P],
                                             v_of(h, vt), start=b == 0, stop=b == len(blocks) - 1)
                        last.then_inc(sem(f"{kind}_values"), 1)
                    else:
                        qt = i
                        pe.wait_ge(sem(f"{kind}_normed"), qt + 1)
                        ps = take(f"{kind}o{qt}", "v")
                        for f in range(4):
                            last = pe.transpose(ps[:, f * P:(f + 1) * P], OT[:, qt % 2, f * P:(f + 1) * P], IDENT)
                        last.then_inc(filled, 1)

            pe.wait_ge(sem("tables_in"), 16)
            pe.wait_ge(sem("rows_in"), 16 * len(ROWS))
            ps = take("vec", "v")
            pe.transpose(ps[:, 0:108], VR[0:108, 0, :], IDENT[0:108, 0:108])
            pe.transpose(ps[:, 512:512 + 68], VR[0:68, 1, :], IDENT[0:68, 0:68]).then_inc(filled, 1)
            pe.wait_ge(sem("silu_c"), 1)
            mod_layer(0)
            gate_rows(0, 2)
            pe.wait_ge(sem("x_in"), 32)
            turn_tiles("h0.", X, range(6), "v")
            pe.wait_ge(*read_of("h0.5"))
            wab = a["w_in_ab"][0]
            for c in range(2):
                gemm_f(f"q{c}", wab, 0, WC, True, "a",
                       pieces=[(m * P + g * DH, DH, wab[:, (4 * g + 2 * c + m) * DH:(4 * g + 2 * c + m + 1) * DH]
                                .rearrange("(k p) n -> p k n", p=P)) for m in range(2) for g in range(2)])
            gemm_f("kv", wab, 512, WC, True, "a")
            for nm, c0, eng in (("ga", 768, "a"), ("gb", 2816, "a"), ("bg", 1792, "v"), ("xb", 1280, "v"), ("cg", 2304, "v")):
                for c in range(2):
                    gemm_f(f"{nm}{c}", wab, c0 + c * WC, WC, True, eng)
            pe.wait_ge(*read_of("kv.ctx"))
            for c, tl in enumerate(([(AQ, 0), (AQ, 1)], [(AQ, 2), (AQ, 3)], [(AKV, 0)])):
                ps = take(f"rope{c}", "v")
                for j, (src, i) in enumerate(tl):
                    last = pe.matmul(ps[:, j * L:(j + 1) * L], tab("rot_ax"), src[:, i, 0:L], start=True, stop=True)
                last.then_inc(filled, 1)
            ps = take("vtok", "a")
            for t in range(6):
                last = pe.transpose(ps[:, t * P:(t + 1) * P], AKV[:, 1, t * P:(t + 1) * P], IDENT)
            last.then_inc(filled, 1)
            pe.wait_ge(*read_of("vtok"))
            pe.wait_ge(sem("roped"), 3)
            attention("A", lambda h, qt: AQ[64 * (h // 4):64 * (h // 4) + 64, h % 4, qt * P:(qt + 1) * P],
                      lambda h, c0: AKV[64 * (h // 4):64 * (h // 4) + 64, 0, c0:c0 + P],
                      lambda h, vt: AVT[:, vt, 64 * (h // 4):64 * (h // 4) + 64], APB, APT, AOT, 640)
            pe.wait_ge(*read_of("Ao5"))
            pe.wait_ge(sem("conv"), 8)
            for c in range(4):
                gemm_t(f"y0.{c}", a["w_out_ab"][0], c * WC, 6, "v")
            if stop <= 1:
                return
            mod_layer(1)
            gate_rows(1, 1)
            pe.wait_ge(sem("x1_ready"), 6)
            turn_tiles("h1.", X, range(6), "v")
            pe.wait_ge(*read_of("h1.5"))
            wc = a["w_in_c"][0]

            def product(kind, key, wv, part):
                label = f"c{kind}{key}.{part}"
                ps = take(label, "v" if kind == "z" else "a")
                if kind in "zq":
                    if part < 2:
                        for k in range(KD):
                            last = pe.matmul(ps[:, 0:L], wv[:, k, part * P:(part + 1) * P], HT[:, k, 0:L],
                                             start=k == 0, stop=k == KD - 1)
                    else:
                        for m in range(HH):
                            for k in range(KD):
                                last = pe.matmul(ps[:, m * LC:(m + 1) * LC], wv[:, k, m * P:(m + 1) * P], HT[:, k, L:LT],
                                                 start=k == 0, stop=k == KD - 1)
                else:
                    for j in range(2):
                        t = 2 * part + j
                        for k in range(KD):
                            last = pe.matmul(ps[:, j * WC:(j + 1) * WC], HT[:, k, t * P:(t + 1) * P], wv[:, k, :],
                                             start=k == 0, stop=k == KD - 1)
                last.then_inc(filled, 1)
                return (kind, key, part, label)

            def products(st):
                if st == len(STEPS):
                    for c in range(4):
                        wv = chunk(cols(wc, 4096 + c * WC))
                        for g in range(2):
                            yield product("g", c, wv, g)
                        used_with_unit()
                    return
                hb, d = STEPS[st]
                wv = chunk(cols(wc, 1024 * (1 + d) + hb * WC))
                for part in range(3):
                    yield product("z", st, wv, part)
                used_with_unit()
                if d == 0:
                    wv = chunk(cols(wc, hb * WC))
                    for part in range(2):
                        yield product("q", hb, wv, part)
                    used_with_unit()
                    wv = chunk(cols(wc, 3072 + hb * WC))
                    for part in range(3):
                        yield product("i", hb, wv, part)
                    used_with_unit()

            rounds[-1, 0] = list(products(0))
            for st, (hb, d) in enumerate(STEPS):
                b, q = st % 2, hb % 2
                K_, Q_, I_ = HK[b], HQ[q], HI[q]
                coming = products(st + 1)
                pe.wait_ge(sem("hg_k"), st + 1)
                pe.wait_ge(*read_of(f"cq{hb}.1"))
                ps = take(f"dg{st}", "v")
                for j in range(TL * HH):
                    ch, h = divmod(j, HH)
                    last = pe.matmul(ps[:, j * P:(j + 1) * P], K_[:, h, ch * P:(ch + 1) * P],
                                     Q_[:, h, ch * P:(ch + 1) * P], start=True, stop=True)
                last.then_inc(filled, 1)
                pe.wait_ge(sem("hg_ks"), st + 1)
                pe.wait_ge(sem("hg_qi"), st + 1)
                pe.wait_ge(*read_of(f"ci{hb}.2"))
                seq = hg_seq(d)
                for i in range(7):
                    ch = seq[i] if i < 6 else None
                    if i < 6 and ch < TL:
                        pe.wait_ge(*read_of(f"su{st}.{i - 1}"))
                        ps = take(f"oi{st}.{i}", "v")
                        for h in range(HH):
                            last = pe.matmul(ps[:, h * P:(h + 1) * P], HT_[b][:, h, ch * P:(ch + 1) * P], HS[:, h, :],
                                             start=True, stop=True)
                        last.then_inc(filled, 1)
                    if i < 5:
                        ps = take(f"kt{st}.{i}", "a")
                        for h in range(HH):
                            last = pe.transpose(ps[:, h * P:(h + 1) * P], HZ[b][:, h, ch * P:(ch + 1) * P], IDENT)
                        last.then_inc(filled, 1)
                    pe.wait_ge(sem("hg_w"), 7 * st + i + 1)
                    ps = take(f"lv{st}.{i}", "v")
                    W = HW[(7 * st + i) % 2]
                    for j in range(TL * HH):
                        c4, h = divmod(j, HH)
                        wt = W[:, h, c4 * P:(c4 + 1) * P]
                        rv = wt.rearrange("p (b s h) -> p b s h", s=2, h=LEVELS[i])
                        last = pe.matmul(ps[:, j * 64:(j + 1) * 64], wt, rv[:, :, 1 - d, :], start=True, stop=True)
                    last.then_inc(filled, 1)
                    done = next(coming, None)
                    rounds[st, i] = [done] if done else []
                    if i < 5:
                        pe.wait_ge(*read_of(f"kt{st}.{i}"))
                        ps = take(f"su{st}.{i}", "v")
                        for h in range(HH):
                            last = pe.matmul(ps[:, h * P:(h + 1) * P], HKT[i % 2][:, h, :], I_[:, ch, h * P:(h + 1) * P],
                                             start=True, stop=True)
                        last.then_inc(filled, 1)
                rounds[st, 7] = list(coming)
                if d == 1:
                    pe.wait_ge(*read_of(f"lv{st}.6"))
                    ps = take(f"oo{hb}", "v")
                    for j in range(TL * HH):
                        ch, h = divmod(j, HH)
                        last = pe.matmul(ps[:, j * P:(j + 1) * P], HSC[:, j, :], I_[:, ch, h * P:(h + 1) * P],
                                         start=True, stop=True)
                    last.then_inc(filled, 1)
            for t in range(TL):
                pe.wait_ge(sem("c_y"), t + 1)
                turn_tiles("cy", HO, (t,), "a")
            pe.wait_ge(*read_of("cy3"))
            for c in range(4):
                gemm_t(f"y1.{c}", a["w_out_c"][0], c * WC, 4, "v")
            if stop <= 2:
                return
            def pre_norm(n, eng="v"):
                for t in range(TL):
                    pe.wait_ge(sem("xn_ready"), 4 * (n - 1) + t + 1)
                    turn_tiles(f"n{n}.", XN, (t,), eng)
                pe.wait_ge(*read_of(f"n{n}.3"))

            pre_norm(1)
            we = a["ev_w_in_2"][0]
            def s5_input(st):
                for jj in range(2):
                    j = 2 * st + jj
                    at = 32 * (j % 4)
                    ps = take(f"bu{j}", "v")
                    for k in range(2):
                        last = pe.matmul(ps[:, k * L:(k + 1) * L], SBD[k][at:at + 32, j // 4, :], EU[at:at + 32, j // 4, :],
                                         start=True, stop=True, tile_position=(at, 0))
                    last.then_inc(filled, 1)

            def s5_output(st):
                pe.wait_ge(sem("s5_hr"), st + 1)
                pe.wait_ge(sem("s5_hi"), st + 1)
                ps = take(f"s5y{st}", "v")
                for jj in range(2):
                    at = 32 * ((2 * st + jj) % 4)
                    for k, H in enumerate((SHR, SHI)):
                        last = pe.matmul(ps[at:at + 32, 0:L], SCD[k][:, st // 2, at:at + 32], H[st % 2][:, jj, :],
                                         start=k == 0, stop=k == 1, tile_position=(0, at))
                last.then_inc(filled, 1)

            gemm_f("eu0", we, 3 * AW, WC, False, "a")
            pe.wait_ge(sem("s5_rows_in"), 32)
            pe.wait_ge(sem("s5_dt_rows"), 1)
            ps = take("s5rows", "v")
            pe.transpose(ps[:, 0:48], SROW[0:48, :], IDENT[0:48, 0:48]).then_inc(filled, 1)
            gemm_f("eu1", we, 3 * AW + WC, WC, False, "a")
            pe.wait_ge(sem("s5_cexp"), 1)
            ps = take("s5c", "v")
            for k in range(2):
                for i in range(4):
                    last = pe.transpose(ps[:, (4 * k + i) * P:(4 * k + i + 1) * P], SCEX[k][:, i, :], IDENT)
            last.then_inc(filled, 1)
            pe.wait_ge(sem("s5_bblk"), 1)
            ps = take("s5b", "v")
            for k in range(2):
                for i in range(4):
                    last = pe.transpose(ps[:, (4 * k + i) * P:(4 * k + i + 1) * P],
                                        SBBL[k][:, 4 * i:4 * i + 4, :].rearrange("p j c -> p (j c)"), IDENT)
            last.then_inc(filled, 1)
            pe.wait_ge(*read_of("s5b"))
            pe.wait_ge(*read_of("eu1.lat"))
            for st in range(S5_STEPS):
                s5_input(st)
                if st < 4:
                    gemm_f(f"eqk{st}", we, st * WC, WC, False, "a")
                elif st < 6:
                    gemm_t(f"ev{st - 4}", we, 2 * AW + (st - 4) * WC, TL, "a")
                if st:
                    s5_output(st - 1)
                if 1 <= st < 5:
                    c = st - 1
                    pe.wait_ge(*read_of(f"eqk{c}.lat"))
                    ps = take(f"erope{c}", "v")
                    for j in range(2):
                        last = pe.matmul(ps[:, j * L:(j + 1) * L], tab("rot_pt"), EQK[:, 2 * c + j, :], start=True, stop=True)
                    last.then_inc(filled, 1)
            s5_output(S5_STEPS - 1)
            pe.wait_ge(sem("s5_gelu"), 4)
            for c in range(2):
                wv = chunk(cols(a["s5_w_glu_2"][0], c * WC, WC, 0, 4), 4)
                ps = take(f"glu{c}", "a")
                for m in range(2):
                    for k in range(4):
                        last = pe.matmul(ps[:, m * L:(m + 1) * L], wv[:, k, m * P:(m + 1) * P], HT[:, 4 + k, 0:L],
                                         start=k == 0, stop=k == 3)
                last.then_inc(filled, 1)
                used_with_unit()
            pe.wait_ge(sem("eroped"), 4)
            pe.wait_ge(*read_of("ev1.t0"))
            attention("E", lambda h, qt: EQK[64 * (h % 2):64 * (h % 2) + 64, h // 2, qt * P:(qt + 1) * P],
                      lambda h, c0: EQK[64 * (h % 2):64 * (h % 2) + 64, 4 + h // 2, c0:c0 + P],
                      lambda h, vt: EV[:, vt, h * DH:(h + 1) * DH], EPB, EPT, EOT, L)
            pe.wait_ge(*read_of("Eo3"))
            pe.wait_ge(sem("s5_out"), 4)
            for c in range(4):
                gemm_t(f"em{c}", a["ev_w_out_2"][0], c * WC, TL, "a")
            if stop <= 3:
                return

            def split_chunk(wt, c0, k0, kt):
                chunk(cols(wt, c0, WC, k0, kt), kt)
                n = len(chunks) - 1
                split_chunks.append(n)
                splits.append((n % WSLOTS, kt, wload[n % WSLOTS], wcount[n % WSLOTS]))
                pe.wait_ge(sem("w_hi"), len(splits))
                pe.wait_ge(sem("w_lo"), len(splits))
                return W_HI[:, (len(splits) - 1) % 2], W_LO[n % WSLOTS]

            def from_parts(label, eng, hi, lo):
                ps = take(label, eng)
                for m in range(2):
                    ms = slice(m * P, (m + 1) * P)
                    for k in range(KD):
                        o = ps[:, m * L:(m + 1) * L]
                        pe.matmul(o, hi[:, k, ms], X_HI[:, k, :], start=k == 0, stop=False)
                        pe.matmul(o, hi[:, k, ms], X_LO[:, k, :], start=False, stop=False)
                        last = pe.matmul(o, lo[:, k, ms], X_HI[:, k, :], start=False, stop=k == KD - 1)
                last.then_inc(filled, 1)
                used_with_unit()

            def ffn(l, n):
                for t in range(TL):
                    pe.wait_ge(sem("xn_ready"), 4 * (n - 1) + t + 1)
                    turn_tiles(f"n{n}.", FX, (t,), "v")
                pe.wait_ge(sem("x_hi"), TL * (2 * l + 1))
                pe.wait_ge(sem("x_lo"), TL * (2 * l + 1))
                for what, half, c, _ in ffn_steps(l):
                    c0, c1 = HALVES[half]
                    if what == "pair":
                        for nm, wt, eng in (("fg", "ffn_w_gate_2", "a"), ("fu", "ffn_w_up_2", "v")):
                            hi, lo = split_chunk(a[wt][l], c * WC, 0, KD)
                            from_parts(f"{nm}{l}.{c}", eng, hi, lo)
                        continue
                    if c == 0:
                        pe.wait_ge(sem("f_hi"), l * (KF // 2) + c1)
                        pe.wait_ge(sem("f_lo"), l * (KF // 2) + c1)
                    kts = (8, 2 * (c1 - c0) - 8)
                    ps = take(f"fm{l}{half}{c}", "v" if half else "a")
                    for ci, kt in enumerate(kts):
                        hi, lo = split_chunk(a["ffn_w_down_2"][l], c * WC, 2 * c0 + 8 * ci, kt)
                        for t in range(TL):
                            o = ps[:, t * WC:(t + 1) * WC]
                            ts = slice(t * P, (t + 1) * P)
                            for k in range(kt):
                                f = 8 * ci + k
                                end = ci == 1 and k == kt - 1
                                pe.matmul(o, F_HI[f // 2][:, f % 2, ts], hi[:, k, :], start=ci == 0 and k == 0 and t % 2 == 0, stop=False,
                                          skip_group_check=True)
                                pe.matmul(o, F_HI[f // 2][:, f % 2, ts], lo[:, k, :], start=False, stop=False, skip_group_check=True)
                                last = pe.matmul(o, F_LO[f // 2][:, f % 2, ts], hi[:, k, :], start=False, stop=end, skip_group_check=True)
                        if ci == 0:
                            used_now(last)
                    last.then_inc(filled, 1)
                    used_with_unit()

            ffn(0, 2)
            if stop <= 4:
                return
            pre_norm(3)
            pe.wait_ge(sem("x_hi"), 2 * TL)
            pe.wait_ge(sem("x_lo"), 2 * TL)
            for c in range(4):
                from_parts(f"rx{c}", "v", *split_chunk(a["od_w_in_2"][0], c * WC, 0, KD))
            from_parts("rz0", "a", *split_chunk(a["od_w_in_2"][0], D, 0, KD))
            pe.wait_ge(sem("rg_conv"), 8)
            for nm, wt in (("r", a["rg_w_r_2"][0]), ("i", a["rg_w_i_2"][0])):
                wv = chunk([(0, WC, wt.rearrange("h (k p) j -> p (h k) j", p=P))])
                for h in range(4):
                    ps = take(f"rg{nm}{h}", "a")
                    for m in range(2):
                        for k in range(2):
                            last = pe.matmul(ps[:, m * L:(m + 1) * L], wv[:, 2 * h + k, m * P:(m + 1) * P],
                                             RXC[:, 2 * h + k, :], start=k == 0, stop=k == 1)
                    last.then_inc(filled, 1)
                used_with_unit()
            for c in range(1, 4):
                from_parts(f"rz{c}", "a", *split_chunk(a["od_w_in_2"][0], D + c * WC, 0, KD))
            pe.wait_ge(sem("rg_out"), 8)
            for c in range(4):
                gemm_t(f"om{c}", a["od_w_out_2"][0], c * WC, TL, "a", RM)
            if stop <= 5:
                return
            ffn(1, 4)

        @block.sync
        def _(sp):
            sp.dma_start(TAB[:, :], a["tables"]).then_inc(sem("tables_in"), 16)
            for c0, rows, n in ROWS:
                r = c0 % P
                sp.dma_start(VR[r:r + n, c0 // P, :], rows).then_inc(sem("rows_in"), 16)
            for n, (pieces, kt) in enumerate(chunks):
                if n == 4:
                    sp.dma_start(X[:, 0:TL, :], a["x"][0].rearrange("(t p) n -> p t n", p=P)).then_inc(sem("x_in"), 16)
                    sp.dma_start(X[:, TL:6, :], a["ctx"][0].rearrange("(t p) n -> p t n", p=P)).then_inc(sem("x_in"), 16)
                if n >= WSLOTS:
                    sp.wait_ge(*released[n - WSLOTS])
                for c0, m, src in pieces:
                    sp.dma_start(WR[:, n % WSLOTS, 0:kt, c0:c0 + m], src).then_inc(wload[n % WSLOTS], 16)

        @block.scalar
        def _(act):
            ch_ = Chain(act, "act_chain")
            link = ch_.link

            def pair(label, dst, c, ctx_, func=ACT.Copy):
                n, t0 = (LC, L) if ctx_ else (L, 0)
                act.wait_ge(*fill_of(label))
                act.activation(dst[:, 2 * c:2 * c + 2, t0:t0 + n], bank(label)[:, 0:2 * n].rearrange("p (m t) -> p m t", m=2),
                               func).then_inc(emptied["a"], 1)

            def bcast_row(dst, src):
                return act.dma_start(dst, src.partition_broadcast(P))

            bcast_row(BC[:, 0, :], a["ln_g"][0]).then_inc(sem("bc_in"), 16)
            bcast_row(BC[:, 1, :], a["ln_b"][0]).then_inc(sem("bc_in"), 16)
            bcast_row(SM[:, 0:8], a["sink_ab"][0]).then_inc(sem("sink_in"), 16)
            act.wait_ge(*read_of("vec"))
            for j, c0 in enumerate((V_C, V_CC)):
                last = act.activation(SC[:, :, j], VEC[:, c0:c0 + 8], ACT.Silu)
                link(last) if j == 0 else None
            last.then_inc(sem("silu_c"), 1)
            for j in range(2):
                act.wait_ge(*fill_of(f"gate0.{j}"))
                ps = bank(f"gate0.{j}")
                act.activation(GT[:, j, :], ps[:, :], ACT.Copy).then_inc(emptied["a"], 1)
            for c in range(2):
                for x in (0, 1):
                    pair(f"q{c}" + (".lat", ".ctx")[x], AQ, c, x)
            for x in (0, 1):
                pair("kv" + (".lat", ".ctx")[x], AKV, 0, x)
            for nm, dst in (("ga", AGA), ("gb", AGB)):
                for c in range(2):
                    for x in (0, 1):
                        pair(f"{nm}{c}" + (".lat", ".ctx")[x], dst, c, x, ACT.Silu)
            act.wait_ge(*fill_of("vtok"))
            act.activation(AVT[:, :, :], ring[units["vtok"][0] % 3][:, 0:6 * P].rearrange("p (t c) -> p t c", t=6), ACT.Copy).then_inc(emptied["a"], 1)

            def attention(kind, PB, PT, scale, sink):
                n = NT_ATT[kind] * HEADS
                for what, i in att_events(n):
                    qt, h = divmod(i, HEADS)
                    if what == "scores":
                        nb = len(att_blocks(kind, qt))
                        act.wait_ge(*fill_of(f"{kind}s{i}"))
                        ps = bank(f"{kind}s{i}")
                        act.wait_ge(sem(f"{kind}_max"), i + 1)
                        if i >= 2:
                            act.wait_ge(*fill_of(f"{kind}t{i - 2}"))
                        col = 32 + 16 * (qt % 2) + h
                        if h == 0 and qt >= 2:
                            act.wait_ge(sem(f"{kind}_normed"), qt - 1)
                        ins = act.activation(PB[:, i % 2, 0:nb * P], ps[:, 0:nb * P], ACT.Exp,
                                             bias=SM[:, col:col + 1], scale=scale,
                                             accum_out=SM[:, col + 8:col + 9])
                        ins.then_inc(emptied["a"], 1)
                        if h == HEADS - 1 and sink:
                            act.wait_ge(sem(f"{kind}_sinkarg"), qt + 1)
                            s0 = 64 + 8 * (qt % 2)
                            act.activation(SM[:, s0:s0 + 8], SM[:, s0:s0 + 8], ACT.Exp).then_inc(sem(f"{kind}_sink"), 1)
                    elif what == "turn" and i % 2 == 0:
                        nb = len(att_blocks(kind, qt))
                        act.wait_ge(*fill_of(f"{kind}t{i}"))
                        ps = bank(f"{kind}t{i}")
                        if i >= 2:
                            act.wait_ge(sem(f"{kind}_values"), i - 1)
                        act.activation(PT[:, i % 2, 0:nb * P], ps[:, 0:nb * P], ACT.Copy).then_inc(emptied["a"], 1)

            attention("A", APB, APT, 0.125, True)

            def ln_root(k, tiles):
                act.wait_ge(sem("ln_var"), k)
                act.activation(SM[:, 96:96 + tiles], SM[:, 96:96 + tiles], ACT.Sqrt).then_inc(sem("ln_root"), 1)

            ln_root(1, 6)
            act.wait_ge(sem("x1_ready"), 6)
            bcast_row(BC[:, 0, :], a["ln_g"][1]).then_inc(sem("bc_in"), 16)
            bcast_row(BC[:, 1, :], a["ln_b"][1]).then_inc(sem("bc_in"), 16)
            if stop <= 1:
                return
            bcast_row(GN, a["gnorm_c"][0]).then_inc(sem("gn_in"), 16)
            act.wait_ge(*fill_of("gate1.0"))
            ps = bank("gate1.0")
            act.activation(GT[:, 0, :], ps[:, :], ACT.Copy).then_inc(emptied["a"], 1)

            def take_products(key):
                for kind, k, part, label in rounds[key]:
                    if kind == "z":
                        continue
                    act.wait_ge(*fill_of(label))
                    two = bank(label)[:, 0:512].rearrange("p (t c) -> p t c", t=2)
                    if kind == "q":
                        act.activation(HQ[k % 2][:, part, :], bank(label)[:, 0:L], ACT.Silu).then_inc(emptied["a"], 1)
                    elif kind == "i":
                        act.activation(HI[k % 2][:, 2 * part:2 * part + 2, :], two, ACT.Copy).then_inc(emptied["a"], 1)
                    else:
                        act.activation(CG[:, 2 * part:2 * part + 2, k * WC:(k + 1) * WC], two, ACT.Silu).then_inc(emptied["a"], 1)

            DEC = [SM[:, 128 + 12 * b:140 + 12 * b] for b in range(2)]

            def log1p_exp(st):
                t = HT_[st % 2]
                act.wait_ge(sem("hg_abs"), st + 1)
                link(act.activation(t[:, :, :], t[:, :, :], ACT.Exp, scale=-1.0))
                act.activation(t[:, :, :], t[:, :, :], ACT.Ln, bias=ONES[:, 0:1]).then_inc(sem("hg_ln"), 1)

            def keys(st):
                act.wait_ge(sem("hg_karg"), st + 1)
                k = HK[st % 2]
                act.activation(k[:, :, :], k[:, :, :], ACT.Exp).then_inc(sem("hg_k"), 1)

            def state_factors(st):
                b, d = st % 2, STEPS[st][1]
                act.wait_ge(sem("hg_arg"), st + 1)
                act.activation(DEC[b], DEC[b], ACT.Exp)
                act.activation(HZ[b][:, :, :], (HP if d else HZ)[b][:, :, :], ACT.Exp)
                act.activation(HT_[b][:, :, 0:L], (HT_ if d else HP)[b][:, :, 0:L], ACT.Exp).then_inc(sem("hg_exps"), 1)

            def level_exp(g):
                act.wait_ge(sem("hg_warg"), g + 1)
                act.activation(HW[g % 2][:, :, :], HW[g % 2][:, :, :], ACT.Exp).then_inc(sem("hg_wexp"), 1)

            take_products((-1, 0))
            log1p_exp(0)
            keys(0)
            state_factors(0)
            for st in range(len(STEPS)):
                more = st + 1 < len(STEPS)
                level_exp(7 * st)
                level_exp(7 * st + 1)
                for i in range(7):
                    if i < 5:
                        act.wait_ge(*fill_of(f"kt{st}.{i}"))
                        act.activation(HKT[i % 2][:, :, :], bank(f"kt{st}.{i}")[:, 0:HH * P].rearrange("p (h c) -> p h c", h=HH),
                                       ACT.Copy).then_inc(emptied["a"], 1)
                        level_exp(7 * st + i + 2)
                    take_products((st, i))
                    if more and i == 3:
                        log1p_exp(st + 1)
                    if more and i == 5:
                        keys(st + 1)
                    if more and i == 6:
                        state_factors(st + 1)
                take_products((st, 7))
            act.wait_ge(sem("c_ms"), 1)
            act.activation(SM[:, 160:192], SM[:, 160:192], ACT.Sqrt).then_inc(sem("c_root"), 1)
            for t in range(4):
                act.wait_ge(*fill_of(f"cy{t}"))
                ps = bank(f"cy{t}")
                act.activation(HT[:, :, t * P:(t + 1) * P], ps[:, :].rearrange("p (k c) -> p k c", k=KD), ACT.Copy).then_inc(emptied["a"], 1)
            ln_root(2, 4)
            if stop <= 2:
                return
            def row_stats(name, at, ready=None, lo=0, hi=D, col=200):
                src, junk = at
                for t in range(TL):
                    if ready:
                        act.wait_ge(sem(ready), t + 1)
                    ins = act.activation(junk[:, t, lo:hi], src[:, t, lo:hi], ACT.Square, accum_out=SM[:, col + t:col + t + 1])
                ins.then_inc(sem(name), 1)

            def root(name, n):
                act.wait_ge(sem(name + "_ms"), n)
                act.activation(SM[:, 200:204], SM[:, 200:204], ACT.Sqrt).then_inc(sem(name + "_root"), 1)

            def pre_norm(n, ready, dst):
                row_stats("rms_sum", (X, dst), ready)
                root("rms", 2 * n - 1)
                act.wait_ge(sem("rms_inv"), 2 * n - 1)
                for t in range(TL):
                    act.activation(dst[:, t, :], X[:, t, :], ACT.Copy, scale=SM[:, 200 + t:201 + t]).then_inc(sem("xn_ready"), 1)

            def post_norm(n, name, dst, junk):
                for c in range(4):
                    act.wait_ge(*fill_of(f"{name}{c}.t0"))
                    ps = bank(f"{name}{c}.t0")
                    ins = act.activation(dst[:, :, c * WC:(c + 1) * WC], ps[:, :].rearrange("p (t c) -> p t c", t=4), ACT.Copy)
                    ins.then_inc(emptied["a"], 1)
                    if c >= 2:
                        act.wait_ge(*read_of(f"{name}{c}.t0"))
                        row_stats("rms_part" if c == 2 else "rms_sum", (dst, junk), None, 3 * WC * (c - 2), WC * (c + 1), 204 if c == 2 else 200)
                root("rms", 2 * n)

            act.wait_ge(sem("x2_ready"), 4)
            bcast_row(BC[:, 0, :], a["norm_mix_post_2"][0]).then_inc(sem("bc_in"), 16)
            bcast_row(BC[:, 1, :], a["norm_ffn_post_2"][0]).then_inc(sem("bc_in"), 16)
            act.dma_start(EPOS.bitcast(I32), a["positions_2"][0].partition_broadcast(P)).then_inc(sem("pos_in"), 16)
            act.dma_start(SROW[0:16, :], a["s5_a_re_2"][0].rearrange("(j g) p -> j (g p)", g=2)).then_inc(sem("s5_rows_in"), 16)
            act.dma_start(SROW[16:32, :], a["s5_a_im_2"][0].rearrange("(j g) p -> j (g p)", g=2)).then_inc(sem("s5_rows_in"), 16)
            act.dma_start(SM[32:48, 240:242], a["s5_log_dt_2"][0].rearrange("(j g) -> j g", g=2)).then_inc(sem("s5_dt_in"), 16)
            for k, nm in enumerate(("re", "im")):
                act.dma_start(SBRAW[k], a[f"s5_b_{nm}_2"][0].rearrange("(j g) p c -> (g p) j c", g=2)).then_inc(sem("s5_b_in"), 16)
                act.dma_start(SCRAW[k], a[f"s5_c_{nm}_2"][0].rearrange("(i g) c p -> (g c) i p", i=4)).then_inc(sem("s5_c_in"), 16)
            pre_norm(1, "x2_ready", XN)
            pair("eu0.lat", EU, 0, 0)
            act.wait_ge(sem("rope_arg"), 1)
            link(act.activation(COSP, COSP, ACT.Sin))
            act.activation(SINP, SINP, ACT.Sin).then_inc(sem("rope_tab"), 1)
            pr = lambda k: SPR[:, k, :]
            act.wait_ge(*read_of("s5rows"))
            act.activation(pr(2), pr(2), ACT.Exp).then_inc(sem("s5_dt"), 1)
            act.wait_ge(sem("s5_ang"), 1)
            link(act.activation(pr(5), pr(3), ACT.Exp))
            link(act.activation(pr(6), pr(6), ACT.Sin))
            act.activation(pr(7), pr(7), ACT.Sin).then_inc(sem("s5_sc"), 1)
            pair("eu1.lat", EU, 1, 0)
            for c in range(4):
                pair(f"eqk{c}.lat", EQK, c, 0)
            for c in range(2):
                act.wait_ge(*fill_of(f"ev{c}.t0"))
                ps = bank(f"ev{c}.t0")
                act.activation(EV[:, :, c * WC:(c + 1) * WC], ps[:, :].rearrange("p (t c) -> p t c", t=4), ACT.Copy).then_inc(emptied["a"], 1)
            for i in range(4):
                act.wait_ge(*read_of(f"s5y{2 * i + 1}"))
                act.activation(HT[:, 4 + i, 0:L], EU[:, i, :], ACT.Gelu_apprx_tanh).then_inc(sem("s5_gelu"), 1)
            for c in range(2):
                act.wait_ge(*fill_of(f"glu{c}"))
                ps = bank(f"glu{c}")
                act.activation(EU[:, 2 * c:2 * c + 2, :], ps[:, :].rearrange("p (m t) -> p m t", m=2), ACT.Sigmoid).then_inc(emptied["a"], 1)
            attention("E", EPB, EPT, 0.125, False)
            post_norm(1, "em", MX, XN)
            if stop <= 3:
                return

            def hi_parts(upto, end):
                while made["hi"] <= min(upto, end - 1):
                    i = made["hi"]
                    slot, kt = splits[i][:2]
                    if i >= 2:
                        act.wait_ge(*released[split_chunks[i - 2]])
                    act.wait_ge(sem("w_masked"), i + 1)
                    act.activation(W_HI[:, i % 2, 0:kt, :], WM[:, 0:kt, :], ACT.Copy).then_inc(sem("w_hi"), 1)
                    made["hi"] += 1

            def x_hi_parts(index):
                for t in range(TL):
                    ts = slice(t * P, (t + 1) * P)
                    act.wait_ge(sem("x_masked"), TL * index + t + 1)
                    act.activation(X_HI[:, :, ts], NM[:, :, ts], ACT.Copy).then_inc(sem("x_hi"), 1)

            def ffn(l, n, ready):
                pre_norm(n, ready, FX)
                first, end = FIRST[l], ffn_end(l)
                hi_parts(first, end)
                x_hi_parts(2 * l)
                hi_parts(first + 1, end)
                for what, half, c, at in ffn_steps(l):
                    if what == "pair":
                        q = l * (KF // 2) + c
                        hi_parts(at + 1, end)
                        act.wait_ge(*fill_of(f"fg{l}.{c}"))
                        if q >= 2:
                            act.wait_ge(sem("f_lo"), q - 1)
                        act.activation(FSG[:, q % 2], bank(f"fg{l}.{c}")[:, :].rearrange("p (m t) -> p m t", m=2),
                                       ACT.Silu).then_inc(emptied["a"], 1)
                        hi_parts(at + 2, end)
                        act.wait_ge(sem("f_masked"), q + 1)
                        act.activation(F_HI[c - HALVES[half][0]][:, :, :], FM, ACT.Copy).then_inc(sem("f_hi"), 1)
                    else:
                        hi_parts(at + 2, end)
                        if half == 0:
                            act.wait_ge(*fill_of(f"fm{l}0{c}"))
                            act.activation(FX[:, :, c * WC:(c + 1) * WC],
                                           bank(f"fm{l}0{c}")[:, :].rearrange("p (t c) -> p t c", t=TL), ACT.Copy).then_inc(emptied["a"], 1)
                for c in (2, 3):
                    act.wait_ge(*read_of(f"fm{l}1{c}"))
                    row_stats("rms_part" if c == 2 else "rms_sum", (FX, view(x_at + 4 * D, TL, D)), None, 3 * WC * (c - 2), WC * (c + 1), 204 if c == 2 else 200)
                root("rms", 2 * n)

            ffn(0, 2, "x3_ready")
            if stop <= 4:
                return
            act.wait_ge(sem("x4_ready"), 4)
            bcast_row(BC[:, 0, :], a["norm_mix_post_2"][1]).then_inc(sem("bc_in"), 16)
            bcast_row(BC[:, 1, :], a["norm_ffn_post_2"][1]).then_inc(sem("bc_in"), 16)
            pre_norm(3, "x4_ready", XN)
            hi_parts(RG0, RG_END)
            x_hi_parts(1)
            hi_parts(RG0 + 1, RG_END)
            act.wait_ge(sem("lam_abs"), 1)
            link(act.activation(SM[:, 216:224], SM[:, 216:224], ACT.Exp, scale=-1.0))
            act.activation(SM[:, 216:224], SM[:, 216:224], ACT.Ln, bias=ONES[:, 0:1]).then_inc(sem("lam_ln"), 1)
            hi_parts(RG0 + 4, RG_END)
            pair("rz0", RZG, 0, 0, ACT.Gelu_apprx_tanh)
            hi_parts(RG0 + 5, RG_END)
            for nm, dst, v0 in (("r", RA, V_BR), ("i", RGI, V_BI)):
                for h in range(4):
                    act.wait_ge(*fill_of(f"rg{nm}{h}"))
                    ps = bank(f"rg{nm}{h}")
                    for m in range(2):
                        t = 2 * h + m
                        last = act.activation(dst[:, t, :], ps[:, m * L:(m + 1) * L], ACT.Sigmoid, bias=VEC[:, v0 + t:v0 + t + 1])
                    last.then_inc(emptied["a"], 1)
                if nm == "r":
                    hi_parts(RG0 + 6, RG_END)
            act.wait_ge(*read_of("rgi3"))
            act.wait_ge(sem("rg_sp"), 1)
            for t in range(8):
                link(act.activation(RTH[:, t, :], RA[:, t, :], ACT.Tanh, scale=SM[:, 224 + t:225 + t]))
                act.activation(RA[:, t, :], RA[:, t, :], ACT.Exp, scale=SM[:, 232 + t:233 + t]).then_inc(sem("rg_a"), 1)
            hi_parts(RG0 + 7, RG_END)
            pair("rz1", RZG, 1, 0, ACT.Gelu_apprx_tanh)
            for t in range(8):
                act.wait_ge(sem("rg_msq"), t + 1)
                act.activation(RM[:, t, :], RM[:, t, :], ACT.Sqrt).then_inc(sem("rg_mult"), 1)
            for c in (2, 3):
                pair(f"rz{c}", RZG, c, 0, ACT.Gelu_apprx_tanh)
            post_norm(3, "om", MX3, RJ)
            if stop <= 5:
                return
            ffn(1, 4, "x5_ready")

        @block.vector
        def _(dve):
            ch_ = Chain(dve, "dve_chain")
            link = ch_.link

            def mod_layer(l):
                for what, g in MOD_STEPS:
                    label = f"mod_{what}{l}.{g}"
                    dve.wait_ge(*fill_of(label))
                    if what == "rows":
                        dve.tensor_copy(MR[0:2, g, :], bank(label)[0:2, :]).then_inc(emptied["v"], 1)
                        continue
                    b = VEC[:, V_BADA + 24 * l + 8 * g:V_BADA + 24 * l + 8 * g + 8]
                    dve.tensor_tensor(MOD[:, l, 8 * g:8 * g + 8, :], bank(label)[:, 0:16].rearrange("p (m j) -> p m j", j=2),
                                      b.unsqueeze(2).to_broadcast([P, 8, 2]), ALU.add).then_inc(emptied["v"], 1)
                    if g == 1:
                        dve.wait_ge(*read_of(label))
                        link(dve.tensor_scalar(MOD[:, l, 8:16, :], MOD[:, l, 8:16, :], 1.0, None, ALU.add))
                dve.wait_ge(*read_of(f"mod_turn{l}.2"))

            def gate_diag(l, n):
                for j in range(n):
                    if j:
                        dve.wait_ge(*fill_of(f"gate{l}.{j - 1}"))
                    dve.tensor_tensor(DG[:, :, :], IDENT.unsqueeze(1).to_broadcast([P, KD, P]),
                                      MOD[:, l, 16:24, j].unsqueeze(2).to_broadcast([P, KD, P]),
                                      ALU.mult).then_inc(sem(f"gate_diag{l}"), 1)

            def modulated(l, name, tiles):
                for t in tiles:
                    dve.wait_ge(*fill_of(f"{name}{t}"))
                    ps = bank(f"{name}{t}")
                    j = 0 if t < TL else 1
                    dst = HT[:, :, t * P:(t + 1) * P]
                    link(dve.tensor_tensor(dst, ps[:, :].rearrange("p (k c) -> p k c", k=KD),
                                           MOD[:, l, 8:16, j].unsqueeze(2).to_broadcast([P, KD, P]), ALU.mult))
                    dve.tensor_tensor(dst, dst, MOD[:, l, 0:8, j].unsqueeze(2).to_broadcast([P, KD, P]), ALU.add).then_inc(emptied["v"], 1)

            def join_gated(name, tiles, tmp):
                for c in range(4):
                    for g, t0, nt in ((0, 0, 4), (1, 4, 2)):
                        if t0 >= tiles:
                            continue
                        dve.wait_ge(*fill_of(f"{name}.{c}.t{g}"))
                        ps = bank(f"{name}.{c}.t{g}")
                        gate = GT[:, g, c * WC:(c + 1) * WC].unsqueeze(1).to_broadcast([P, nt, WC])
                        xs = X[:, t0:t0 + nt, c * WC:(c + 1) * WC]
                        ins = dve.tensor_tensor(tmp[:, 0:nt, :], ps[:, 0:nt * WC].rearrange("p (t c) -> p t c", t=nt), gate, ALU.mult)
                        ins.then_inc(emptied["v"], 1)
                        dve.wait_ge(*read_of(f"{name}.{c}.t{g}"))
                        link(dve.scalar_tensor_tensor(out=xs, in0=xs, scalar=ALPHA, in1=tmp[:, 0:nt, :], op0=ALU.mult, op1=ALU.add))

            def layer_norm(k, tiles, bc_count):
                for t in range(tiles):
                    for h in range(2):
                        last = dve.bn_stats(SM[:, 256 + 12 * t + 6 * h:256 + 12 * t + 6 * h + 6], X[:, t, h * 512:(h + 1) * 512])
                    link(last)
                    link(dve.bn_aggr(SM[:, 104 + 2 * t:106 + 2 * t], SM[:, 256 + 12 * t:268 + 12 * t]))
                mv = SM[:, 104:104 + 2 * tiles].rearrange("p (t m) -> p t m", m=2)
                dve.tensor_scalar(SM[:, 96:96 + tiles], mv[:, :, 1], LN_EPS, None, ALU.add).then_inc(sem("ln_var"), 1)
                dve.wait_ge(sem("ln_root"), k)
                link(dve.reciprocal(SM[:, 96:96 + tiles], SM[:, 96:96 + tiles]))
                dve.wait_ge(sem("bc_in"), bc_count)
                for t in range(tiles):
                    link(dve.scalar_tensor_tensor(out=X[:, t, :], in0=X[:, t, :], scalar=SM[:, 104 + 2 * t:105 + 2 * t],
                                                  in1=BC[:, 0, :], op0=ALU.subtract, op1=ALU.mult))
                    dve.scalar_tensor_tensor(out=X[:, t, :], in0=X[:, t, :], scalar=SM[:, 96 + t:97 + t], in1=BC[:, 1, :],
                                             op0=ALU.mult, op1=ALU.add).then_inc(sem(f"x{k}_ready"), 1)

            dve.wait_ge(*fill_of("vec"))
            ps = bank("vec")
            link(dve.tensor_copy(VEC[:, 0:108], ps[:, 0:108]))
            ins = dve.tensor_copy(VEC[:, 128:196], ps[:, 512:580])
            ins.then_inc(emptied["v"], 1)
            dve.wait_ge(*read_of("vec"))
            dve.wait_ge(sem("sink_in"), 16)
            link(dve.tensor_scalar(SM[:, 8:16], SM[:, 0:8], -1.0, None, ALU.mult))
            mod_layer(0)
            gate_diag(0, 2)
            modulated(0, "h0.", range(6))
            zero = tab("chunk", 0, 1)
            for i in range(4):
                for e in (0, L + 1, L + 2, LT + 3):
                    dve.memset(AU[:, i, e:e + 1], 0.0)
            lat_u = lambda c: AU[:, 2 * c:2 * c + 2, 1:1 + L]
            ctx_u = lambda c: AU[:, 2 * c:2 * c + 2, L + 3:L + 3 + LC]

            def two(ps, n):
                return ps[:, 0:2 * n].rearrange("p (m t) -> p m t", m=2)

            dve.wait_ge(*read_of("gb1.ctx"))
            for c in range(2):
                dve.wait_ge(*fill_of(f"bg{c}.lat"))
                dve.tensor_tensor(AGB[:, 2 * c:2 * c + 2, 0:L], AGB[:, 2 * c:2 * c + 2, 0:L], two(bank(f"bg{c}.lat"), L), ALU.mult).then_inc(emptied["v"], 1)
                dve.wait_ge(*fill_of(f"bg{c}.ctx"))
                dve.tensor_tensor(AGB[:, 2 * c:2 * c + 2, L:LT], AGB[:, 2 * c:2 * c + 2, L:LT], two(bank(f"bg{c}.ctx"), LC), ALU.mult).then_inc(emptied["v"], 1)
            for c in range(2):
                dve.wait_ge(*fill_of(f"xb{c}.lat"))
                dve.tensor_copy(lat_u(c), two(bank(f"xb{c}.lat"), L)).then_inc(emptied["v"], 1)
                dve.wait_ge(*fill_of(f"xb{c}.ctx"))
                dve.tensor_copy(ctx_u(c), two(bank(f"xb{c}.ctx"), LC)).then_inc(emptied["v"], 1)
            dve.wait_ge(*read_of("xb1.ctx"))
            for c in range(2):
                dve.wait_ge(*fill_of(f"cg{c}.lat"))
                dve.tensor_tensor(lat_u(c), lat_u(c), two(bank(f"cg{c}.lat"), L), ALU.mult).then_inc(emptied["v"], 1)
                dve.wait_ge(*fill_of(f"cg{c}.ctx"))
                dve.tensor_tensor(ctx_u(c), ctx_u(c), two(bank(f"cg{c}.ctx"), LC), ALU.mult).then_inc(emptied["v"], 1)
            cosb = lambda n: tab("cos_ax").unsqueeze(1).to_broadcast([P, n, L])
            sinb = lambda n: tab("sin_ax").unsqueeze(1).to_broadcast([P, n, L])

            def rope(label, x, n, cb, sb_, tmp, name, count):
                dve.wait_ge(*fill_of(label))
                ps = bank(label)
                ins = dve.tensor_tensor(tmp[:, 0:n, :], ps[:, 0:n * L].rearrange("p (m t) -> p m t", m=n), sb_(n), ALU.mult)
                ins.then_inc(emptied["v"], 1)
                dve.wait_ge(*read_of(label))
                link(dve.tensor_tensor(x, x, cb(n), ALU.mult))
                dve.tensor_tensor(x, x, tmp[:, 0:n, :], ALU.add).then_inc(sem(name), 1)
                dve.wait_ge(sem(name), count)

            rope("rope0", AQ[:, 0:2, 0:L], 2, cosb, sinb, ROT, "roped", 1)
            rope("rope1", AQ[:, 2:4, 0:L], 2, cosb, sinb, ROT, "roped", 2)
            rope("rope2", AKV[:, 0:1, 0:L], 1, cosb, sinb, ROT, "roped", 3)

            def conv_tile(i):
                for s0, n, d0 in ((0, L, 0), (L + 2, LC, L)):
                    acc = ACV[:, i % 2, d0:d0 + n]
                    wcol = lambda j: VEC[:, V_CONV + 4 * j + i:V_CONV + 4 * j + i + 1]
                    link(dve.tensor_scalar(acc, AU[:, i, s0:s0 + n], wcol(0), None, ALU.mult))
                    for j in (1, 2):
                        link(dve.scalar_tensor_tensor(out=acc, in0=AU[:, i, s0 + j:s0 + j + n], scalar=wcol(j), in1=acc,
                                                      op0=ALU.mult, op1=ALU.add))
                    dve.tensor_tensor(HT[:, 4 + i, d0:d0 + n], acc, AGB[:, i, d0:d0 + n], ALU.mult).then_inc(sem("conv"), 1)

            def attention(kind, PT, OT, scale, sink, finish, between):
                n = NT_ATT[kind] * HEADS
                for what, i in att_events(n):
                    qt, h = divmod(i, HEADS)
                    if what == "scores":
                        nb = len(att_blocks(kind, qt))
                        nu, e, k = units[f"{kind}s{i}"]
                        dve.wait_ge(filled, nu + 1)
                        col = 32 + 16 * (qt % 2) + h
                        if h == 0 and qt >= 2:
                            dve.wait_ge(*read_of(f"{kind}s{(qt - 1) * HEADS - 1}"))
                            if sink:
                                dve.wait_ge(sem(f"{kind}_sink"), qt - 1)
                        link(dve.tensor_reduce(SM[:, 80:81], ring[nu % 3][:, 0:nb * P], AX.X, ALU.max))
                        ins = dve.tensor_scalar(SM[:, col:col + 1], SM[:, 80:81], -scale,
                                                SM[:, 8 + h:9 + h] if sink else None,
                                                ALU.mult, *([ALU.min] if sink else []))
                        ins.then_inc(sem(f"{kind}_max"), 1)
                        dve.wait_ge(sem(f"{kind}_max"), i + 1)
                        if h == HEADS - 1 and sink:
                            s0, b0 = 64 + 8 * (qt % 2), 32 + 16 * (qt % 2)
                            dve.tensor_tensor(SM[:, s0:s0 + 8], SM[:, 0:8], SM[:, b0:b0 + 8], ALU.add).then_inc(sem(f"{kind}_sinkarg"), 1)
                    elif what == "turn" and i % 2:
                        nb = len(att_blocks(kind, qt))
                        dve.wait_ge(*fill_of(f"{kind}t{i}"))
                        ps = bank(f"{kind}t{i}")
                        if i >= 2:
                            dve.wait_ge(sem(f"{kind}_values"), i - 1)
                        dve.tensor_copy(PT[:, i % 2, 0:nb * P], ps[:, 0:nb * P]).then_inc(emptied["v"], 1)
                    elif what == "finish":
                        qt = i
                        last_s = units[f"{kind}s{qt * HEADS + HEADS - 1}"]
                        dve.wait_ge(emptied["a"], last_s[2])
                        den = SM[:, 32 + 16 * (qt % 2) + 8:32 + 16 * (qt % 2) + 16]
                        if sink:
                            dve.wait_ge(sem(f"{kind}_sink"), qt + 1)
                            s0 = 64 + 8 * (qt % 2)
                            link(dve.tensor_tensor(SM[:, 82:90], den, SM[:, s0:s0 + 8], ALU.add))
                            link(dve.reciprocal(SM[:, 82:90], SM[:, 82:90]))
                        else:
                            link(dve.reciprocal(SM[:, 82:90], den))
                        dve.wait_ge(sem(f"{kind}_values"), (qt + 1) * HEADS)
                        if qt >= 2:
                            dve.wait_ge(*fill_of(f"{kind}o{qt - 2}"))
                        dve.tensor_tensor(OT[:, qt % 2, :].rearrange("p (h c) -> p h c", h=HEADS),
                                          obank[qt % 2][:, :].rearrange("p (h c) -> p h c", h=HEADS),
                                          SM[:, 82:90].unsqueeze(2).to_broadcast([P, HEADS, DH]),
                                          ALU.mult).then_inc(sem(f"{kind}_normed"), 1)
                        dve.wait_ge(sem(f"{kind}_normed"), qt + 1)
                        between(qt)
                        dve.wait_ge(*fill_of(f"{kind}o{qt}"))
                        ps = bank(f"{kind}o{qt}")
                        finish(qt, ps[:, 0:512].rearrange("p (f c) -> p f c", f=4))

            def finish_a(qt, o):
                dve.tensor_tensor(HT[:, 0:4, qt * P:(qt + 1) * P], o, AGA[:, :, qt * P:(qt + 1) * P], ALU.mult).then_inc(emptied["v"], 1)

            attention("A", APT, AOT, 0.125, True, finish_a, lambda qt: conv_tile(qt) if qt < 4 else None)
            join_gated("y0", 6, ATMP)
            layer_norm(1, 6, 32)
            if stop <= 1:
                return

            mod_layer(1)
            gate_diag(1, 1)
            modulated(1, "h1.", range(6))
            QS = 128.0 ** -0.5

            def take_products(key):
                for kind, k, part, label in rounds[key]:
                    if kind == "z":
                        z = HZ[k % 2]
                        dve.wait_ge(*fill_of(label))
                        if part < 2:
                            dve.tensor_copy(z[:, part, 0:L], bank(label)[:, 0:L]).then_inc(emptied["v"], 1)
                        else:
                            dve.tensor_copy(z[:, :, L:LT], two(bank(label), LC)).then_inc(emptied["v"], 1)

            DEC = [SM[:, 128 + 12 * b:140 + 12 * b].rearrange("p (h c) -> p h c", h=HH) for b in range(2)]
            PL = [SM[:, 352 + 12 * b:364 + 12 * b].rearrange("p (h c) -> p h c", h=HH) for b in range(2)]

            def abs_z(st):
                z = HZ[st % 2]
                dve.wait_ge(*read_of(f"cz{st}.2"))
                dve.scalar_tensor_tensor(out=HT_[st % 2][:, :, :], in0=z[:, :, :], scalar=-1.0, in1=z[:, :, :],
                                         op0=ALU.mult, op1=ALU.max).then_inc(sem("hg_abs"), 1)

            def log_f_and_sums(st):
                b = st % 2
                dve.wait_ge(sem("hg_ln"), st + 1)
                dve.scalar_tensor_tensor(out=HT_[b][:, :, :], in0=HZ[b][:, :, :], scalar=0.0, in1=HT_[b][:, :, :],
                                         op0=ALU.min, op1=ALU.subtract).then_inc(sem("hg_lf"), 1)
                dve.wait_ge(sem("hg_lf"), st + 1)
                for h in range(HH):
                    dve.tensor_tensor_scan(HP[b][:, h, 0:L], tab("chunk"), HT_[b][:, h, 0:L], 0.0, ALU.mult, ALU.add)
                    last = dve.tensor_tensor_scan(HP[b][:, h, L:LT], tab("chunk", 0, LC), HT_[b][:, h, L:LT], 0.0, ALU.mult, ALU.add)
                link(last)
                link(dve.tensor_copy(PL[b], HP[b][:, :, :].rearrange("p h (c t) -> p h c t", t=P)[:, :, :, P - 1]))
                dve.tensor_copy(DEC[b], PL[b]).then_inc(sem("hg_sums"), 1)

            def state_operands(st):
                b, q = st % 2, STEPS[st][0] % 2
                dve.wait_ge(sem("hg_k"), st + 1)
                dve.wait_ge(sem("hg_exps"), st + 1)
                dve.tensor_tensor(HZ[b][:, :, :], HZ[b][:, :, :], HK[b][:, :, :], ALU.mult).then_inc(sem("hg_ks"), 1)
                dve.wait_ge(*read_of(f"cq{STEPS[st][0]}.1"))
                dve.tensor_tensor(HT_[b][:, :, 0:L], HT_[b][:, :, 0:L], HQ[q][:, :, :], ALU.mult).then_inc(sem("hg_qi"), 1)

            def level_operand(g):
                st, li = divmod(g, 7)
                hb, d = STEPS[st]
                dve.wait_ge(sem("hg_wexp"), g + 1)
                w4 = HW[g % 2][:, :, :].rearrange("p g (b s h) -> p g b s h", s=2, h=LEVELS[li])
                for side in range(2):
                    f = (HK[st % 2] if side == d else HQ[hb % 2])[:, :, 0:L]
                    f4 = f.rearrange("p g (b s h) -> p g b s h", s=2, h=LEVELS[li])
                    last = dve.tensor_tensor(w4[:, :, :, side, :], w4[:, :, :, side, :], f4[:, :, :, side, :], ALU.mult)
                last.then_inc(sem("hg_w"), 1)

            take_products((-1, 0))
            abs_z(0)
            log_f_and_sums(0)
            state_operands(0)
            for st, (hb, d) in enumerate(STEPS):
                more = st + 1 < len(STEPS)
                b = st % 2
                level_operand(7 * st)
                dve.wait_ge(*fill_of(f"dg{st}"))
                src = bank(f"dg{st}")[:, :].rearrange("p (j c) -> p j c", j=TL * HH)
                idb = IDENT.unsqueeze(1).to_broadcast([P, TL * HH, P])
                if d == 0:
                    dve.tensor_tensor(HSC[:, :, :], src, idb, ALU.mult).then_inc(emptied["v"], 1)
                    dve.wait_ge(*read_of(f"dg{st}"))
                else:
                    dve.tensor_tensor(HDG[:, :, :], src, idb, ALU.mult).then_inc(emptied["v"], 1)
                    dve.wait_ge(*read_of(f"dg{st}"))
                    link(dve.tensor_tensor(HSC[:, :, :], HSC[:, :, :], HDG[:, :, :], ALU.add))
                seq = hg_seq(d)
                for i in range(7):
                    ch = seq[i] if i < 6 else None
                    if i < 6 and ch < TL:
                        dve.wait_ge(*fill_of(f"oi{st}.{i}"))
                        o = HO[:, ch, hb * WC:(hb + 1) * WC]
                        ps = bank(f"oi{st}.{i}")[:, 0:WC]
                        if d == 0:
                            dve.tensor_scalar(o, ps, QS, None, ALU.mult).then_inc(emptied["v"], 1)
                        else:
                            dve.scalar_tensor_tensor(out=o, in0=ps, scalar=QS, in1=o, op0=ALU.mult, op1=ALU.add).then_inc(emptied["v"], 1)
                    if i < 6:
                        level_operand(7 * st + i + 1)
                    dve.wait_ge(*fill_of(f"lv{st}.{i}"))
                    h2 = LEVELS[i]
                    nb = 64 // h2
                    m = tab("lv_f" if d == 0 else "lv_b", 64 * i, 64 * i + 64).bitcast(U32)
                    m = m.rearrange("p (b h) -> p b h", h=h2).unsqueeze(1).to_broadcast([P, TL * HH, nb, h2])
                    o = HSC[:, :, :].rearrange("p j (b s h) -> p j b s h", s=2, h=h2)[:, :, :, 1 - d, :]
                    ps = bank(f"lv{st}.{i}")[:, 0:512].rearrange("p (j b h) -> p j b h", j=TL * HH, h=h2)
                    dve.copy_predicated(o, m, ps).then_inc(emptied["v"], 1)
                    dve.wait_ge(*read_of(f"lv{st}.{i}"))
                    take_products((st, i))
                    if more and i == 2:
                        abs_z(st + 1)
                    if more and i == 4:
                        log_f_and_sums(st + 1)
                    if i < 5:
                        dve.wait_ge(*fill_of(f"su{st}.{i}"))
                        ps = bank(f"su{st}.{i}")
                        if i == 0:
                            dve.tensor_copy(HS[:, :, :], ps[:, 0:WC].rearrange("p (h c) -> p h c", h=HH)).then_inc(emptied["v"], 1)
                        else:
                            for h in range(HH):
                                ins = dve.scalar_tensor_tensor(out=HS[:, h, :], in0=HS[:, h, :], scalar=DEC[b][:, h, ch:ch + 1],
                                                               in1=ps[:, h * P:(h + 1) * P], op0=ALU.mult, op1=ALU.add)
                            ins.then_inc(emptied["v"], 1)
                        dve.wait_ge(*read_of(f"su{st}.{i}"))
                    if more and i == 6:
                        state_operands(st + 1)
                take_products((st, 7))
                if d == 1:
                    dve.wait_ge(*fill_of(f"oo{hb}"))
                    o = HO[:, :, hb * WC:(hb + 1) * WC]
                    dve.scalar_tensor_tensor(out=o, in0=bank(f"oo{hb}")[:, :].rearrange("p (t c) -> p t c", t=TL), scalar=QS, in1=o,
                                             op0=ALU.mult, op1=ALU.add).then_inc(emptied["v"], 1)
                    dve.wait_ge(*read_of(f"oo{hb}"))
                    link(dve.tensor_tensor(HSQ, o, o, ALU.mult))
                    link(dve.tensor_reduce(SM[:, 160:192].rearrange("p (t h) -> p t h", t=TL)[:, :, HH * hb:HH * hb + HH],
                                           HSQ.rearrange("p t (h c) -> p t h c", h=HH), AX.X, ALU.add))
            MS = SM[:, 160:192].rearrange("p (t h) -> p t h", t=4)
            o3 = lambda t: HO[:, t, :].rearrange("p (h c) -> p h c", h=HEADS)
            dve.tensor_scalar(SM[:, 160:192], SM[:, 160:192], 1.0 / P, RMS_EPS, ALU.mult, ALU.add).then_inc(sem("c_ms"), 1)
            dve.wait_ge(sem("gn_in"), 16)
            dve.wait_ge(*read_of("cg3.1"))
            g3 = lambda t: CG[:, t, :].rearrange("p (h c) -> p h c", h=HEADS)
            for t in range(TL):
                last = dve.tensor_tensor(g3(t), g3(t), GN.unsqueeze(1).to_broadcast([P, HEADS, P]), ALU.mult)
            link(last)
            dve.wait_ge(sem("c_root"), 1)
            link(dve.reciprocal(SM[:, 160:192], SM[:, 160:192]))
            for t in range(TL):
                link(dve.tensor_tensor(o3(t), o3(t), MS[:, t, :].unsqueeze(2).to_broadcast([P, HEADS, P]), ALU.mult))
                dve.tensor_tensor(HO[:, t, :], HO[:, t, :], CG[:, t, :], ALU.mult).then_inc(sem("c_y"), 1)
            join_gated("y1", 4, CTMP)
            layer_norm(2, 4, 64)
            if stop <= 2:
                return
            R4 = SM[:, 200:204]

            def inv_rms(k):
                dve.wait_ge(sem("rms_sum"), k)
                if k % 2 == 0:
                    dve.wait_ge(sem("rms_part"), k // 2)
                    link(dve.tensor_tensor(R4, R4, SM[:, 204:208], ALU.add))
                dve.tensor_scalar(R4, R4, 1.0 / D, RMS_EPS, ALU.mult, ALU.add).then_inc(sem("rms_ms"), 1)
                dve.wait_ge(sem("rms_root"), k)
                dve.reciprocal(R4, R4).then_inc(sem("rms_inv"), 1)
                dve.wait_ge(sem("rms_inv"), k)

            def pre_norm(n, v0):
                inv_rms(2 * n - 1)
                for t in range(TL):
                    dve.wait_ge(*fill_of(f"n{n}.{t}"))
                    ps = bank(f"n{n}.{t}")
                    dve.tensor_tensor(HT[:, :, t * P:(t + 1) * P], ps[:, :].rearrange("p (k c) -> p k c", k=KD),
                                           VEC[:, v0:v0 + 8].unsqueeze(2).to_broadcast([P, KD, P]), ALU.mult).then_inc(emptied["v"], 1)

            def weighted(src, G, b, c):
                cs = slice(c * WC, (c + 1) * WC)
                link(dve.tensor_tensor(G[:, :, cs], src[:, :, cs], BC[:, b, cs].unsqueeze(1).to_broadcast([P, TL, WC]), ALU.mult))

            def post_norm(n, G):
                inv_rms(2 * n)
                for t in range(TL):
                    dve.scalar_tensor_tensor(out=X[:, t, :], in0=G[:, t, :], scalar=SM[:, 200 + t:201 + t],
                                             in1=X[:, t, :], op0=ALU.mult, op1=ALU.add).then_inc(sem(f"x{n + 2}_ready"), 1)

            def mixer_norm(n, name, count, out_, G):
                dve.wait_ge(sem("bc_in"), count)
                for c in range(4):
                    dve.wait_ge(*read_of(f"{name}{c}.t0"))
                    weighted(out_, G, 0, c)
                post_norm(n, G)

            C1, C2 = 6.28125, 0.0019340515136718750
            C3 = TWO_PI - C1 - C2
            PI_ = 3.1415925

            def sine_args(ang, s_, c_, tmp, ready):
                link(dve.tensor_scalar(tmp, ang, 1.0 / TWO_PI, MAGIC, ALU.mult, ALU.add))
                link(dve.tensor_scalar(tmp, tmp, -MAGIC, None, ALU.add))
                link(dve.scalar_tensor_tensor(out=s_, in0=tmp, scalar=-C1, in1=ang, op0=ALU.mult, op1=ALU.add))
                link(dve.scalar_tensor_tensor(out=s_, in0=tmp, scalar=-C2, in1=s_, op0=ALU.mult, op1=ALU.add))
                link(dve.scalar_tensor_tensor(out=s_, in0=tmp, scalar=-C3, in1=s_, op0=ALU.mult, op1=ALU.add))
                link(dve.tensor_scalar(c_, s_, np.pi / 2, None, ALU.add))
                link(dve.tensor_scalar(tmp, c_, np.pi, TWO_PI, ALU.is_gt, ALU.mult))
                link(dve.tensor_tensor(c_, c_, tmp, ALU.subtract))
                link(dve.tensor_scalar(c_, c_, PI_, -PI_, ALU.min, ALU.max))
                dve.tensor_scalar(s_, s_, PI_, -PI_, ALU.min, ALU.max).then_inc(sem(ready), 1)

            colt = lambda k: tab("cols", k, k + 1)
            pre_norm(1, V_NPRE)
            dve.wait_ge(sem("pos_in"), 16)
            A1, A2 = SP1[:, 0, :], SP2[:, 0, :]
            link(dve.tensor_copy(A1, EPOS.bitcast(I32)))
            link(dve.tensor_scalar(A1, A1, colt(0), None, ALU.mult))
            sine_args(A1, SINP, COSP, A2, "rope_arg")
            dve.wait_ge(sem("s5_dt_in"), 16)
            dve.tensor_copy(SROW[32:48, :].rearrange("j (g p) -> j g p", g=2),
                            SM[32:48, 240:242].unsqueeze(2).to_broadcast([16, 2, DH])).then_inc(sem("s5_dt_rows"), 1)
            dve.wait_ge(sem("s5_c_in"), 32)
            for k, sg in ((0, 1.0), (1, -1.0)):
                for gg in range(2):
                    ins = dve.tensor_scalar(SCEX[k][:, :, gg * DH:(gg + 1) * DH], SCRAW[k], colt(2 + gg), sg, ALU.mult, ALU.mult)
                    if (k, gg) != (1, 1):
                        link(ins)
            ins.then_inc(sem("s5_cexp"), 1)
            pr = lambda k: SPR[:, k, :]
            dve.wait_ge(*fill_of("s5rows"))
            ps = bank("s5rows")
            dve.tensor_copy(SPR[:, 0:3, :], ps[:, 0:48].rearrange("p (k j) -> p k j", k=3)).then_inc(emptied["v"], 1)
            dve.wait_ge(*read_of("s5rows"))
            dve.wait_ge(sem("s5_dt"), 1)
            mul = lambda o, x, y: link(dve.tensor_tensor(o, x, y, ALU.mult))
            add = lambda o, x, y: link(dve.tensor_tensor(o, x, y, ALU.add))
            sub = lambda o, x, y: link(dve.tensor_tensor(o, x, y, ALU.subtract))
            mul(pr(3), pr(0), pr(2))
            mul(pr(4), pr(1), pr(2))
            sine_args(pr(4), pr(6), pr(7), pr(8), "s5_ang")
            dve.wait_ge(sem("s5_ang"), 1)
            mul(pr(8), pr(0), pr(0))
            mul(pr(9), pr(1), pr(1))
            add(pr(8), pr(8), pr(9))
            link(dve.reciprocal(pr(8), pr(8)))
            dve.wait_ge(sem("s5_sc"), 1)
            mul(pr(9), pr(5), pr(7))
            link(dve.tensor_scalar(pr(9), pr(9), -1.0, None, ALU.add))
            mul(pr(10), pr(5), pr(6))
            mul(pr(11), pr(9), pr(0))
            mul(pr(12), pr(10), pr(1))
            add(pr(11), pr(11), pr(12))
            mul(pr(11), pr(11), pr(8))
            mul(pr(12), pr(10), pr(0))
            mul(pr(13), pr(9), pr(1))
            sub(pr(12), pr(12), pr(13))
            mul(pr(12), pr(12), pr(8))
            dve.wait_ge(sem("s5_b_in"), 32)
            wr, wi = (pr(k).unsqueeze(2).to_broadcast([P, 16, 16]) for k in (11, 12))
            q1 = A1[:, 0:256].rearrange("p (j c) -> p j c", j=16)
            q2 = A1[:, 256:512].rearrange("p (j c) -> p j c", j=16)
            q3 = A2[:, 0:256].rearrange("p (j c) -> p j c", j=16)
            mul(q1, SBRAW[0], wr)
            mul(q2, SBRAW[1], wi)
            sub(q1, q1, q2)
            mul(q2, SBRAW[0], wi)
            mul(q3, SBRAW[1], wr)
            add(q2, q2, q3)
            for k, q in ((0, q1), (1, q2)):
                for gg in range(2):
                    ins = dve.tensor_scalar(SBBL[k][:, :, gg * 16:(gg + 1) * 16], q, colt(4 + gg), None, ALU.mult)
                    if (k, gg) != (1, 1):
                        link(ins)
            ins.then_inc(sem("s5_bblk"), 1)
            dve.wait_ge(*fill_of("s5c"))
            ps = bank("s5c")
            for k in range(2):
                ins = dve.tensor_copy(SCD[k], ps[:, 512 * k:512 * k + 512].rearrange("p (i c) -> p i c", i=4))
                link(ins) if k == 0 else ins.then_inc(emptied["v"], 1)
            dve.wait_ge(*fill_of("s5b"))
            ps = bank("s5b")
            for k in range(2):
                ins = dve.tensor_copy(SBD[k], ps[:, 512 * k:512 * k + 512].rearrange("p (i c) -> p i c", i=4))
                link(ins) if k == 0 else ins.then_inc(emptied["v"], 1)

            def s5_step(st):
                b = st % 2
                er, ei, br, bi = SER[b], SEI[b], SBR[b], SBI[b]
                dve.wait_ge(sem("s5_tables"), st + 1)
                if st >= 2:
                    dve.wait_ge(sem("s5_hi"), st - 1)
                if st:
                    dve.wait_ge(sem("s5_hr"), st)
                for jj in range(2):
                    label = f"bu{2 * st + jj}"
                    dve.wait_ge(*fill_of(label))
                    ur, ui = bank(label)[:, 0:L], bank(label)[:, L:2 * L]
                    dve.tensor_tensor(br[:, jj, :], er[:, jj, :], ur, ALU.mult)
                    dve.tensor_tensor(bi[:, jj, :], er[:, jj, :], ui, ALU.mult)
                    dve.tensor_tensor(SP1[:, jj, :], ei[:, jj, :], ui, ALU.mult)
                    dve.tensor_tensor(SP2[:, jj, :], ei[:, jj, :], ur, ALU.mult).then_inc(emptied["v"], 1)
                dve.wait_ge(*read_of(f"bu{2 * st + 1}"))
                dve.tensor_tensor(br, br, SP1, ALU.add)
                link(dve.tensor_tensor(bi, bi, SP2, ALU.subtract))
                for jj in range(2):
                    rho = pr(5)[:, 2 * st + jj:2 * st + jj + 1].to_broadcast([P, L])
                    dve.tensor_tensor_scan(br[:, jj, :], rho, br[:, jj, :], 0.0, ALU.mult, ALU.add)
                    last = dve.tensor_tensor_scan(bi[:, jj, :], rho, bi[:, jj, :], 0.0, ALU.mult, ALU.add)
                last.then_inc(sem("s5_sums"), 1)
                dve.wait_ge(sem("s5_sums"), st + 1)
                if st >= 2:
                    dve.wait_ge(*fill_of(f"s5y{st - 2}"))
                dve.tensor_tensor(SHR[b], er, br, ALU.mult)
                link(dve.tensor_tensor(SP1, ei, bi, ALU.mult))
                dve.tensor_tensor(SHR[b], SHR[b], SP1, ALU.subtract).then_inc(sem("s5_hr"), 1)

            def s5_skip(st):
                label, i, half = f"s5y{st}", st // 2, slice(64 * (st % 2), 64 * (st % 2) + 64)
                dve.wait_ge(*fill_of(label))
                dve.scalar_tensor_tensor(out=EU[half, i, :], in0=EU[half, i, :], scalar=VEC[half, V_D + i:V_D + i + 1],
                                         in1=bank(label)[half, 0:L], op0=ALU.mult, op1=ALU.add).then_inc(emptied["v"], 1)

            dve.wait_ge(sem("rope_tab"), 1)
            cosb = lambda n: COSP.unsqueeze(1).to_broadcast([P, n, L])
            sinb = lambda n: SINP.unsqueeze(1).to_broadcast([P, n, L])
            for st in range(S5_STEPS):
                s5_step(st)
                if st:
                    s5_skip(st - 1)
                if 1 <= st < 5:
                    c = st - 1
                    rope(f"erope{c}", EQK[:, 2 * c:2 * c + 2, :], 2, cosb, sinb, EROT, "eroped", c + 1)
            s5_skip(S5_STEPS - 1)

            def gate_s5(qt):
                if qt == 0:
                    dve.wait_ge(*read_of("glu1"))
                    for m in range(4):
                        dve.tensor_tensor(HT[:, 4 + m, 0:L], HT[:, 4 + m, 0:L], EU[:, m, :], ALU.mult).then_inc(sem("s5_out"), 1)

            def finish_e(qt, o):
                dve.tensor_copy(HT[:, 0:4, qt * P:(qt + 1) * P], o).then_inc(emptied["v"], 1)

            attention("E", EPT, EOT, 0.125, False, finish_e, gate_s5)
            mixer_norm(1, "em", 96, MX, view(w + TL * D, TL, D))
            if stop <= 3:
                return

            def mask(upto, end):
                while made["masked"] <= min(upto, end - 1):
                    i = made["masked"]
                    slot, kt, loaded, count_ = splits[i]
                    dve.wait_ge(loaded, count_)
                    if i:
                        dve.wait_ge(sem("w_hi"), i)
                        dve.wait_ge(sem("w_lo"), i)
                    dve.tensor_scalar(WM[:, 0:kt, :].bitcast(I32), WR[:, slot, 0:kt, :].bitcast(I32), LOW_BITS_OFF, None,
                                      ALU.bitwise_and).then_inc(sem("w_masked"), 1)
                    made["masked"] += 1

            def split_norm(n, v0):
                inv_rms(2 * n - 1)
                for t in range(TL):
                    ts = slice(t * P, (t + 1) * P)
                    dve.wait_ge(*fill_of(f"n{n}.{t}"))
                    dve.tensor_tensor(NT[:, :, ts], bank(f"n{n}.{t}")[:, :].rearrange("p (k c) -> p k c", k=KD),
                                      VEC[:, v0:v0 + 8].unsqueeze(2).to_broadcast([P, KD, P]), ALU.mult).then_inc(emptied["v"], 1)
                    dve.wait_ge(*read_of(f"n{n}.{t}"))
                    dve.tensor_scalar(NM[:, :, ts].bitcast(I32), NT[:, :, ts].bitcast(I32), LOW_BITS_OFF, None,
                                      ALU.bitwise_and).then_inc(sem("x_masked"), 1)

            def ffn(l, n, count):
                first, end = FIRST[l], ffn_end(l)
                mask(first, end)
                split_norm(n, V_NFFN + 8 * l)
                mask(first + 1, end)
                for what, half, c, at in ffn_steps(l):
                    mask(at + 2, end)
                    if what == "pair":
                        q = l * (KF // 2) + c
                        g = FSG[:, q % 2]
                        dve.wait_ge(*fill_of(f"fu{l}.{c}"))
                        dve.wait_ge(*read_of(f"fg{l}.{c}"))
                        dve.tensor_tensor(g, g, bank(f"fu{l}.{c}")[:, :].rearrange("p (m t) -> p m t", m=2), ALU.mult).then_inc(emptied["v"], 1)
                        dve.wait_ge(*read_of(f"fu{l}.{c}"))
                        if q:
                            dve.wait_ge(sem("f_hi"), q)
                            dve.wait_ge(sem("f_lo"), q)
                        dve.tensor_scalar(FM.bitcast(I32), g.bitcast(I32), LOW_BITS_OFF, None, ALU.bitwise_and).then_inc(sem("f_masked"), 1)
                    elif half == 1:
                        o = FX[:, :, c * WC:(c + 1) * WC]
                        dve.wait_ge(*fill_of(f"fm{l}1{c}"))
                        dve.wait_ge(*read_of(f"fm{l}0{c}"))
                        dve.tensor_tensor(o, o, bank(f"fm{l}1{c}")[:, :].rearrange("p (t c) -> p t c", t=TL), ALU.add).then_inc(emptied["v"], 1)
                        if c == 0:
                            dve.wait_ge(sem("bc_in"), count)
                            dve.wait_ge(sem("f_hi"), (l + 1) * (KF // 2))
                            dve.wait_ge(sem("f_lo"), (l + 1) * (KF // 2))
                        dve.wait_ge(*read_of(f"fm{l}1{c}"))
                        weighted(FX, FG, 1, c)
                post_norm(n, FG)

            ffn(0, 2, 96)
            if stop <= 4:
                return
            lam, sp = VEC[:, V_LAM:V_LAM + 8], SM[:, 216:224]
            dve.scalar_tensor_tensor(out=sp, in0=lam, scalar=-1.0, in1=lam, op0=ALU.mult, op1=ALU.max).then_inc(sem("lam_abs"), 1)
            mask(RG0, RG_END)
            split_norm(3, V_NPRE + 8)
            mask(RG0 + 1, RG_END)
            dve.wait_ge(sem("lam_ln"), 1)
            link(dve.tensor_scalar(SM[:, 224:232], lam, -1.0, 0.0, ALU.mult, ALU.max))
            link(dve.tensor_tensor(sp, sp, SM[:, 224:232], ALU.add))
            link(dve.tensor_scalar(SM[:, 224:232], sp, 8.0, None, ALU.mult))
            dve.tensor_scalar(SM[:, 232:240], sp, -8.0, None, ALU.mult).then_inc(sem("rg_sp"), 1)
            dve.wait_ge(sem("x_hi"), 2 * TL)
            dve.wait_ge(sem("x_lo"), 2 * TL)
            link(dve.memset(RXB[:, :, 0:3], 0.0))
            for c in range(4):
                mask(RG0 + min(c + 2, 4), RG_END)
                dve.wait_ge(*fill_of(f"rx{c}"))
                dve.tensor_copy(RXB[:, 2 * c:2 * c + 2, 3:3 + L], two(bank(f"rx{c}"), L)).then_inc(emptied["v"], 1)
            dve.wait_ge(*read_of("rx3"))
            for t in range(8):
                wcol = lambda j: VEC[:, V_RCW + 8 * j + t:V_RCW + 8 * j + t + 1]
                link(dve.tensor_scalar(RXC[:, t, :], RXB[:, t, 0:L], wcol(0), VEC[:, V_RCB + t:V_RCB + t + 1], ALU.mult, ALU.add))
                for j in (1, 2, 3):
                    ins = dve.scalar_tensor_tensor(out=RXC[:, t, :], in0=RXB[:, t, j:j + L], scalar=wcol(j), in1=RXC[:, t, :],
                                                   op0=ALU.mult, op1=ALU.add)
                    if j < 3:
                        link(ins)
                ins.then_inc(sem("rg_conv"), 1)
            mask(RG0 + 6, RG_END)
            dve.wait_ge(*read_of("rgi3"))
            dve.wait_ge(sem("rg_conv"), 8)
            mask(RG0 + 7, RG_END)
            for t in range(8):
                dve.wait_ge(sem("rg_a"), t + 1)
                dve.tensor_tensor(RGI[:, t, :], RGI[:, t, :], RXC[:, t, :], ALU.mult)
                if t >= 2:
                    dve.wait_ge(sem("rg_msq"), t - 1)
                link(dve.tensor_tensor(RA2[t % 2], RA[:, t, :], RA[:, t, :], ALU.mult))
                dve.scalar_tensor_tensor(out=RM[:, t, :], in0=RA2[t % 2], scalar=1.0, in1=RTH[:, t, :],
                                         op0=ALU.add, op1=ALU.mult).then_inc(sem("rg_msq"), 1)
            for t in range(8):
                dve.wait_ge(sem("rg_mult"), t + 1)
                link(dve.tensor_tensor(RGI[:, t, :], RGI[:, t, :], RM[:, t, :], ALU.mult))
                link(dve.tensor_tensor_scan(RXC[:, t, :], RA[:, t, :], RGI[:, t, :], 0.0, ALU.mult, ALU.add))
            dve.wait_ge(*read_of("rz3"))
            for t in range(8):
                dve.tensor_tensor(RM[:, t, :], RXC[:, t, :], RZG[:, t, :], ALU.mult).then_inc(sem("rg_out"), 1)
            mixer_norm(3, "om", 128, MX3, G3)
            if stop <= 5:
                return
            ffn(1, 4, 128)

        @block.gpsimd
        def _(pool):
            PL = [SM[:, 352 + 12 * b:364 + 12 * b].rearrange("p (h c) -> p h c", h=HH) for b in range(2)]

            def key_args(st):
                b = st % 2
                pool.wait_ge(sem("hg_lf"), st + 1)
                pool.tensor_tensor(HK[b][:, :, :], HT_[b][:, :, :], HZ[b][:, :, :], ALU.subtract).then_inc(sem("hg_karg"), 1)

            def state_args(st):
                b, d = st % 2, STEPS[st][1]
                pool.wait_ge(sem("hg_sums"), st + 1)
                if d == 1:
                    pool.tensor_tensor(HP[b][:, :, :], HP[b][:, :, :], HT_[b][:, :, :], ALU.subtract).then_inc(sem("hg_excl"), 1)
                    pool.wait_ge(sem("hg_excl"), STEPS[st][0] + 1)
                pool.wait_ge(sem("hg_karg"), st + 1)
                n = 4 if d else 6
                dst = (HT_ if d else HZ)[b]
                for h in range(HH):
                    c3 = lambda ap: ap[:, h, 0:n * P].rearrange("p (c t) -> p c t", t=P)
                    last = pool.tensor_tensor(c3(dst), PL[b][:, h, 0:n].unsqueeze(2).to_broadcast([P, n, P]), c3(HP[b]), ALU.subtract)
                last.then_inc(sem("hg_arg"), 1)

            def level_args(g):
                st, li = divmod(g, 7)
                d, h2 = STEPS[st][1], LEVELS[li]
                if g >= 2:
                    pool.wait_ge(*fill_of(f"lv{(g - 2) // 7}.{(g - 2) % 7}"))
                n = L // (2 * h2)
                p4 = HP[st % 2][:, :, 0:L].rearrange("p g (b s h) -> p g b s h", s=2, h=h2)
                w4 = HW[g % 2][:, :, :].rearrange("p g (b s h) -> p g b s h", s=2, h=h2)
                ref = p4[:, :, :, 0, h2 - 1:h2] if d == 0 else p4[:, :, :, 1, 0:1]
                ref = ref.to_broadcast([P, HH, n, h2])
                pool.tensor_tensor(w4[:, :, :, 0, :], ref, p4[:, :, :, 0, :], ALU.subtract)
                pool.tensor_tensor(w4[:, :, :, 1, :], p4[:, :, :, 1, :], ref, ALU.subtract).then_inc(sem("hg_warg"), 1)

            if stop >= 2:
                key_args(0)
                state_args(0)
                for st in range(len(STEPS)):
                    level_args(7 * st)
                    level_args(7 * st + 1)
                    for i in range(7):
                        if i < 5:
                            level_args(7 * st + i + 2)
                        if st + 1 < len(STEPS) and i == 4:
                            key_args(st + 1)
                        if st + 1 < len(STEPS) and i == 5:
                            state_args(st + 1)

            def s5_tables():
                link = Chain(pool, "pool_chain").link
                tt = pool.tensor_tensor
                EC, ES = lambda k: SPR[:, 14 + k, :], lambda k: SPR[:, 23 + k, :]

                def doubled(R, I, T, c, s_, n):
                    lo, hi = slice(0, n), slice(n, 2 * n)
                    tt(R[:, :, hi], R[:, :, lo], c, ALU.mult)
                    tt(T, R[:, :, lo], s_, ALU.mult)
                    link(tt(I[:, :, hi], I[:, :, lo], s_, ALU.mult))
                    link(tt(R[:, :, hi], R[:, :, hi], I[:, :, hi], ALU.subtract))
                    link(tt(I[:, :, hi], I[:, :, lo], c, ALU.mult))
                    ins = tt(I[:, :, hi], I[:, :, hi], T, ALU.add)
                    if n < L // 2:
                        link(ins)
                    return ins

                pool.wait_ge(sem("s5_sc"), 1)
                pool.tensor_copy(EC(0), SPR[:, 7, :])
                link(pool.tensor_copy(ES(0), SPR[:, 6, :]))
                t1, t2 = SP3[:, 0, 0:16], SP3[:, 0, 16:32]
                for k in range(8):
                    tt(t1, EC(k), EC(k), ALU.mult)
                    tt(ES(k + 1), EC(k), ES(k), ALU.mult)
                    link(tt(t2, ES(k), ES(k), ALU.mult))
                    tt(EC(k + 1), t1, t2, ALU.subtract)
                    link(tt(ES(k + 1), ES(k + 1), ES(k + 1), ALU.add))
                pool.memset(SE0[0][:, :, 0:1], 1.0)
                link(pool.memset(SE0[1][:, :, 0:1], 0.0))
                for k in range(5):
                    n = 1 << k
                    at = lambda v: v.unsqueeze(2).to_broadcast([P, 16, n])
                    T = SP3[:, 0, 0:16 * n].rearrange("p (j t) -> p j t", j=16)
                    doubled(SE0[0], SE0[1], T, at(EC(k)), at(ES(k)), n)

                def tables(st):
                    b, js = st % 2, slice(2 * st, 2 * st + 2)
                    if st >= 2:
                        pool.wait_ge(sem("s5_hr"), st - 1)
                    pool.tensor_copy(SER[b][:, :, 0:32], SE0[0][:, js, :])
                    link(pool.tensor_copy(SEI[b][:, :, 0:32], SE0[1][:, js, :]))
                    for k in range(5, 9):
                        n = 1 << k
                        at = lambda v: v[:, js].unsqueeze(2).to_broadcast([P, 2, n])
                        last = doubled(SER[b], SEI[b], SP3[:, :, 0:n], at(EC(k)), at(ES(k)), n)
                    last.then_inc(sem("s5_tables"), 1)
                    pool.wait_ge(sem("s5_tables"), st + 1)

                tables(0)
                tables(1)
                for st in range(S5_STEPS):
                    b = st % 2
                    pool.wait_ge(sem("s5_sums"), st + 1)
                    if st >= 2:
                        pool.wait_ge(*fill_of(f"s5y{st - 2}"))
                    tt(SHI[b], SER[b], SBI[b], ALU.mult)
                    link(tt(SP3, SEI[b], SBR[b], ALU.mult))
                    tt(SHI[b], SHI[b], SP3, ALU.add).then_inc(sem("s5_hi"), 1)
                    pool.wait_ge(sem("s5_hi"), st + 1)
                    if st + 2 < S5_STEPS:
                        tables(st + 2)

            def lo_parts(upto, end):
                while made["lo"] <= min(upto, end - 1):
                    i = made["lo"]
                    slot, kt = splits[i][:2]
                    pool.wait_ge(sem("w_masked"), i + 1)
                    pool.tensor_tensor(W_LO[slot][:, 0:kt, :], WR[:, slot, 0:kt, :], WM[:, 0:kt, :], ALU.subtract).then_inc(sem("w_lo"), 1)
                    made["lo"] += 1

            def x_lo_parts(index):
                for t in range(TL):
                    ts = slice(t * P, (t + 1) * P)
                    pool.wait_ge(sem("x_masked"), TL * index + t + 1)
                    pool.tensor_tensor(X_LO[:, :, ts], NT[:, :, ts], NM[:, :, ts], ALU.subtract).then_inc(sem("x_lo"), 1)

            def ffn(l):
                first, end = FIRST[l], ffn_end(l)
                lo_parts(first, end)
                x_lo_parts(2 * l)
                lo_parts(first + 1, end)
                for what, half, c, at in ffn_steps(l):
                    lo_parts(at + 2, end)
                    if what == "pair":
                        q = l * (KF // 2) + c
                        pool.wait_ge(sem("f_masked"), q + 1)
                        pool.tensor_tensor(F_LO[c - HALVES[half][0]][:, :, :], FSG[:, q % 2], FM, ALU.subtract).then_inc(sem("f_lo"), 1)

            if stop >= 3:
                s5_tables()
            if stop >= 4:
                ffn(0)
            if stop >= 5:
                lo_parts(RG0, RG_END)
                x_lo_parts(1)
                lo_parts(RG_END - 1, RG_END)
            if stop >= 6:
                ffn(1)

            last = min(stop, 6)
            for t in range(TL):
                pool.wait_ge(sem(f"x{last}_ready"), t + 1)
                pool.dma_start(out[0, t * P:(t + 1) * P, :], X[:, t, :]).then_inc(sem("out_written"), 16)
            pool.wait_ge(sem("out_written"), 16 * TL)
            if last <= 2:
                pool.wait_ge(sem("bc_in"), 64)




def kernel(**inputs):
    import numpy as _np
    import concourse.bacc as _bacc
    from concourse import mybir as _mybir
    from concourse.bass_utils import run_bass_kernel_spmd as _run

    nc = _bacc.Bacc("TRN2", target_bir_lowering=False, num_devices=1)
    arrays, aps = {}, {}
    for name, x in list(inputs.items()) + [("tables", make_tables())]:
        x = _np.ascontiguousarray(x)
        arrays[f"in_{name}"] = x
        aps[name] = nc.dram_tensor(f"in_{name}", x.shape, _mybir.dt.from_np(x.dtype), kind="ExternalInput").ap()
    out = nc.dram_tensor("out_0", (1, L, D), F32, kind="ExternalOutput").ap()
    program(nc, aps, out)
    r = _run(nc, [arrays], core_ids=[0])
    return r.results[0]["out_0"]
```
